# Optimizing a Trainium2 kernel written in Bass

```python
import jax
import jax.numpy as jnp
from jax import lax
import numpy as np

D_MODEL = 1024
BATCH = 1
SEQ = 1024
DEPTH = 1
DEC_BATCH = 8
DEC_SEQ = 4
PAST_LEN = 8192
PAGE_SIZE = 128

PLE_DIM = 256
GDN_WIDTH = D_MODEL // 2
GDN_HEAD_DIM = 128
GDN_HEADS = GDN_WIDTH // GDN_HEAD_DIM
GDN_QKV_DIM = 3 * GDN_WIDTH
GDN_CONV = 4
GDN_CHUNK = 64
SC_WIDTH = D_MODEL - GDN_WIDTH
SC_CONV = 3
D_FF = 4 * D_MODEL
EPS = 1e-6
OFF_QKV = 0
OFF_A = OFF_QKV + GDN_QKV_DIM
OFF_B = OFF_A + GDN_HEADS
OFF_Z = OFF_B + GDN_HEADS
OFF_SC_B = OFF_Z + GDN_WIDTH
OFF_SC_C = OFF_SC_B + SC_WIDTH
OFF_SC_H = OFF_SC_C + SC_WIDTH
IN_DIM = OFF_SC_H + SC_WIDTH

kernel_name = "hymba_gdn_shortconv_decode_step"

def rmsnorm(x, w):
    xf = x.astype(jnp.float32)
    y = xf * lax.rsqrt(jnp.mean(xf * xf, axis=-1, keepdims=True) + EPS)
    return (y * w.astype(jnp.float32)).astype(x.dtype)

def l2norm(x):
    xf = x.astype(jnp.float32)
    return xf * lax.rsqrt(jnp.sum(xf * xf, axis=-1, keepdims=True) + EPS)

def causal_dwconv(xp, w):
    width = w.shape[0]
    t = xp.shape[1] - (width - 1)
    out = xp[:, 0:t] * w[0]
    for j in range(1, width):
        out = out + xp[:, j:j + t] * w[j]
    return out

def gated_delta_rule(q, k, v, log_a, beta, s0):
    bsz, t, nh, dk = q.shape
    dv = v.shape[-1]
    c = GDN_CHUNK if t % GDN_CHUNK == 0 else t
    n = t // c

    def to_chunks(a):
        a = a.reshape(bsz, n, c, nh, *a.shape[3:])
        return jnp.moveaxis(a, 3, 1)

    q, k, v, log_a, beta = (to_chunks(a) for a in (q, k, v, log_a, beta))
    g = jnp.cumsum(log_a, axis=-1)
    idx = jnp.arange(c)
    lower = idx[:, None] >= idx[None, :]
    strict = idx[:, None] > idx[None, :]
    diff = g[..., :, None] - g[..., None, :]
    decay = jnp.where(lower, jnp.exp(jnp.where(lower, diff, 0.0)), 0.0)
    kk = jnp.einsum("bhnid,bhnjd->bhnij", k, k)
    a_mat = jnp.eye(c, dtype=jnp.float32) + jnp.where(strict, beta[..., :, None] * kk * decay, 0.0)
    rhs = jnp.concatenate([v * beta[..., None], k * (beta * jnp.exp(g))[..., None]], axis=-1)
    sol = lax.linalg.triangular_solve(a_mat, rhs, left_side=True, lower=True, unit_diagonal=True)
    u, w = sol[..., :dv], sol[..., dv:]
    qk = jnp.einsum("bhnid,bhnjd->bhnij", q, k) * decay

    def step(s, xs):
        q_c, k_c, u_c, w_c, g_c, qk_c = xs
        v_new = u_c - jnp.einsum("bhcd,bhde->bhce", w_c, s)
        o_c = (jnp.einsum("bhcd,bhde->bhce", q_c * jnp.exp(g_c)[..., None], s)
               + jnp.einsum("bhij,bhje->bhie", qk_c, v_new))
        g_last = g_c[..., -1:]
        s = (s * jnp.exp(g_last)[..., None]
             + jnp.einsum("bhcd,bhce->bhde", k_c * jnp.exp(g_last - g_c)[..., None], v_new))
        return s, o_c

    xs = tuple(jnp.moveaxis(a, 2, 0) for a in (q, k, u, w, g, qk))
    s_final, o = lax.scan(step, s0, xs)
    o = jnp.transpose(o, (1, 0, 3, 2, 4)).reshape(bsz, t, nh, dv)
    return o, s_final

def hybrid_layer(x, p, conv_qkv_buf, s0, conv_sc_buf, norm_mix, w_in, w_conv_qkv, a_log, dt_bias,
                 w_gdn_norm, w_conv_sc, w_out, norm_mlp, w_up, w_down, norm_ple, w_ple_gate, w_ple_proj):
    bsz, t, _ = x.shape
    h = rmsnorm(x, norm_mix)
    proj = h @ w_in
    qkv_in = jnp.concatenate([conv_qkv_buf.astype(proj.dtype), proj[..., OFF_QKV:OFF_A]], axis=1)
    qkv = jax.nn.silu(causal_dwconv(qkv_in, w_conv_qkv))
    q, k, v = jnp.split(qkv, 3, axis=-1)
    q = l2norm(q.reshape(bsz, t, GDN_HEADS, GDN_HEAD_DIM)) * (GDN_HEAD_DIM ** -0.5)
    k = l2norm(k.reshape(bsz, t, GDN_HEADS, GDN_HEAD_DIM))
    v = v.reshape(bsz, t, GDN_HEADS, GDN_HEAD_DIM).astype(jnp.float32)
    log_a = -jnp.exp(a_log.astype(jnp.float32)) * jax.nn.softplus(
        proj[..., OFF_A:OFF_B].astype(jnp.float32) + dt_bias.astype(jnp.float32))
    beta = jax.nn.sigmoid(proj[..., OFF_B:OFF_Z].astype(jnp.float32))
    o, s_new = gated_delta_rule(q, k, v, log_a, beta, s0.astype(jnp.float32))
    z = proj[..., OFF_Z:OFF_SC_B].reshape(bsz, t, GDN_HEADS, GDN_HEAD_DIM).astype(jnp.float32)
    o = (rmsnorm(o, w_gdn_norm) * jax.nn.silu(z)).reshape(bsz, t, GDN_WIDTH).astype(x.dtype)
    sc_in = jnp.concatenate([conv_sc_buf.astype(proj.dtype),
                             proj[..., OFF_SC_C:OFF_SC_H] * proj[..., OFF_SC_H:IN_DIM]], axis=1)
    y_sc = proj[..., OFF_SC_B:OFF_SC_C] * causal_dwconv(sc_in, w_conv_sc)
    x = x + jnp.concatenate([o, y_sc.astype(x.dtype)], axis=-1) @ w_out
    u_ff = jax.nn.relu(rmsnorm(x, norm_mlp) @ w_up)
    x = x + (u_ff * u_ff) @ w_down
    gate = jax.nn.sigmoid(rmsnorm(x, norm_ple) @ w_ple_gate)
    x = x + gate * (p @ w_ple_proj)
    return x, qkv_in[:, -(GDN_CONV - 1):], s_new.astype(s0.dtype), sc_in[:, -(SC_CONV - 1):]

def setup_inputs(seed: int = 0) -> dict:
    key = jax.random.key(seed)
    ks = jax.random.split(key, 24)
    f32 = jnp.float32
    nrm = lambda k_, shape, scale: jax.random.normal(k_, shape, f32) * scale
    gain = lambda k_, shape: 1.0 + 0.02 * jax.random.normal(k_, shape, f32)
    a_init = jax.random.uniform(ks[10], (DEPTH, GDN_HEADS), f32, 1.0, 16.0)
    dt = jnp.exp(jax.random.uniform(ks[11], (DEPTH, GDN_HEADS), f32, np.log(1e-3), np.log(1e-1)))
    return {
        "x_prompt": nrm(ks[0], (BATCH, SEQ, D_MODEL), 1.0),
        "x_sample": nrm(ks[1], (DEC_BATCH, DEC_SEQ, D_MODEL), 1.0),
        "state_gdn_conv": nrm(ks[2], (DEPTH, DEC_BATCH, GDN_CONV - 1, GDN_QKV_DIM), 1.0),
        "state_gdn": nrm(ks[3], (DEPTH, DEC_BATCH, GDN_HEADS, GDN_HEAD_DIM, GDN_HEAD_DIM), 0.3),
        "state_sc_conv": nrm(ks[4], (DEPTH, DEC_BATCH, SC_CONV - 1, SC_WIDTH), 1.0),
        "p_prompt": nrm(ks[5], (DEPTH, BATCH, SEQ, PLE_DIM), 1.0),
        "p_sample": nrm(ks[6], (DEPTH, DEC_BATCH, DEC_SEQ, PLE_DIM), 1.0),
        "norm_mix": gain(ks[7], (DEPTH, D_MODEL)),
        "w_in": nrm(ks[8], (DEPTH, D_MODEL, IN_DIM), D_MODEL ** -0.5),
        "w_conv_qkv": nrm(ks[9], (DEPTH, GDN_CONV, GDN_QKV_DIM), GDN_CONV ** -0.5),
        "a_log": jnp.log(a_init),
        "dt_bias": dt + jnp.log(-jnp.expm1(-dt)),
        "w_gdn_norm": gain(ks[12], (DEPTH, GDN_HEAD_DIM)),
        "w_conv_sc": nrm(ks[13], (DEPTH, SC_CONV, SC_WIDTH), SC_CONV ** -0.5),
        "w_out": nrm(ks[14], (DEPTH, D_MODEL, D_MODEL), D_MODEL ** -0.5),
        "norm_mlp": gain(ks[15], (DEPTH, D_MODEL)),
        "w_up": nrm(ks[16], (DEPTH, D_MODEL, D_FF), D_MODEL ** -0.5),
        "w_down": nrm(ks[17], (DEPTH, D_FF, D_MODEL), D_FF ** -0.5),
        "norm_ple": gain(ks[18], (DEPTH, D_MODEL)),
        "w_ple_gate": nrm(ks[19], (DEPTH, D_MODEL, D_MODEL), D_MODEL ** -0.5),
        "w_ple_proj": nrm(ks[20], (DEPTH, PLE_DIM, D_MODEL), PLE_DIM ** -0.5),
        "norm_f": gain(ks[21], (D_MODEL,)),
    }

def reference(x_prompt, x_sample, state_gdn_conv, state_gdn, state_sc_conv, p_prompt, p_sample,
              norm_mix, w_in, w_conv_qkv, a_log, dt_bias, w_gdn_norm, w_conv_sc, w_out,
              norm_mlp, w_up, w_down, norm_ple, w_ple_gate, w_ple_proj, norm_f):
    bp = x_prompt.shape[0]
    dt_ = x_prompt.dtype
    zero_conv_qkv = jnp.zeros((bp, GDN_CONV - 1, GDN_QKV_DIM), dt_)
    zero_s = jnp.zeros((bp, GDN_HEADS, GDN_HEAD_DIM, GDN_HEAD_DIM), dt_)
    zero_conv_sc = jnp.zeros((bp, SC_CONV - 1, SC_WIDTH), dt_)
    hp, hs = x_prompt, x_sample
    pc, ps, psc, sc, ss, ssc = [], [], [], [], [], []
    for i in range(DEPTH):
        wts = (norm_mix[i], w_in[i], w_conv_qkv[i], a_log[i], dt_bias[i], w_gdn_norm[i], w_conv_sc[i],
               w_out[i], norm_mlp[i], w_up[i], w_down[i], norm_ple[i], w_ple_gate[i], w_ple_proj[i])
        hp, c1, s1, c2 = hybrid_layer(hp, p_prompt[i], zero_conv_qkv, zero_s, zero_conv_sc, *wts)
        hs, c3, s3, c4 = hybrid_layer(hs, p_sample[i], state_gdn_conv[i], state_gdn[i], state_sc_conv[i], *wts)
        pc.append(c1); ps.append(s1); psc.append(c2)
        sc.append(c3); ss.append(s3); ssc.append(c4)
    y_prompt = rmsnorm(hp, norm_f)
    y_sample = rmsnorm(hs, norm_f)
    return (y_prompt, y_sample, jnp.stack(pc), jnp.stack(ps), jnp.stack(psc),
            jnp.stack(sc), jnp.stack(ss), jnp.stack(ssc))


_drawn_inputs = setup_inputs


def setup_inputs(seed=0):
    import zlib

    import numpy as np

    out = dict(_drawn_inputs(seed))
    spreads = {}
    factors = {'w_gdn_norm': 8.0, 'norm_mlp': 3.749, 'norm_ple': 8.0, 'norm_f': 2.747}
    for name, (base, spread) in spreads.items():
        noise = np.random.default_rng([zlib.crc32(name.encode()), seed]).standard_normal(out[name].shape)
        drawn = base * np.exp(spread * noise) if base else spread * noise
        out[name] = jnp.asarray(drawn.astype(out[name].dtype))
    for name, factor in factors.items():
        out[name] = (out[name] * factor).astype(out[name].dtype)
    return out
```

```python
import concourse.bass as bass
from concourse import mybir
from contextlib import ExitStack

P = 128
D = 1024
KD = D // P
TP = 1024
NB = 8
NT = 4
TS = NB * NT
T = TP + TS
TH = T // 3
NTT = TP // P
H = 4
GW = H * P
QKV = 3 * GW
NQ = QKV // P
SCW = D - GW
NSC = SCW // P
CW = 4
SW = 3
PAD = CW - 1
SEG = PAD + NT
PRE = PAD + TP + NB * SEG
CV = PRE - PAD
FF = 4 * D
FC = 4
NFC = FF // P // FC
PLE = 256
KP = PLE // P
EPS = 1e-6
OFF_A = QKV
OFF_Z = OFF_A + 2 * H
OFF_SB = OFF_Z + GW
OFF_SC = OFF_SB + SCW
OFF_SH = OFF_SC + SCW
QSCALE = float(P) ** -0.5
LEVELS = 7
NPAR = NTT + 1

STEPS = (["prep_norm0", "prep_kk0", "prep_norm1", "prep_kk1", "prep_x0", "prep_x1"]
         + [f"{w}{x}_{l}" for l in range(1, LEVELS) for w, x in (("y", 0), ("y", 1), ("z", 0), ("z", 1))]
         + [f"{s}{x}" for x in range(2) for s in ("s_in", "s_solve", "s_out", "s_norm")])
FILL = {s: 12 for s in STEPS}
for _s in STEPS:
    if _s[0] in "yz":
        FILL[_s] = 3
BODY_MM = 4 * KD * 9
_left = BODY_MM - sum(FILL.values())
for _n, _s in enumerate(s for s in STEPS if s[0] in "s"):
    FILL[_s] += _left // 8 + (1 if _n < _left % 8 else 0)


def fill_range(step):
    at = sum(FILL[s] for s in STEPS[:STEPS.index(step)])
    return at, at + FILL[step]


def thirds_after(step):
    a, b = fill_range(step)
    return [t for t in range(12) if a < 24 * (t + 1) <= b]


class Signals:

    def __init__(self, sem):
        self.params_in = sem("params_in")
        self.gain_in = sem("gain_in")
        self.states_in = sem("states_in")
        self.consts_made = sem("consts_made")
        self.masks_made = sem("masks_made")
        self.buffers_zeroed = sem("buffers_zeroed")
        self.made = sem("made")
        self.r_tok_set = sem("r_tok_set")
        self.x_turned = sem("x_turned")
        self.xw_made = sem("xw_made")
        self.xhi_made = sem("xhi_made")
        self.xlo_even = sem("xlo_even")
        self.xlo_odd = sem("xlo_odd")
        self.x_squared = sem("x_squared")
        self.x_root = sem("x_root")
        self.r_made = sem("r_made")
        self.rdiag_made = sem("rdiag_made")
        self.r_spread = sem("r_spread")
        self.r_ready = sem("r_ready")
        self.st_turned = sem("st_turned")
        self.st_ready = sem("st_ready")
        self.w_hi_made = sem("w_hi_made")
        self.w_lo_made = sem("w_lo_made")
        self.mm_done = sem("mm_done")
        self.evacuated = sem("evacuated")
        self.ab_turned = sem("ab_turned")
        self.ab_copied = sem("ab_copied")
        self.ab_exp = sem("ab_exp")
        self.chain = sem("chain")
        self.g_summed = sem("g_summed")
        self.g_copied = sem("g_copied")
        self.g_exp = sem("g_exp")
        self.state_put = sem("state_put")
        self.conv_step = sem("conv_step")
        self.silu_made = sem("silu_made")
        self.state_saved = sem("state_saved")
        self.z_spilled = sem("z_spilled")
        self.ch_made = sem("ch_made")
        self.sc_step = sem("sc_step")
        self.y_made = sem("y_made")
        self.y_spilled = sem("y_spilled")
        self.sc_put = sem("sc_put")
        self.h_scaled = sem("h_scaled")
        self.norms_summed = sem("norms_summed")
        self.kk_made = sem("kk_made")
        self.xt_turned = sem("xt_turned")
        self.y_mm = sem("y_mm")
        self.z_mm = sem("z_mm")
        self.in_mm = sem("in_mm")
        self.solve_mm = sem("solve_mm")
        self.out_mm = sem("out_mm")
        self.onorm_mm = sem("onorm_mm")
        self.squared = sem("squared")
        self.rsq_made = sem("rsq_made")
        self.eg_made = sem("eg_made")
        self.decay_made = sem("decay_made")
        self.x_copied = sem("x_copied")
        self.ycopy_made = sem("ycopy_made")
        self.v_staged = sem("v_staged")
        self.vtok_made = sem("vtok_made")
        self.o_squared = sem("o_squared")
        self.o_rs_made = sem("o_rs_made")
        self.diag_made = sem("diag_made")
        self.diff_made = sem("diff_made")
        self.qk_made = sem("qk_made")
        self.pt_made = sem("pt_made")
        self.at_made = sem("at_made")
        self.x_updated = sem("x_updated")
        self.ktok_made = sem("ktok_made")
        self.r_vec = sem("r_vec")
        self.vnew_made = sem("vnew_made")
        self.s_updated = sem("s_updated")
        self.o_made = sem("o_made")
        self.masked = sem("masked")
        self.at_scaled = sem("at_scaled")
        self.qg_made = sem("qg_made")
        self.lt_made = sem("lt_made")
        self.xt_made = sem("xt_made")
        self.last_kept = sem("last_kept")
        self.sin_loaded = sem("sin_loaded")
        self.q_pe = sem("q_pe")
        self.q_act = sem("q_act")
        self.q_dve = sem("q_dve")
        self.q_pool = sem("q_pool")
        self.so_turned = sem("so_turned")
        self.so_copied = sem("so_copied")
        self.s_out_made = sem("s_out_made")
        self.states_out = sem("states_out")
        self.yt_loaded = sem("yt_loaded")
        self.zt_loaded = sem("zt_loaded")
        self.z_silu = sem("z_silu")
        self.gated = sem("gated")
        self.mix_hi = sem("mix_hi")
        self.mix_lo = sem("mix_lo")
        self.xcol_turned = sem("xcol_turned")
        self.xcol_turned3 = sem("xcol_turned3")
        self.xr_copied = sem("xr_copied")
        self.x_made = sem("x_made")
        self.sq_made = sem("sq_made")
        self.ssq_added = sem("ssq_added")
        self.ssq_zeroed = sem("ssq_zeroed")
        self.rms_mm = sem("rms_mm")
        self.rms_log = sem("rms_log")
        self.rms_ready = sem("rms_ready")
        self.split_hi = sem("split_hi")
        self.split_lo = sem("split_lo")
        self.usq_made = sem("usq_made")
        self.u_hi_made = sem("u_hi_made")
        self.u_lo_made = sem("u_lo_made")
        self.p_loaded = sem("p_loaded")
        self.p_turned = sem("p_turned")
        self.p_hi_made = sem("p_hi_made")
        self.p_lo_made = sem("p_lo_made")
        self.gate_made = sem("gate_made")
        self.x_scaled = sem("x_scaled")
        self.rt_mm = sem("rt_mm")
        self.rt_root = sem("rt_root")
        self.rt_ready = sem("rt_ready")
        self.y_turned = sem("y_turned")
        self.y_act = sem("y_act")
        self.y_dve = sem("y_dve")


def trunk(nc, x_p, x_s, st_qkv, st_gdn, st_sc, p_p, p_s, norm_mix, w_in, w_cq, a_log, dt_bias, w_gn, w_cs,
          w_out, norm_mlp, w_up, w_down, norm_ple, w_gate, w_proj, norm_f,
          y_p, y_s, oc_p, os_p, osc_p, oc_s, os_s, osc_s):
    f32, f32r = mybir.dt.float32, mybir.dt.float32r
    ALU, ACT = mybir.AluOpType, mybir.ActivationFunctionType
    MUL, ADD, SUB, MAX, MIN = ALU.mult, ALU.add, ALU.subtract, ALU.max, ALU.min
    ds = bass.ds

    z_dram = nc.dram_tensor("z_spill", (H, P, T), f32, kind="Internal").ap()
    y_dram = nc.dram_tensor("ysc_spill", (NSC * P, T), f32, kind="Internal").ap()

    win_v = w_in.rearrange("(k p) n -> p k n", p=P)
    wout_v = w_out.rearrange("(k p) n -> p k n", p=P)
    wup_v = w_up.rearrange("(k p) n -> p k n", p=P)
    wdn_v = w_down.rearrange("(k p) n -> p k n", p=P)
    wg_v = w_gate.rearrange("(k p) n -> p k n", p=P)
    wp_v = w_proj.rearrange("(k p) n -> p k n", p=P)

    ctx = ExitStack()
    with ctx:
        def sb(name, shape, dt=f32, scope=ctx):
            return scope.enter_context(nc.sbuf_tensor(name, shape, dt))

        def sem(name):
            return ctx.enter_context(nc.semaphore(name))

        act_hi = sb("act_hi", [P, KD, T], f32r)
        act_lo = sb("act_lo", [P, KD, T], f32r)
        w_raw = [sb(f"w_raw{i}", [P, KD, P]) for i in range(2)]
        w_hi = [sb(f"w_hi{i}", [P, KD, P], f32r) for i in range(2)]
        w_lo = [sb(f"w_lo{i}", [P, KD, P], f32r) for i in range(2)]
        ident = sb("ident", [P, P])
        ones = sb("ones", [P, P])
        r_b = sb("r_b", [P, T])
        n_mix = sb("n_mix", [P, KD])
        n_mlp = sb("n_mlp", [P, KD])
        n_ple = sb("n_ple", [P, KD])
        n_fin = sb("n_fin", [P, KD])
        eps = sb("eps", [P, 1])
        gnw = sb("gnw", [P, 1])
        r_tok = sb("r_tok", [P, NPAR])
        token = sb("token", [P, 20])

        mixer = ExitStack()
        stage_x = ExitStack()
        x_tok = [sb(f"x_tok{t}", [P, D], scope=stage_x) for t in range(NTT + 1)]
        x_sqr = sb("x_sqr", [P, D], scope=stage_x)
        st_in = sb("st_in", [3 * NB, QKV], scope=stage_x)
        sc_in = sb("sc_in", [2 * NB, SCW], scope=stage_x)
        stage_x.close()
        qkv = sb("qkv", [P, NQ, T], scope=mixer)
        m_inc = sb("m_inc", [P, P], scope=mixer)
        m_lev = [sb(f"m_lev{l}", [P, P], scope=mixer) for l in range(LEVELS)]
        m_smp = sb("m_smp", [TS, TS], scope=mixer)
        m_blk = sb("m_blk", [TS, TS], scope=mixer)
        m_bat = sb("m_bat", [TS, NB], scope=mixer)
        st_T = sb("st_T", [P, NQ, PAD * NB], scope=mixer)
        sc_T = sb("sc_T", [P, NSC, 2 * NB], scope=mixer)
        st_O = sb("st_O", [P, NQ, PAD * (NB + 1)], scope=mixer)
        sc_O = sb("sc_O", [P, NSC, 2 * (NB + 1)], scope=mixer)
        cq_w = sb("cq_w", [P, NQ, CW], scope=mixer)
        cs_w = sb("cs_w", [P, NSC, SW], scope=mixer)
        par = sb("par", [P, NPAR, 2 * H], scope=mixer)
        alog = sb("alog", [P, H], scope=mixer)
        dtb = sb("dtb", [P, H], scope=mixer)
        log_a = sb("log_a", [P, NPAR, H], scope=mixer)
        beta = sb("beta", [P, NPAR, H], scope=mixer)
        g_tok = sb("g_tok", [P, NPAR, H], scope=mixer)
        eneg = sb("eneg", [P, NPAR, H], scope=mixer)
        kf = sb("kf", [TS, H], scope=mixer)
        t_a = sb("t_a", [P, NPAR, H], scope=mixer)
        t_b = sb("t_b", [P, NPAR, H], scope=mixer)
        t_c = sb("t_c", [P, NPAR, H], scope=mixer)
        egl = [sb(f"egl{x}", [P, H], scope=mixer) for x in range(2)]
        ktl = [sb(f"ktl{x}", [P, H], scope=mixer) for x in range(2)]
        S = sb("S", [P, H, P], scope=mixer)
        Tb = [sb(f"Tb{i}", [P, H, P], scope=mixer) for i in range(5)]
        kn = [sb(f"kn{x}", [P, H, P], scope=mixer) for x in range(2)]
        AT = [sb(f"AT{x}", [P, H, P], scope=mixer) for x in range(2)]
        PT = [sb(f"PT{x}", [P, H, P], scope=mixer) for x in range(2)]
        qg = [sb(f"qg{x}", [P, H, P], scope=mixer) for x in range(2)]
        X = [sb(f"X{x}", [P, H, P], scope=mixer) for x in range(2)]
        XT = [sb(f"XT{x}", [P, H, P], scope=mixer) for x in range(2)]
        conv = ExitStack()
        pre = [sb(f"pre{i}", [P, PRE], scope=conv) for i in range(2)]
        cv = [sb(f"cv{i}", [P, PRE], scope=conv) for i in range(2)]
        conv.close()
        S_in = sb("S_in", [P, H, NB, P], scope=mixer)
        mixer.close()

        tail = ExitStack()
        u_hi = [sb(f"u_hi{i}", [P, FC, T], f32r, scope=tail) for i in range(2)]
        u_lo = [sb(f"u_lo{i}", [P, FC, T], f32r, scope=tail) for i in range(2)]
        xres = sb("xres", [P, KD, T], scope=tail)
        ssq = sb("ssq", [P, T], scope=tail)
        tm = [sb(f"tm{i}", [P, TH], scope=tail) for i in range(2)]
        sq = [sb(f"sq{i}", [P, TH], scope=tail) for i in range(2)]
        tail.close()
        late = ExitStack()
        o_room = sb("o_room", [P, H, T], scope=late)
        x_col = [sb(f"x_col{i}", [P, NTT + 1, P], scope=late) for i in range(2)]
        late_pad = sb("late_pad", [P, 2 * H * T - 2 * (NTT + 1) * P], scope=late)
        zst = [sb(f"zst{i}", [P, T], scope=late) for i in range(4)]
        late.close()
        ple = ExitStack()
        p_hi = sb("p_hi", [P, KP, T], f32r, scope=ple)
        p_lo = sb("p_lo", [P, KP, T], f32r, scope=ple)
        p_tok = [sb(f"p_tok{t}", [P, PLE], scope=ple) for t in range(NTT + 1)]
        gate = sb("gate", [P, H, T], scope=ple)
        y_tok = [sb(f"y_tok{i}", [P, D], scope=ple) for i in range(3)]
        ple.close()

        pg = [ctx.enter_context(nc.psum_tensor(f"pg{i}", [P, 512], f32)) for i in range(3)]
        bk = [ctx.enter_context(nc.psum_tensor(f"bk{i}", [P, 512], f32)) for i in range(5)]

        x_loaded = [sem(f"x_loaded{t}") for t in range(NTT + 1)]
        raw_in = [sem(f"raw_in{i}") for i in range(2)]
        xcol_in = [sem(f"xcol_in{i}") for i in range(2)]
        y_sent = [sem(f"y_sent{i}") for i in range(3)]
        sm = Signals(sem)

        def at(base, p=0, step=1):
            return base if isinstance(p, int) and p == 0 else p * step + base

        def twelfths(b, p, q):
            return at(12 * b + q, p, 24)

        def cols(n):
            return slice(n * TH, (n + 1) * TH)

        def tokens(t):
            return P if t < NTT else TS

        def heads(ap):
            return ap.rearrange("p (h t) -> p h t", h=H)

        def spread(ap, n):
            return ap[:, :, None].to_broadcast([ap.shape[0], ap.shape[1], n])

        def samples(ap):
            return ap[:, PAD + TP:PRE].rearrange("p (b s) -> p b s", s=SEG)

        def sample_cv(ap):
            return samples(ap)[:, :, 0:NT]

        def flat(ap):
            return ap[:, :, :].rearrange("p h t -> p (h t)")

        SMALL = H * TS

        def hsmall(ap):
            return ap.rearrange("p (h t) -> p h t", h=H)

        U_QKV, U_B, U_OUT = 1, 1 + NQ, 1 + NQ + 16
        U_MLP = U_OUT + KD
        U_PLE = U_MLP + 8 * NFC
        N_UNITS = U_PLE + 10

        def up_unit(c):
            return U_MLP if c == 0 else U_MLP + 4 + 8 * (c - 1)

        def down_unit(c):
            return U_MLP + 8 * (c + 1) if c < NFC - 1 else U_MLP + 8 * NFC - 4

        MLP_ORDER = [("up", 0)]
        for _c in range(NFC):
            if _c + 1 < NFC:
                MLP_ORDER.append(("up", _c + 1))
            MLP_ORDER.append(("down", _c))
        WIDE = 2 * P
        CHAIN_ABS, CHAIN_LOG_A, CHAIN_G = 3, 20, 23
        PARAMS = 16 * (6 + CW + SW)
        ZEROED = 5
        MASKS = 1

        block = ctx.enter_context(nc.Block())

        @block.sync
        def _(sp):
            def load_w(b, p, src, kt):
                if b >= 2 or not isinstance(p, int):
                    sp.wait_ge(sm.w_lo_made, at(b - 1, p, 2))
                dst = w_raw[b % 2][:, :, :].rearrange("p (k d) m -> p k (d m)", k=kt)
                sp.dma_start(dst, src).then_inc(raw_in[b % 2], 16)

            for t in range(NTT + 1):
                src = x_p[0, t * P:(t + 1) * P, :] if t < NTT else x_s.rearrange("b t d -> (b t) d")
                sp.dma_start(x_tok[t][0:tokens(t), :], src).then_inc(x_loaded[t], 16)
                if t == 3:
                    load_w(0, 0, win_v[:, :, OFF_A:OFF_A + P], KD)
            sp.dma_start(st_in[:, :], st_qkv[0].rearrange("b w f -> (b w) f")).then_inc(sm.states_in, 16)
            sp.dma_start(sc_in[:, :], st_sc[0].rearrange("b w f -> (b w) f")).then_inc(sm.states_in, 16)
            for x in range(2):
                load_w(U_QKV + x, 0, win_v[:, :, x * P:(x + 1) * P], KD)
            with sp.Fori(1, NQ // 2) as i:
                for x in range(2):
                    load_w(U_QKV + x, i, win_v[:, :, ds(i * WIDE + x * P, P)], KD)
            with sp.Fori(0, NSC) as j:
                for m, off in enumerate((OFF_Z, OFF_SC, OFF_SH, OFF_SB)):
                    load_w(U_B + m, 2 * j, win_v[:, :, ds(j * P + off, P)], KD)
            for x in range(2):
                load_w(U_OUT + x, 0, wout_v[:, :, x * P:(x + 1) * P], KD)
            sp.wait_ge(sm.y_spilled, 16 * NSC)
            sp.wait_ge(sm.z_spilled, 16 * NSC)
            for h in range(H):
                sp.dma_start(S_in[:, h, :, :], st_gdn[0, :, h, :, :].rearrange("b d e -> d b e")) \
                    .then_inc(sm.sin_loaded, 16)
            sp.wait_ge(sm.s_updated, 4 * (NTT + 1))
            sp.dma_start(os_p[0, 0].rearrange("h d e -> d h e"), S[:, :, :]).then_inc(sm.states_out, 16)
            for h in range(H):
                sp.wait_ge(sm.s_out_made, 2 * (h + 1))
                sp.dma_start(os_s[0, :, h, :, :].rearrange("b d e -> d b e"), S_in[:, h, :, :]) \
                    .then_inc(sm.states_out, 16)
            sp.wait_ge(sm.so_copied, 4)
            for i, buf in enumerate((kn[1], AT[1], PT[1])):
                f = slice(i * GW, (i + 1) * GW)
                flat = buf[:, :, :].rearrange("p h t -> p (h t)")
                sp.dma_start(oc_p[0, 0, :, f], flat[0:PAD, :]).then_inc(sm.states_out, 16)
                sp.dma_start(oc_s[0, :, :, f].rearrange("b w f -> (b w) f"),
                             flat[PAD:PAD * (NB + 1), :]).then_inc(sm.states_out, 16)
            flat = qg[1][:, :, :].rearrange("p h t -> p (h t)")
            sp.dma_start(osc_p[0, 0], flat[0:2, :]).then_inc(sm.states_out, 16)
            sp.dma_start(osc_s[0].rearrange("b w f -> (b w) f"), flat[2:2 * (NB + 1), :]) \
                .then_inc(sm.states_out, 16)
            sp.wait_ge(sm.states_out, 16 * (1 + 6 + 2 + H))
            sp.wait_ge(sm.o_made, NTT + 2)
            for i in range(NSC):
                sp.dma_start(zst[i][:, :], y_dram[i * P:(i + 1) * P, :]).then_inc(sm.yt_loaded, 16)
            for i in range(H):
                sp.wait_ge(sm.mix_lo, i + 1)
                sp.dma_start(zst[i][:, :], z_dram[i]).then_inc(sm.zt_loaded, 16)

            def load_xcol(x, i):
                f = ds(i * WIDE + x * P, P)
                sp.dma_start(x_col[x][:, 0:NTT, :], x_p[0].rearrange("(t p) d -> p t d", p=P)[:, :, f]) \
                    .then_inc(xcol_in[x], 16)
                sp.dma_start(x_col[x][0:TS, NTT, :], x_s.rearrange("b t d -> (b t) d")[:, f]) \
                    .then_inc(xcol_in[x], 16)

            for x in range(2):
                f = slice(x * P, (x + 1) * P)
                sp.dma_start(x_col[x][:, 0:NTT, :], x_p[0].rearrange("(t p) d -> p t d", p=P)[:, :, f]) \
                    .then_inc(xcol_in[x], 16)
                sp.dma_start(x_col[x][0:TS, NTT, :], x_s.rearrange("b t d -> (b t) d")[:, f]) \
                    .then_inc(xcol_in[x], 16)
            with sp.Fori(1, KD // 2) as i:
                for x in range(2):
                    load_w(U_OUT + x, i, wout_v[:, :, ds(i * WIDE + x * P, P)], KD)
                    sp.wait_ge(sm.xcol_turned, at(x - 1, i, 2))
                    load_xcol(x, i)
            for kind, c in MLP_ORDER:
                if kind == "up":
                    with sp.Fori(0, FC // 2) as i:
                        for x in range(2):
                            load_w(up_unit(c) + x, i, wup_v[:, :, ds(i * WIDE + (c * FC + x) * P, P)], KD)
                else:
                    with sp.Fori(0, 2) as i:
                        for x in range(2):
                            load_w(down_unit(c) + x, i,
                                   wdn_v[:, c * FC:(c + 1) * FC, ds(i * 2 * WIDE + x * WIDE, WIDE)], FC)
            for hf in range(2):
                with sp.Fori(0, 2) as i:
                    for x in range(2):
                        load_w(U_PLE + 5 * hf + x, i,
                               wg_v[:, :, ds(i * WIDE + (4 * hf + x) * P, P)], KD)
                load_w(U_PLE + 5 * hf + 4, 0, wp_v[:, :, hf * 4 * P:(hf + 1) * 4 * P], KP)
                if hf == 0:
                    sp.wait_ge(sm.mm_done, 12 * U_PLE)
                    for t in range(NTT + 1):
                        src = p_p[0, 0, t * P:(t + 1) * P, :] if t < NTT else p_s[0].rearrange("b t d -> (b t) d")
                        sp.dma_start(p_tok[t][0:tokens(t), :], src).then_inc(sm.p_loaded, 16)
            for t in range(NTT + 1):
                sp.wait_ge(sm.y_act, t + 1)
                sp.wait_ge(sm.y_dve, t + 1)
                dst = y_p[0, t * P:(t + 1) * P, :] if t < NTT else y_s.rearrange("b t d -> (b t) d")
                sp.dma_start(dst, y_tok[t % 3][0:tokens(t), :]).then_inc(y_sent[t % 3], 16)
            for i in range(3):
                sp.wait_ge(y_sent[i], 16 * 3)

        @block.tensor
        def _(pe):
            mm, turn = nc.tensor.matmul, nc.tensor.transpose

            def group(b, p, q, s, bank, terms):
                if 12 * b + q - 2 * s > 0:
                    pe.wait_ge(sm.evacuated, twelfths(b, p, q - 2 * s))
                for i, (w, a) in enumerate(terms):
                    last = mm(pg[bank][:, 0:TH], w, a, start=i == 0, stop=i == len(terms) - 1)
                last.then_inc(sm.mm_done, s)

            def panel_ready(b, p):
                pe.wait_ge(sm.w_lo_made, at(b + 1, p, 2))

            def parts(slot, kt, d, hi, lo, n):
                wh = w_hi[slot][:, :, :].rearrange("p (k d) m -> p k d m", k=kt)
                wl = w_lo[slot][:, :, :].rearrange("p (k d) m -> p k d m", k=kt)
                out = []
                for k in range(kt):
                    out += [(wh[:, k, d, :], hi[:, k, cols(n)]), (wh[:, k, d, :], lo[:, k, cols(n)]),
                            (wl[:, k, d, :], hi[:, k, cols(n)])]
                return out

            def unit(b, p, kt, hi, lo, ready=None):
                panel_ready(b, p)
                per = KD // kt
                for d in range(per):
                    for n in range(3):
                        if ready is not None and d == 0:
                            pe.wait_ge(*ready(n))
                        s = 4 // per
                        group(b, p, (3 * d + n) * s, s, n, parts(b % 2, kt, d, hi, lo, n))

            pe.wait_ge(sm.consts_made, 3)
            for t in range(NTT + 1):
                n = tokens(t)
                pe.wait_ge(x_loaded[t], 16)
                for hf in range(2):
                    i = 2 * t + hf
                    if i >= 4:
                        pe.wait_ge(sm.xw_made, i - 3)
                    for k in range(4):
                        f = slice((4 * hf + k) * P, (4 * hf + k + 1) * P)
                        last = turn(bk[i % 4][:, k * P:k * P + n], x_tok[t][0:n, f], ident[0:n, 0:n])
                    last.then_inc(sm.x_turned, 1)
            pe.wait_ge(sm.states_in, 32)
            for j in range(NQ):
                turn(bk[4][:, j * 24:(j + 1) * 24], st_in[:, j * P:(j + 1) * P], ident[0:24, 0:24])
            for j in range(NSC):
                last = turn(bk[4][:, 288 + j * 16:288 + (j + 1) * 16], sc_in[:, j * P:(j + 1) * P],
                            ident[0:16, 0:16])
            last.then_inc(sm.st_turned, 1)
            pe.wait_ge(sm.rdiag_made, 3)
            pe.wait_ge(sm.xw_made, 2 * (NTT + 1))
            mm(bk[0][:, :], ones[:, :], Tb[0][:, :, :], start=True, stop=True)
            mm(bk[1][:, :], ones[:, :], Tb[1][:, :, :], start=True, stop=True)
            mm(bk[2][:, 0:TS], ones[0:TS, :], Tb[2][0:TS, 0, 0:TS], start=True, stop=True) \
                .then_inc(sm.r_spread, 1)
            pe.wait_ge(sm.xlo_even, NTT + 1)
            pe.wait_ge(sm.xlo_odd, NTT + 1)
            unit(0, 0, KD, act_hi, act_lo)
            pe.wait_ge(sm.evacuated, 12)
            pe.wait_ge(sm.r_ready, 3)
            for t in range(NTT + 1):
                last = turn(bk[0][0:tokens(t), t * 8:(t + 1) * 8], cv[0][0:8, t * P:t * P + tokens(t)],
                            ident[0:8, 0:8])
            last.then_inc(sm.ab_turned, 1)
            with pe.Fori(0, NQ // 2) as i:
                for x in range(2):
                    unit(U_QKV + x, i, KD, act_hi, act_lo)
            pe.wait_ge(sm.chain, CHAIN_LOG_A)
            pe.wait_ge(sm.masks_made, MASKS)
            mm(bk[0][:, 0:32], m_inc[:, :], log_a[:, 0:NTT, :], start=True, stop=True)
            mm(bk[0][0:TS, 32:36], m_smp[:, :], log_a[0:TS, NTT, :], start=True, stop=True)
            mm(bk[0][0:TS, 36:40], m_blk[:, :], log_a[0:TS, NTT, :], start=True, stop=True) \
                .then_inc(sm.g_summed, 1)

            with pe.Fori(0, NSC) as j:
                def fill(step):
                    a, b = fill_range(step)
                    for i in range(a, b):
                        m, r = divmod(i, KD * 9)
                        n, r = divmod(r, KD * 3)
                        if r == 0:
                            if n == 0:
                                panel_ready(U_B + m, 2 * j)
                            pe.wait_ge(sm.evacuated, twelfths(U_B + m, 2 * j, 4 * n - 8))
                        k, r = divmod(r, 3)
                        slot = (U_B + m) % 2
                        w = (w_hi, w_hi, w_lo)[r][slot][:, k, :]
                        last = mm(pg[n][:, 0:TH], w, (act_hi, act_lo, act_hi)[r][:, k, cols(n)],
                                  start=k == 0 and r == 0, stop=k == KD - 1 and r == 2)
                        if k == KD - 1 and r == 2:
                            last.then_inc(sm.mm_done, 4)

                def per_head(f):
                    for h in range(H):
                        last = f(h, slice(h * P, (h + 1) * P))
                    return last

                for x in range(2):
                    c1 = 2 * j + x + 1
                    pe.wait_ge(sm.squared, 2 * c1)
                    if x == 0:
                        pe.wait_ge(sm.o_made, 2 * j + 1)
                    else:
                        pe.wait_ge(sm.at_made, 2 * j + 1)
                    mm(bk[0][:, :], ones[:, :], Tb[0][:, :, :], start=True, stop=True)
                    mm(bk[1][:, :], ones[:, :], Tb[1][:, :, :], start=True, stop=True)
                    pe.wait_ge(sm.diag_made, c1)
                    mm(bk[2][:, :], ones[:, :], X[x][:, :, :], start=True, stop=True) \
                        .then_inc(sm.norms_summed, 1)
                    fill(f"prep_norm{x}")
                    pe.wait_ge(sm.qk_made, 2 * c1)
                    per_head(lambda h, s: mm(bk[0][:, s], kn[x][:, h, :], kn[x][:, h, :], start=True, stop=True))
                    per_head(lambda h, s: mm(bk[1][:, s], kn[x][:, h, :], Tb[4][:, h, :], start=True, stop=True)) \
                        .then_inc(sm.kk_made, 1)
                    fill(f"prep_kk{x}")
                for x in range(2):
                    pe.wait_ge(sm.xt_made, 4 * j + 2 * x + 2)
                    per_head(lambda h, s: turn(bk[3 + x][:, s], XT[x][:, h, :], ident[:, :])) \
                        .then_inc(sm.xt_turned, 1)
                    fill(f"prep_x{x}")
                for l in range(1, LEVELS):
                    for x in range(2):
                        n1 = at(2 * (l - 1) + x + 1, j, 12)
                        pe.wait_ge(sm.lt_made, n1)
                        pe.wait_ge(sm.x_copied if l == 1 else sm.x_updated,
                                   at(x + 1, j, 2) if l == 1 else at(4 * (l - 2) + 2 * x + 2, j, 22))
                        per_head(lambda h, s: mm(bk[x][:, s], Tb[2 + x][:, h, :], X[x][:, h, :],
                                                 start=True, stop=True)).then_inc(sm.y_mm, 1)
                        fill(f"y{x}_{l}")
                    for x in range(2):
                        zb, ztb = (bk[2], bk[3]) if x == 0 else (bk[4], bk[1])
                        pe.wait_ge(sm.ycopy_made, at(2 * (l - 1) + x + 1, j, 12))
                        if l < LEVELS - 1:
                            per_head(lambda h, s: mm(zb[:, s], XT[x][:, h, :], Tb[x][:, h, :],
                                                     start=True, stop=True))
                        per_head(lambda h, s: mm(ztb[:, s], Tb[x][:, h, :], XT[x][:, h, :],
                                                 start=True, stop=True)).then_inc(sm.z_mm, 1)
                        fill(f"z{x}_{l}")
                for x in range(2):
                    c1 = 2 * j + x + 1
                    pe.wait_ge(sm.v_staged, c1)
                    pe.wait_ge(sm.x_updated, at(21 + x, j, 22))
                    pe.wait_ge(sm.s_updated, at(4 * x + 4, j, 8))
                    per_head(lambda h, s: turn(bk[4][:, s], kn[x][:, h, :], ident[:, :]))
                    per_head(lambda h, s: turn(bk[3][:, s], X[x][:, h, :], ident[:, :]))
                    per_head(lambda h, s: mm(bk[2][:, s], kn[x][:, h, :], S[:, h, :], start=True, stop=True)) \
                        .then_inc(sm.in_mm, 1)
                    fill(f"s_in{x}")
                    pe.wait_ge(sm.r_vec, 4 * c1)
                    pe.wait_ge(sm.o_made, 2 * j + x + 1)
                    per_head(lambda h, s: mm(bk[0][:, s], XT[x][:, h, :], Tb[0][:, h, :], start=True, stop=True)) \
                        .then_inc(sm.solve_mm, 1)
                    fill(f"s_solve{x}")
                    pe.wait_ge(sm.qg_made, 2 * j + x + 2)
                    pe.wait_ge(sm.vnew_made, c1)
                    pe.wait_ge(sm.ktok_made, c1)
                    pe.wait_ge(sm.o_made, 2 * j + x + 1)

                    def out_head(h, s):
                        mm(bk[1][:, s], S[:, h, :], qg[x][:, h, :], start=True, stop=False)
                        return mm(bk[1][:, s], Tb[1][:, h, :], PT[x][:, h, :], start=False, stop=True)

                    per_head(out_head)
                    per_head(lambda h, s: mm(bk[3][:, s], Tb[2][:, h, :], Tb[1][:, h, :], start=True, stop=True)) \
                        .then_inc(sm.out_mm, 1)
                    fill(f"s_out{x}")
                    pe.wait_ge(sm.o_squared, c1)
                    mm(bk[0][:, :], ones[:, :], Tb[4][:, :, :], start=True, stop=True).then_inc(sm.onorm_mm, 1)
                    fill(f"s_norm{x}")

            small = slice(0, H * TS)

            def hs(h):
                return slice(h * TS, (h + 1) * TS)

            T4 = [b[:, :, :].rearrange("p h t -> p (h t)") for b in Tb]
            knf, ATf, PTf, XTf, Xf = [b[0][:, :, :].rearrange("p h t -> p (h t)") for b in (kn, AT, PT, XT, X)]
            pe.wait_ge(sm.q_act, 2)
            pe.wait_ge(sm.q_dve, 1)
            pe.wait_ge(sm.o_made, NTT + 1)
            mm(bk[0][:, small], ones[:, :], T4[0][:, small], start=True, stop=True)
            mm(bk[1][:, small], ones[:, :], T4[1][:, small], start=True, stop=True)
            mm(bk[2][:, small], ones[0:TS, :], Xf[0:TS, small], start=True, stop=True).then_inc(sm.q_pe, 1)
            pe.wait_ge(sm.q_dve, 3)
            pe.wait_ge(sm.q_act, 6)
            for h in range(H):
                mm(bk[0][0:TS, hs(h)], knf[:, hs(h)], knf[:, hs(h)], start=True, stop=True)
            for h in range(H):
                mm(bk[1][0:TS, hs(h)], knf[:, hs(h)], T4[4][:, hs(h)], start=True, stop=True)
            for h in range(H):
                last = turn(bk[3][0:TS, h * P:(h + 1) * P], knf[:, hs(h)], ident[:, :])
            last.then_inc(sm.q_pe, 1)
            pe.wait_ge(sm.q_pool, 5)
            for h in range(H):
                last = turn(bk[0][0:TS, 256 + h * TS:256 + (h + 1) * TS], XTf[0:TS, hs(h)], ident[0:TS, 0:TS])
            last.then_inc(sm.q_pe, 1)
            pe.wait_ge(sm.q_dve, 7)
            pe.wait_ge(sm.sin_loaded, 16 * H)
            for h in range(H):
                for b in range(NB):
                    c = (h * NB + b) * 8
                    last = mm(bk[4][:, c:c + 8], S_in[:, h, b, :], T4[0][:, c:c + 8], start=True, stop=True)
            last.then_inc(sm.q_pe, 1)
            pe.wait_ge(sm.q_act, 9)
            for h in range(H):
                last = mm(bk[1][0:TS, 256 + h * TS:256 + (h + 1) * TS], T4[2][0:TS, hs(h)], Xf[0:TS, hs(h)],
                          start=True, stop=True)
            last.then_inc(sm.q_pe, 1)
            pe.wait_ge(sm.q_act, 10)
            for h in range(H):
                last = mm(bk[2][0:TS, hs(h)], T4[3][0:TS, hs(h)], XTf[0:TS, hs(h)], start=True, stop=True)
            last.then_inc(sm.q_pe, 1)
            pe.wait_ge(sm.q_dve, 8)
            for h in range(H):
                last = turn(bk[0][0:TS, h * P:(h + 1) * P], T4[1][:, hs(h)], ident[:, :])
            last.then_inc(sm.q_pe, 1)
            pe.wait_ge(sm.q_dve, 9)
            pe.wait_ge(sm.q_act, 11)
            for h in range(H):
                last = mm(bk[2][0:TS, h * P:(h + 1) * P], XTf[0:TS, hs(h)], T4[3][0:TS, h * P:(h + 1) * P],
                          start=True, stop=True)
            last.then_inc(sm.q_pe, 1)
            pe.wait_ge(sm.q_dve, 10)
            for h in range(H):
                last = mm(bk[1][:, hs(h)], T4[2][0:TS, h * P:(h + 1) * P], PTf[0:TS, hs(h)], start=True, stop=True)
            last.then_inc(sm.q_pe, 1)
            pe.wait_ge(sm.q_dve, 11)
            for i in range(2 * H):
                pe.wait_ge(sm.q_pool, 6 + i)
                if i >= 2:
                    pe.wait_ge(sm.s_out_made, i - 1)
                mm(bk[2 + i % 2][:, :], T4[0][0:TS, i // 2 * P:(i // 2 + 1) * P],
                   (AT, X)[i % 2][0][0:TS, :, :], start=True, stop=True).then_inc(sm.q_pe, 1)
            pe.wait_ge(sm.q_act, 12)
            mm(bk[0][:, small], ones[:, :], T4[4][:, small], start=True, stop=True).then_inc(sm.onorm_mm, 1)
            pe.wait_ge(sm.s_out_made, 2 * H)
            for i in range(NQ):
                if i % 4 == 0 and i > 0:
                    pe.wait_ge(sm.so_copied, i // 4)
                last = turn(bk[3][0:27, (i % 4) * P:(i % 4 + 1) * P], st_O[:, i, :], ident[:, :])
                if i % 4 == 3:
                    last.then_inc(sm.so_turned, 1)
            pe.wait_ge(sm.so_copied, 3)
            for i in range(NSC):
                last = turn(bk[3][0:18, i * P:(i + 1) * P], sc_O[:, i, :], ident[:, :])
            last.then_inc(sm.so_turned, 1)

            pieces = [[(0, 0, 128, 0), (1, 0, 128, 128), (2, 0, 96, 256)],
                      [(2, 96, 128, 0), (3, 0, 128, 32), (4, 0, 128, 160), (5, 0, 64, 288)],
                      [(5, 64, 128, 0), (6, 0, 128, 64), (7, 0, 128, 192), (8, 0, 32, 320)]]

            def out_unit(x, i):
                b = U_OUT + x
                panel_ready(b, i)
                for n in range(3):
                    pe.wait_ge(sm.mix_lo, KD)
                    group(b, i, 4 * n, 4, n, parts(b % 2, KD, 0, act_hi, act_lo, n))
                    pe.wait_ge(sm.consts_made, 3)
                    pe.wait_ge(xcol_in[x], at(32, i, 32))
                    for t, a, e, c in pieces[n]:
                        last = turn(bk[n][:, c:c + e - a], x_col[x][a:e, t, :], ident[a:e, a:e])
                    last.then_inc(sm.xcol_turned if n == 2 else sm.xcol_turned3, 1)

            with pe.Fori(0, KD // 2) as i:
                for x in range(2):
                    out_unit(x, i)

            def sum_squares():
                for n in range(3):
                    last = mm(bk[n][:, 0:TH], ones[:, :], ssq[:, cols(n)], start=True, stop=True)
                last.then_inc(sm.rms_mm, 1)

            pe.wait_ge(sm.ssq_added, 2 + 3 * KD)
            pe.wait_ge(sm.evacuated, 12 * U_MLP)
            sum_squares()
            for kind, c in MLP_ORDER:
                u = up_unit(c) if kind == "up" else down_unit(c)
                if kind == "up":
                    pe.wait_ge(sm.evacuated, 12 * u - 2)
                    with pe.Fori(0, FC // 2) as i:
                        for x in range(2):
                            unit(u + x, i, KD, act_hi, act_lo, lambda n: (sm.split_lo, KD * (n + 1)))
                else:
                    with pe.Fori(0, 2) as i:
                        for x in range(2):
                            unit(u + x, i, FC, u_hi[c % 2], u_lo[c % 2],
                                 lambda n: (sm.u_lo_made, 2 + 3 * FC * (c + 1)))
            pe.wait_ge(sm.ssq_added, 2 + 6 * KD)
            pe.wait_ge(sm.evacuated, 12 * U_PLE)
            sum_squares()
            for hf in range(2):
                u = U_PLE + 5 * hf
                pe.wait_ge(sm.evacuated, 12 * u)
                with pe.Fori(0, 2) as i:
                    for x in range(2):
                        unit(u + x, i, KD, act_hi, act_lo, lambda n: (sm.split_lo, 3 * KD + KD * (n + 1)))
                if hf == 0:
                    pe.wait_ge(sm.p_loaded, 16 * (NTT + 1))
                    pe.wait_ge(sm.rms_ready, 6)
                    for k in range(KP):
                        for t in range(NTT):
                            last = turn(bk[2 * k + t // 4][:, (t % 4) * P:(t % 4 + 1) * P],
                                        p_tok[t][:, k * P:(k + 1) * P], ident[:, :])
                    for k in range(KP):
                        last = turn(bk[4][:, k * TS:(k + 1) * TS], p_tok[NTT][0:TS, k * P:(k + 1) * P],
                                    ident[0:TS, 0:TS])
                    last.then_inc(sm.p_turned, 1)
                unit(u + 4, 0, KP, p_hi, p_lo, lambda n: (sm.p_lo_made, 6))
            pe.wait_ge(sm.ssq_added, 2 + 9 * KD)
            for t in range(NTT + 1):
                n = tokens(t)
                last = mm(bk[4][0:n, t:t + 1], ssq[:, t * P:t * P + n], ones[:, 0:1], start=True, stop=True)
            last.then_inc(sm.rt_mm, 1)
            pe.wait_ge(sm.x_scaled, 3 * KD)
            for t in range(NTT + 1):
                n = tokens(t)
                if t >= 2:
                    pe.wait_ge(sm.y_act, t - 1)
                    pe.wait_ge(sm.y_dve, t - 1)
                for k in range(KD):
                    last = turn(bk[2 * (t % 2) + k // 4][0:n, (k % 4) * P:(k % 4 + 1) * P],
                                xres[:, k, t * P:t * P + n], ident[:, :])
                last.then_inc(sm.y_turned, 1)

        @block.scalar
        def _(act):
            def op(out, in_, func, **kw):
                return nc.scalar.activation(out, in_, func, **kw)

            def split_w(b, p):
                if b >= 2:
                    act.wait_ge(sm.mm_done, twelfths(b - 1, p, 0))
                act.wait_ge(raw_in[b % 2], at(16 * (b // 2 + 1), p, 16))
                act.wait_ge(sm.consts_made, 3)
                op(w_hi[b % 2][:, :, :], w_raw[b % 2][:, :, :], ACT.Copy).then_inc(sm.w_hi_made, 1)

            def unit_done(b, p):
                if b + 2 + (2 * p if isinstance(p, int) else 0) < N_UNITS:
                    split_w(b + 2, p)

            act.wait_ge(sm.consts_made, 3)
            for t in range(NTT + 1):
                n = tokens(t)
                for hf in range(2):
                    i = 2 * t + hf
                    act.wait_ge(sm.xw_made, i + 1)
                    op(act_hi[:, 4 * hf:4 * hf + 4, t * P:t * P + n], Tb[i % 4][:, :, 0:n], ACT.Copy) \
                        .then_inc(sm.xhi_made, 1)
                if t == 0:
                    act.wait_ge(sm.r_tok_set, 2)
                else:
                    act.wait_ge(sm.x_squared, t)
                op(x_sqr[0:n, :], x_tok[t][0:n, :], ACT.Square, accum_out=r_tok[0:n, t:t + 1]) \
                    .then_inc(sm.x_squared, 1)
                if t == 3:
                    split_w(0, 0)
            act.wait_ge(sm.x_squared, NTT + 1)
            op(r_tok[:, :], r_tok[:, :], ACT.Sqrt, scale=1.0 / D, bias=eps[:, 0:1]).then_inc(sm.x_root, 1)
            split_w(1, 0)
            act.wait_ge(sm.st_turned, 1)
            op(st_T[:, :, :], bk[4][:, 0:288].rearrange("p (j b) -> p j b", j=NQ), ACT.Copy).then_inc(sm.st_ready, 1)
            op(sc_T[:, :, :], bk[4][:, 288:352].rearrange("p (j b) -> p j b", j=NSC), ACT.Copy) \
                .then_inc(sm.st_ready, 1)
            act.wait_ge(sm.r_spread, 1)
            op(r_b[:, 0:512], bk[0][:, :], ACT.Copy).then_inc(sm.r_ready, 1)
            op(r_b[:, 512:TP], bk[1][:, :], ACT.Copy).then_inc(sm.r_ready, 1)
            op(r_b[:, TP:T], bk[2][:, 0:TS], ACT.Copy).then_inc(sm.r_ready, 1)
            unit_done(0, 0)
            act.wait_ge(sm.ab_turned, 1)
            act.wait_ge(sm.buffers_zeroed, ZEROED)
            op(par[:, 0:NTT, :], bk[0][:, 0:64].rearrange("p (t c) -> p t c", t=NTT), ACT.Copy) \
                .then_inc(sm.ab_copied, 1)
            op(par[0:TS, NTT, :], bk[0][0:TS, 64:72], ACT.Copy).then_inc(sm.ab_copied, 1)
            act.wait_ge(sm.ab_copied, 2)
            act.wait_ge(sm.params_in, PARAMS)
            op(beta[:, :, :], par[:, :, H:2 * H], ACT.Exp, scale=-1.0).then_inc(sm.ab_exp, 1)
            op(alog[:, :], alog[:, :], ACT.Exp).then_inc(sm.ab_exp, 1)
            act.wait_ge(sm.chain, CHAIN_ABS)
            op(t_b[:, :, :], t_b[:, :, :], ACT.Exp, scale=-1.0).then_inc(sm.ab_exp, 1)
            with act.Fori(0, NQ // 2) as i:
                for x in range(2):
                    b = U_QKV + x
                    unit_done(b, i)
                    act.wait_ge(sm.conv_step, at(12 + 4 * x, i, 8))
                    act.wait_ge(sm.consts_made, 3)
                    j = ds(2 * i + x, 1)
                    op(qkv[:, j, 0:TP].rearrange("p a t -> p (a t)"), cv[x][:, 0:TP], ACT.Silu)
                    op(qkv[:, j, TP:T].rearrange("p a (b t) -> p (a b) t", t=NT), sample_cv(cv[x]), ACT.Silu) \
                        .then_inc(sm.silu_made, 1)
            act.wait_ge(sm.g_summed, 1)
            op(g_tok[:, 0:NTT, :], bk[0][:, 0:32].rearrange("p (t h) -> p t h", h=H), ACT.Copy).then_inc(sm.g_copied, 1)
            op(g_tok[0:TS, NTT, :], bk[0][0:TS, 32:36], ACT.Copy).then_inc(sm.g_copied, 1)
            act.wait_ge(sm.g_copied, 2)
            op(eneg[:, :, :], g_tok[:, :, :], ACT.Exp).then_inc(sm.g_exp, 1)
            act.wait_ge(sm.chain, CHAIN_G)
            op(kf[:, :], kf[:, :], ACT.Exp).then_inc(sm.g_exp, 1)

            with act.Fori(0, NSC) as j:
                def chunk_cols(x):
                    return ds(j * 2 * P + x * P, P)

                def squares(x):
                    op(Tb[0][:, :, :], qkv[:, 0:H, chunk_cols(x)], ACT.Square).then_inc(sm.squared, 1)
                    op(Tb[1][:, :, :], qkv[:, H:2 * H, chunk_cols(x)], ACT.Square).then_inc(sm.squared, 1)

                squares(0)
                for step in STEPS:
                    x = int(step[-1]) if step[0] not in "yz" else int(step[1])
                    c1 = 2 * j + x + 1
                    if step.startswith("prep_norm"):
                        act.wait_ge(sm.norms_summed, c1)
                        act.wait_ge(sm.consts_made, 3)
                        op(Tb[0][:, :, :], heads(bk[0]), ACT.Ln, bias=eps[:, 0:1]).then_inc(sm.rsq_made, 1)
                        op(Tb[1][:, :, :], heads(bk[1]), ACT.Ln, bias=eps[:, 0:1]).then_inc(sm.rsq_made, 1)
                        act.wait_ge(sm.qg_made, c1)
                        op(Tb[3][:, :, :], heads(bk[2]), ACT.Exp).then_inc(sm.eg_made, 1)
                        for i in range(2):
                            act.wait_ge(sm.rsq_made, at(4 * x + 1 + i, j, 8))
                            act.wait_ge(sm.consts_made, 3)
                            op(Tb[i][:, :, :], Tb[i][:, :, :], ACT.Exp, scale=-0.5).then_inc(sm.rsq_made, 1)
                        act.wait_ge(sm.diff_made, 4 * c1)
                        op(Tb[2][:, :, :], Tb[2][:, :, :], ACT.Exp).then_inc(sm.decay_made, 1)
                        if x == 0:
                            act.wait_ge(sm.qk_made, 2 * c1)
                            act.wait_ge(sm.consts_made, 3)
                            squares(1)
                    elif step.startswith("prep_x"):
                        act.wait_ge(sm.xt_turned, c1)
                        op(X[x][:, :, :], heads(bk[3 + x]), ACT.Copy).then_inc(sm.x_copied, 1)
                    elif step[0] == "y":
                        l = int(step[3:])
                        act.wait_ge(sm.y_mm, at(2 * (l - 1) + x + 1, j, 12))
                        op(Tb[x][:, :, :], heads(bk[x]), ACT.Copy).then_inc(sm.ycopy_made, 1)
                    elif step == f"z1_{LEVELS - 1}":
                        act.wait_ge(sm.z_mm, at(12, j, 12))
                        act.wait_ge(sm.consts_made, 3)
                        for xx in range(2):
                            op(X[xx][:, :, :], qkv[:, 2 * H:3 * H, chunk_cols(xx)], ACT.Copy).then_inc(sm.v_staged, 1)
                    elif step.startswith("s_in"):
                        act.wait_ge(sm.in_mm, c1)
                        op(Tb[3][:, :, :], heads(bk[3]), ACT.Copy).then_inc(sm.vtok_made, 1)
                    elif step.startswith("s_out"):
                        act.wait_ge(sm.out_mm, c1)
                        act.wait_ge(sm.qg_made, 2 * j + 3)
                        act.wait_ge(sm.o_made, c1)
                        op(Tb[4][:, :, :], heads(bk[1]), ACT.Square).then_inc(sm.o_squared, 1)
                    elif step.startswith("s_norm"):
                        act.wait_ge(sm.onorm_mm, c1)
                        act.wait_ge(sm.consts_made, 3)
                        op(Tb[4][:, :, :], heads(bk[0]), ACT.Ln, scale=1.0 / P, bias=eps[:, 0:1]) \
                            .then_inc(sm.o_rs_made, 1)
                        act.wait_ge(sm.o_rs_made, at(2 * x + 1, j, 4))
                        act.wait_ge(sm.consts_made, 3)
                        op(Tb[4][:, :, :], Tb[4][:, :, :], ACT.Exp, scale=-0.5).then_inc(sm.o_rs_made, 1)
                    for t in thirds_after(step):
                        if t % 3 == 2:
                            unit_done(U_B + t // 3, 2 * j)

            F = [flat(b) for b in Tb]
            sm_q, sm_k = qkv[:, 0:H, TP:T], qkv[:, H:2 * H, TP:T]
            act.wait_ge(sm.o_made, NTT + 1)
            op(hsmall(F[0][:, 0:SMALL]), sm_q, ACT.Square).then_inc(sm.q_act, 1)
            op(hsmall(F[1][:, 0:SMALL]), sm_k, ACT.Square).then_inc(sm.q_act, 1)
            act.wait_ge(sm.q_pe, 1)
            for i in range(2):
                op(F[i][:, 0:SMALL], bk[i][:, 0:SMALL], ACT.Ln, bias=eps[:, 0:1]).then_inc(sm.q_act, 1)
            for i in range(2):
                act.wait_ge(sm.q_act, 3 + i)
                op(F[i][:, 0:SMALL], F[i][:, 0:SMALL], ACT.Exp, scale=-0.5).then_inc(sm.q_act, 1)
            op(flat(qg[0])[:, 0:SMALL], bk[2][:, 0:SMALL], ACT.Exp).then_inc(sm.q_act, 1)
            act.wait_ge(sm.diff_made, 4 * (NTT + 1))
            op(F[2][0:TS, 0:SMALL], F[2][0:TS, 0:SMALL], ACT.Exp).then_inc(sm.q_act, 1)
            act.wait_ge(sm.q_pe, 3)
            op(flat(X[0])[0:TS, 0:SMALL], bk[0][0:TS, 256:256 + SMALL], ACT.Copy).then_inc(sm.q_act, 1)
            act.wait_ge(sm.q_pe, 5)
            op(F[3][0:TS, 0:SMALL], bk[1][0:TS, 256:256 + SMALL], ACT.Copy).then_inc(sm.q_act, 1)
            act.wait_ge(sm.q_pe, 7)
            op(F[3][0:TS, :], bk[0][0:TS, :], ACT.Copy).then_inc(sm.q_act, 1)
            act.wait_ge(sm.q_dve, 12)
            op(F[4][:, 0:SMALL], F[1][:, 0:SMALL], ACT.Square).then_inc(sm.q_act, 1)
            act.wait_ge(sm.onorm_mm, NTT + 1)
            op(F[4][:, 0:SMALL], bk[0][:, 0:SMALL], ACT.Ln, scale=1.0 / P, bias=eps[:, 0:1]).then_inc(sm.q_act, 1)
            act.wait_ge(sm.q_act, 13)
            op(F[4][:, 0:SMALL], F[4][:, 0:SMALL], ACT.Exp, scale=-0.5).then_inc(sm.q_act, 1)
            for i, buf in enumerate((kn[1], AT[1], PT[1], qg[1])):
                n = 27 if i < 3 else 18
                act.wait_ge(sm.so_turned, i + 1)
                op(flat(buf)[0:n, :], bk[3][0:n, :], ACT.Copy).then_inc(sm.so_copied, 1)

            for i in range(NSC):
                act.wait_ge(sm.yt_loaded, 16 * NSC)
                act.wait_ge(sm.mm_done, 12 * U_OUT)
                op(act_hi[:, H + i, :], zst[i][:, :], ACT.Copy).then_inc(sm.mix_hi, 1)
            for i in range(H):
                act.wait_ge(sm.zt_loaded, 16 * H)
                op(zst[i][:, :], zst[i][:, :], ACT.Silu).then_inc(sm.z_silu, 1)
            for i in range(H):
                act.wait_ge(sm.gated, i + 1)
                op(act_hi[:, i, :], qkv[:, i, :], ACT.Copy).then_inc(sm.mix_hi, 1)

            def rms(scale_count):
                act.wait_ge(sm.rms_mm, scale_count)
                for n in range(3):
                    op(r_b[:, cols(n)], bk[n][:, 0:TH], ACT.Ln, scale=1.0 / D, bias=eps[:, 0:1]) \
                        .then_inc(sm.rms_log, 1)
                for n in range(3):
                    act.wait_ge(sm.rms_log, 3 * scale_count)
                    op(r_b[:, cols(n)], r_b[:, cols(n)], ACT.Exp, scale=-0.5).then_inc(sm.rms_ready, 1)

            def split_x(gain, n):
                for k in range(KD):
                    op(act_hi[:, k, cols(n)], xres[:, k, cols(n)], ACT.Copy, scale=gain[:, k:k + 1]) \
                        .then_inc(sm.split_hi, 1)

            x_flat = xres[:, :, :].rearrange("p k t -> p (k t)")
            with act.Fori(0, KD // 2) as i:
                for x in range(2):
                    b = U_OUT + x
                    for n in range(3):
                        g = 3 * x + n
                        act.wait_ge(sm.xcol_turned if n == 2 else sm.xcol_turned3,
                                    at(x + 1, i, 2) if n == 2 else at(2 * x + n + 1, i, 4))
                        act.wait_ge(sm.consts_made, 3)
                        op(xres[:, ds(2 * i + x, 1), cols(n)].rearrange("p a t -> p (a t)"), bk[n][:, 0:TH],
                           ACT.Copy).then_inc(sm.xr_copied, 1)
                    for n in range(3):
                        g = 3 * x + n
                        if n == 2:
                            unit_done(b, i)
                        act.wait_ge(sm.evacuated, twelfths(b, i, 4 * n + 4))
                        act.wait_ge(sm.ssq_added, at(g + 1, i, 6))
                        if x == 0:
                            op(token[:, 16 + n:17 + n], token[:, 13:14], ACT.Copy)
                        op(sq[g % 2][:, :], x_flat[:, ds(i * 2 * T + x * T + n * TH, TH)], ACT.Square) \
                            .then_inc(sm.sq_made, 1)
            split_x(n_mlp, 0)
            rms(1)
            split_x(n_mlp, 1)
            split_x(n_mlp, 2)

            ups = 0
            for kind, c in MLP_ORDER:
                u = up_unit(c) if kind == "up" else down_unit(c)
                if kind == "up":
                    with act.Fori(0, FC // 2) as i:
                        for x in range(2):
                            for n in range(3):
                                g = 3 * x + n
                                base = ups + g + 1
                                act.wait_ge(sm.evacuated, twelfths(u + x, i, 4 * n + 4))
                                act.wait_ge(sm.u_lo_made, at(base, i, 6))
                                op(sq[g % 2][:, :], tm[g % 2][:, :], ACT.Square).then_inc(sm.usq_made, 1)
                                act.wait_ge(sm.usq_made, at(2 + base, i, 6))
                                if c >= 2 and n == 0:
                                    act.wait_ge(sm.mm_done, 12 * (down_unit(c - 2) + 4))
                                act.wait_ge(sm.consts_made, 3)
                                op(u_hi[c % 2][:, ds(2 * i + x, 1), cols(n)].rearrange("p a t -> p (a t)"),
                                   sq[g % 2][:, :], ACT.Copy).then_inc(sm.u_hi_made, 1)
                            unit_done(u + x, i)
                    ups += 3 * FC
                else:
                    with act.Fori(0, 2) as i:
                        for x in range(2):
                            if c == NFC - 1:
                                for g in range(6):
                                    act.wait_ge(sm.evacuated, twelfths(u + x, i, 2 * g + 2))
                                    act.wait_ge(sm.ssq_added, at(3 * KD + 6 * x + g + 1, i, 12))
                                    act.wait_ge(sm.consts_made, 3)
                                    k = ds(4 * i + 2 * x + g // 3, 1)
                                    op(sq[g % 2][:, :], xres[:, k, cols(g % 3)].rearrange("p a t -> p (a t)"),
                                       ACT.Square).then_inc(sm.sq_made, 1)
                            unit_done(u + x, i)
            split_x(n_ple, 0)
            rms(2)
            split_x(n_ple, 1)
            split_x(n_ple, 2)

            for hf in range(2):
                u = U_PLE + 5 * hf

                def gates(i):
                    for x in range(2):
                        for n in range(3):
                            act.wait_ge(sm.evacuated, twelfths(u + x, i, 4 * n + 4))
                            act.wait_ge(sm.consts_made, 3)
                            op(gate[:, ds(2 * i + x, 1), cols(n)].rearrange("p a t -> p (a t)"),
                               tm[(3 * x + n) % 2][:, :], ACT.Sigmoid).then_inc(sm.gate_made, 1)
                        unit_done(u + x, i)

                if hf == 0:
                    with act.Fori(0, 2) as i:
                        gates(i)
                else:
                    for i in range(2):
                        gates(i)
                if hf == 0:
                    act.wait_ge(sm.p_turned, 1)
                    for k in range(KP):
                        for i in range(2):
                            op(p_hi[:, k, i * 512:(i + 1) * 512], bk[2 * k + i][:, :], ACT.Copy) \
                                .then_inc(sm.p_hi_made, 1)
                    for k in range(KP):
                        op(p_hi[:, k, TP:T], bk[4][:, k * TS:(k + 1) * TS], ACT.Copy).then_inc(sm.p_hi_made, 1)
                for g in range(12):
                    k = 4 * hf + g // 3
                    act.wait_ge(sm.x_made, 12 * hf + g + 1)
                    act.wait_ge(sm.ssq_added, 6 * KD + 12 * hf + g + 1)
                    op(sq[g % 2][:, :], xres[:, k, cols(g % 3)], ACT.Square).then_inc(sm.sq_made, 1)
                    act.wait_ge(sm.sq_made, 6 * KD + 12 * hf + g + 1)
                    op(xres[:, k, cols(g % 3)], xres[:, k, cols(g % 3)], ACT.Copy, scale=n_fin[:, k:k + 1]) \
                        .then_inc(sm.x_scaled, 1)
                unit_done(u + 4, 0)
            act.wait_ge(sm.rt_mm, 1)
            op(r_tok[:, 0:NTT], bk[4][:, 0:NTT], ACT.Sqrt, scale=1.0 / D, bias=eps[:, 0:1]).then_inc(sm.rt_root, 1)
            op(r_tok[0:TS, NTT:NPAR], bk[4][0:TS, NTT:NPAR], ACT.Sqrt, scale=1.0 / D, bias=eps[0:TS, 0:1]) \
                .then_inc(sm.rt_root, 1)
            act.wait_ge(sm.rt_ready, 1)
            for t in range(NTT + 1):
                n = tokens(t)
                act.wait_ge(sm.y_turned, t + 1)
                if t >= 3:
                    act.wait_ge(y_sent[t % 3], 16 * (t // 3))
                op(y_tok[t % 3][0:n, 0:512], bk[2 * (t % 2)][0:n, :], ACT.Copy, scale=r_tok[0:n, t:t + 1]) \
                    .then_inc(sm.y_act, 1)

        @block.vector
        def _(dve):
            tt, ts_, stt = nc.vector.tensor_tensor, nc.vector.tensor_scalar, nc.vector.scalar_tensor_tensor

            def split_w(b, p):
                dve.wait_ge(sm.w_hi_made, at(b + 1, p, 2))
                tt(w_lo[b % 2][:, :, :], w_raw[b % 2][:, :, :], w_hi[b % 2][:, :, :].bitcast(f32), SUB) \
                    .then_inc(sm.w_lo_made, 1)

            def unit_done(b, p):
                if b + 2 + (2 * p if isinstance(p, int) else 0) < N_UNITS:
                    split_w(b + 2, p)

            def product_ready(b, p, q):
                dve.wait_ge(sm.mm_done, twelfths(b, p, q))

            steps = [0]

            def link(ins):
                steps[0] += 1
                ins.then_inc(sm.chain, 1)
                dve.wait_ge(sm.chain, steps[0])

            dve.wait_ge(sm.gain_in, 16)
            for t in range(NTT + 1):
                n = tokens(t)
                for hf in range(2):
                    i = 2 * t + hf
                    dve.wait_ge(sm.x_turned, i + 1)
                    if i >= 4:
                        dve.wait_ge(sm.xlo_odd if hf else sm.xlo_even, t - 1)
                    tt(Tb[i % 4][:, :, 0:n], heads(bk[i % 4])[:, :, 0:n], spread(n_mix[:, 4 * hf:4 * hf + 4], n), MUL) \
                        .then_inc(sm.xw_made, 1)
                dve.wait_ge(sm.xhi_made, 2 * t + 1)
                tt(act_lo[:, 0:4, t * P:t * P + n], Tb[2 * t % 4][:, :, 0:n],
                   act_hi[:, 0:4, t * P:t * P + n].bitcast(f32), SUB).then_inc(sm.xlo_even, 1)
                if t == 3:
                    split_w(0, 0)
            dve.wait_ge(sm.x_root, 1)
            nc.vector.reciprocal(r_tok[:, :], r_tok[:, :]).then_inc(sm.r_made, 1)
            dve.wait_ge(sm.r_made, 1)
            dve.wait_ge(sm.xlo_odd, NTT + 1)
            dve.wait_ge(sm.xlo_even, NTT + 1)
            for i in range(2):
                tt(Tb[i][:, :, :], ident[:, None, :].to_broadcast([P, 4, P]), spread(r_tok[:, 4 * i:4 * i + 4], P),
                   MUL).then_inc(sm.rdiag_made, 1)
            ts_(Tb[2][0:TS, 0, 0:TS], ident[0:TS, 0:TS], r_tok[0:TS, NTT:NPAR], None, MUL).then_inc(sm.rdiag_made, 1)
            split_w(1, 0)
            dve.wait_ge(sm.r_ready, 3)
            for n in range(3):
                product_ready(0, 0, 4 * n + 4)
                tt(cv[0][0:8, cols(n)], pg[n][0:8, 0:TH], r_b[0:8, cols(n)], MUL).then_inc(sm.evacuated, 4)
            unit_done(0, 0)
            dve.wait_ge(sm.ab_copied, 2)
            dve.wait_ge(sm.params_in, PARAMS)
            link(tt(t_a[:, :, :], par[:, :, 0:H], dtb[:, None, :].to_broadcast([P, NPAR, H]), ADD))
            link(ts_(t_b[:, :, :], t_a[:, :, :], -1.0, None, MUL))
            link(tt(t_b[:, :, :], t_b[:, :, :], t_a[:, :, :], MAX))
            assert steps[0] == CHAIN_ABS
            dve.wait_ge(sm.ab_exp, 3)
            link(ts_(t_c[:, :, :], t_b[:, :, :], 2.0, None, ADD))
            link(nc.vector.reciprocal(t_c[:, :, :], t_c[:, :, :]))
            link(tt(t_b[:, :, :], t_b[:, :, :], t_c[:, :, :], MUL))
            link(tt(t_c[:, :, :], t_b[:, :, :], t_b[:, :, :], MUL))
            link(ts_(log_a[:, :, :], t_c[:, :, :], 1.0 / 19, None, MUL))
            for d in (17, 15, 13, 11, 9, 7, 5, 3):
                link(stt(log_a[:, :, :], log_a[:, :, :], 1.0 / d, t_c[:, :, :], ADD, MUL))
            link(stt(log_a[:, :, :], log_a[:, :, :], 1.0, t_b[:, :, :], ADD, MUL))
            link(ts_(t_a[:, :, :], t_a[:, :, :], 0.0, None, MAX))
            link(stt(log_a[:, :, :], log_a[:, :, :], 2.0, t_a[:, :, :], MUL, ADD))
            link(stt(log_a[:, :, :], log_a[:, :, :], -1.0, alog[:, None, :].to_broadcast([P, NPAR, H]), MUL, MUL))
            assert steps[0] == CHAIN_LOG_A
            link(ts_(beta[:, :, :], beta[:, :, :], 1.0, None, ADD))
            link(nc.vector.reciprocal(beta[:, :, :], beta[:, :, :]))

            def to_columns(buf, n, b, p, inc):
                a = n * TH
                e = min(a + TH, TP)
                last = tt(buf[:, PAD + a:PAD + e], pg[n][:, 0:e - a], r_b[:, a:e], MUL)
                if n == 2:
                    last = tt(samples(buf)[:, :, PAD:SEG], pg[n][:, e - a:TH].rearrange("p (b t) -> p b t", t=NT),
                              r_b[:, TP:T].rearrange("p (b t) -> p b t", t=NT), MUL)
                last.then_inc(sm.evacuated, inc)

            with dve.Fori(0, NQ // 2) as i:
                for x in range(2):
                    b = U_QKV + x
                    dve.wait_ge(sm.state_put, at(x + 1, i, 2))
                    for n in range(3):
                        product_ready(b, i, 4 * n + 4)
                        to_columns(pre[x], n, b, i, 4)
                    unit_done(b, i)
                    dve.wait_ge(sm.evacuated, twelfths(b, i, 12))
                    dve.wait_ge(sm.silu_made, at(x + 1, i, 2))
                    j = ds(2 * i + x, 1)

                    def tap(w):
                        return cq_w[:, j, w:w + 1].rearrange("p a w -> p (a w)")

                    ts_(cv[x][:, 0:CV], pre[x][:, 0:CV], tap(0), None, MUL).then_inc(sm.conv_step, 1)
                    for w in range(1, CW):
                        dve.wait_ge(sm.conv_step, at(8 + 4 * x + w, i, 8))
                        stt(cv[x][:, 0:CV], pre[x][:, w:w + CV], tap(w), cv[x][:, 0:CV], MUL, ADD) \
                            .then_inc(sm.conv_step, 1)
            dve.wait_ge(sm.g_copied, 2)
            link(tt(kf[:, :], bk[0][0:TS, 36:40], g_tok[0:TS, NTT, :], SUB))
            assert steps[0] == CHAIN_G
            dve.wait_ge(sm.g_exp, 1)
            link(ts_(eneg[:, :, :], eneg[:, :, :], -1.0, None, MUL))
            dve.wait_ge(sm.silu_made, NQ + 2)

            def chunk(ap, c):
                return ap[:, c, :].rearrange("p a h -> p (a h)")

            def third(t, j):
                m, n = divmod(t, 3)
                b, p = U_B + m, 2 * j
                product_ready(b, p, 4 * n + 4)
                if m == 2:
                    if n == 0:
                        dve.wait_ge(sm.sc_put, j + 1)
                    to_columns(pre[1], n, b, p, 4)
                else:
                    if t == 0:
                        dve.wait_ge(sm.y_made, 3 * j + 3)
                    if t == 9:
                        dve.wait_ge(sm.ch_made, 3 * j + 3)
                    tt(cv[0 if m == 0 else 1][:, cols(n)], pg[n][:, 0:TH], r_b[:, cols(n)], MUL) \
                        .then_inc(sm.evacuated, 4)
                if n == 2:
                    unit_done(b, p)
                if t == 9:
                    dve.wait_ge(sm.z_spilled, 16 * j + 16)
                    for w in range(SW):
                        tap = cs_w[:, ds(j, 1), w:w + 1].rearrange("p a w -> p (a w)")
                        src = pre[1][:, w + 1:w + 1 + CV]
                        if w == 0:
                            ts_(cv[0][:, 0:CV], src, tap, None, MUL).then_inc(sm.sc_step, 1)
                        else:
                            dve.wait_ge(sm.sc_step, at(w, j, 3))
                            stt(cv[0][:, 0:CV], src, tap, cv[0][:, 0:CV], MUL, ADD).then_inc(sm.sc_step, 1)

            with dve.Fori(0, NSC) as j:
                def diagonal(x):
                    tt(X[x][:, :, :], ident[:, None, :].to_broadcast([P, H, P]),
                       spread(chunk(g_tok, ds(2 * j + x, 1)), P), MUL).then_inc(sm.diag_made, 1)

                diagonal(0)
                for step in STEPS:
                    x = int(step[-1]) if step[0] not in "yz" else int(step[1])
                    c1 = 2 * j + x + 1
                    c = ds(2 * j + x, 1)
                    tok = ds(j * 2 * P + x * P, P)
                    if step.startswith("prep_norm"):
                        if x == 0:
                            diagonal(1)
                        dve.wait_ge(sm.norms_summed, c1)
                        dve.wait_ge(sm.last_kept, at(2 * x + 1, j, 4))
                        dve.wait_ge(sm.eg_made, c1)
                        for h in range(H):
                            ts_(Tb[2][:, h, :], bk[2][:, h * P:(h + 1) * P],
                                g_tok[:, c, h:h + 1].rearrange("p a h -> p (a h)"), 0.0, SUB, MIN) \
                                .then_inc(sm.diff_made, 1)
                        dve.wait_ge(sm.rsq_made, 4 * c1)
                        dve.wait_ge(sm.qg_made, c1)
                        for h in range(H):
                            last = stt(Tb[4][:, h, :], qkv[:, h, tok], QSCALE, Tb[0][:, h, :], MUL, MUL)
                        last.then_inc(sm.qk_made, 1)
                        tt(kn[x][:, :, :], qkv[:, H:2 * H, tok], Tb[1][:, :, :], MUL).then_inc(sm.qk_made, 1)
                    elif step.startswith("prep_kk"):
                        dve.wait_ge(sm.kk_made, c1)
                        dve.wait_ge(sm.masked, c1)
                        tt(PT[x][:, :, :], heads(bk[1]), Tb[2][:, :, :], MUL).then_inc(sm.pt_made, 1)
                        dve.wait_ge(sm.at_scaled, c1)
                        tt(AT[x][:, :, :], heads(bk[0]), AT[x][:, :, :], MUL).then_inc(sm.at_made, 1)
                    elif step[0] == "z":
                        l = int(step[3:])
                        dve.wait_ge(sm.z_mm, at(2 * (l - 1) + x + 1, j, 12))
                        zb, ztb = (bk[2], bk[3]) if x == 0 else (bk[4], bk[1])
                        if l == 1:
                            dve.wait_ge(sm.x_copied, c1)
                        if l > 1:
                            dve.wait_ge(sm.x_updated, at(4 * (l - 2) + 2 * x + 2, j, 22))
                        if l < LEVELS - 1:
                            tt(X[x][:, :, :], X[x][:, :, :], heads(zb), SUB).then_inc(sm.x_updated, 1)
                        tt(XT[x][:, :, :], XT[x][:, :, :], heads(ztb), SUB).then_inc(sm.x_updated, 1)
                    elif step.startswith("s_in"):
                        dve.wait_ge(sm.in_mm, c1)
                        tt(Tb[2][:, :, :], heads(bk[4]), spread(ktl[x][:, :], P), MUL).then_inc(sm.ktok_made, 1)
                        dve.wait_ge(sm.vtok_made, c1)
                        for h in range(H):
                            stt(Tb[0][:, h, :], bk[2][:, h * P:(h + 1) * P],
                                eneg[:, c, h:h + 1].rearrange("p a h -> p (a h)"), Tb[3][:, h, :], MUL, ADD) \
                                .then_inc(sm.r_vec, 1)
                    elif step.startswith("s_solve"):
                        dve.wait_ge(sm.solve_mm, c1)
                        tt(Tb[1][:, :, :], heads(bk[0]), spread(chunk(beta, c), P), MUL).then_inc(sm.vnew_made, 1)
                    elif step.startswith("s_out"):
                        dve.wait_ge(sm.out_mm, c1)
                        for h in range(H):
                            stt(S[:, h, :], S[:, h, :], egl[x][:, h:h + 1], bk[3][:, h * P:(h + 1) * P], MUL, ADD) \
                                .then_inc(sm.s_updated, 1)
                    elif step.startswith("s_norm"):
                        dve.wait_ge(sm.o_rs_made, at(2 * x + 2, j, 4))
                        tt(qkv[:, 0:H, tok], heads(bk[1]), Tb[4][:, :, :], MUL).then_inc(sm.o_made, 1)
                    for t in thirds_after(step):
                        third(t, j)

            F = [flat(b) for b in Tb]
            X0, XT0, AT0, PT0, G0 = [flat(b[0]) for b in (X, XT, AT, PT, qg)]
            sq_, sk_, sv_ = [qkv[:, a * H:(a + 1) * H, TP:T] for a in range(3)]
            tt(hsmall(X0[0:TS, 0:SMALL]), ident[0:TS, None, 0:TS].to_broadcast([TS, H, TS]),
               spread(g_tok[0:TS, NTT, :], TS), MUL).then_inc(sm.q_dve, 1)
            dve.wait_ge(sm.q_pe, 1)
            dve.wait_ge(sm.q_act, 7)
            for h in range(H):
                ts_(F[2][0:TS, h * TS:(h + 1) * TS], bk[2][0:TS, h * TS:(h + 1) * TS], g_tok[0:TS, NTT, h:h + 1],
                    0.0, SUB, MIN).then_inc(sm.diff_made, 1)
            dve.wait_ge(sm.q_act, 6)
            stt(hsmall(F[4][:, 0:SMALL]), sq_, QSCALE, hsmall(F[0][:, 0:SMALL]), MUL, MUL).then_inc(sm.q_dve, 1)
            tt(hsmall(flat(kn[0])[:, 0:SMALL]), sk_, hsmall(F[1][:, 0:SMALL]), MUL).then_inc(sm.q_dve, 1)
            dve.wait_ge(sm.q_pe, 2)
            dve.wait_ge(sm.q_pool, 1)
            tt(PT0[0:TS, 0:SMALL], bk[1][0:TS, 0:SMALL], F[2][0:TS, 0:SMALL], MUL).then_inc(sm.q_dve, 1)
            dve.wait_ge(sm.q_pool, 2)
            tt(AT0[0:TS, 0:SMALL], bk[0][0:TS, 0:SMALL], AT0[0:TS, 0:SMALL], MUL).then_inc(sm.q_dve, 1)
            dve.wait_ge(sm.q_act, 7)
            dve.wait_ge(sm.q_dve, 3)
            kq = F[0][:, 0:2 * SMALL].rearrange("p (h b a t) -> p (h b) a t", b=NB, a=2, t=NT)

            def by_sequence(ap):
                return ap.rearrange("p (hb t) -> p hb t", t=NT)

            for a, src in enumerate((flat(kn[0]), F[4])):
                tt(kq[:, :, a, :], by_sequence(src[:, 0:SMALL]), by_sequence(G0[:, 0:SMALL]), MUL).then_inc(sm.q_dve, 1)
            dve.wait_ge(sm.q_pe, 4)
            kqs = bk[4][:, 0:2 * SMALL].rearrange("p (h b a t) -> p h b a t", h=H, a=2, t=NT)
            for h in range(H):
                last = tt(F[1][:, h * TS:(h + 1) * TS].rearrange("p (b t) -> p b t", t=NT),
                          sv_[:, h, :].rearrange("p (b t) -> p b t", t=NT), kqs[:, h, :, 0, :], SUB)
            last.then_inc(sm.q_dve, 1)
            dve.wait_ge(sm.q_pe, 6)
            tt(XT0[0:TS, 0:SMALL], XT0[0:TS, 0:SMALL], bk[2][0:TS, 0:SMALL], SUB).then_inc(sm.q_dve, 1)
            dve.wait_ge(sm.q_pe, 8)
            tt(heads(F[2])[0:TS], heads(bk[2])[0:TS], spread(beta[0:TS, NTT, :], P), MUL).then_inc(sm.q_dve, 1)
            tt(heads(F[0])[0:TS], heads(bk[3])[0:TS], spread(kf[:, :], P), MUL).then_inc(sm.q_dve, 1)
            dve.wait_ge(sm.q_pe, 9)
            link(nc.vector.tensor_copy(F[1][:, 0:SMALL], bk[1][:, 0:SMALL]))
            tt(by_sequence(F[1][:, 0:SMALL]), by_sequence(F[1][:, 0:SMALL]),
               bk[4][:, 0:2 * SMALL].rearrange("p (hb a t) -> p hb a t", a=2, t=NT)[:, :, 1, :], ADD) \
                .then_inc(sm.q_dve, 1)
            gl = G0[:, 0:SMALL].rearrange("p (h b t) -> p h b t", h=H, t=NT)
            for h in range(H):
                tt(S_in[:, h, :, :], S_in[:, h, :, :], gl[:, h, :, NT - 1:NT].to_broadcast([P, NB, P]), MUL) \
                    .then_inc(sm.q_dve, 1)
            for i in range(2 * H):
                dve.wait_ge(sm.q_pe, 10 + i)
                dve.wait_ge(sm.q_dve, 13 + i // 2)
                part = S_in[:, i // 2, 4 * (i % 2):4 * (i % 2) + 4, :]
                tt(part, part, heads(bk[2 + i % 2]), ADD).then_inc(sm.s_out_made, 1)
            dve.wait_ge(sm.q_act, 14)
            tt(qkv[:, 0:H, TP:T], hsmall(F[1][:, 0:SMALL]), hsmall(F[4][:, 0:SMALL]), MUL).then_inc(sm.o_made, 1)

            dve.wait_ge(sm.o_made, NTT + 2)
            for i in range(NSC):
                dve.wait_ge(sm.mix_hi, i + 1)
                tt(act_lo[:, H + i, :], zst[i][:, :], act_hi[:, H + i, :].bitcast(f32), SUB).then_inc(sm.mix_lo, 1)
            for i in range(H):
                dve.wait_ge(sm.z_silu, i + 1)
                stt(qkv[:, i, :], qkv[:, i, :], gnw[:, 0:1], zst[i][:, :], MUL, MUL).then_inc(sm.gated, 1)
            for i in range(H):
                dve.wait_ge(sm.mix_hi, NSC + i + 1)
                tt(act_lo[:, i, :], qkv[:, i, :], act_hi[:, i, :].bitcast(f32), SUB).then_inc(sm.mix_lo, 1)

            def split_x(gain, n, count):
                for k in range(KD):
                    dve.wait_ge(sm.split_hi, count + KD * n + k + 1)
                    stt(act_lo[:, k, cols(n)], xres[:, k, cols(n)], gain[:, k:k + 1],
                        act_hi[:, k, cols(n)].bitcast(f32), MUL, SUB).then_inc(sm.split_lo, 1)

            def rows(ap):
                return ap.rearrange("p a t -> p (a t)")

            with dve.Fori(0, KD // 2) as i:
                for x in range(2):
                    b = U_OUT + x
                    for n in range(3):
                        product_ready(b, i, 4 * n + 4)
                        dve.wait_ge(sm.xr_copied, at(3 * x + n + 1, i, 6))
                        x_t = rows(xres[:, ds(2 * i + x, 1), cols(n)])
                        tt(x_t, x_t, pg[n][:, 0:TH], ADD).then_inc(sm.evacuated, 4)
                    unit_done(b, i)
            split_x(n_mlp, 0, 0)
            split_x(n_mlp, 1, 0)
            split_x(n_mlp, 2, 0)
            ups = 0
            for kind, c in MLP_ORDER:
                u = up_unit(c) if kind == "up" else down_unit(c)
                if kind == "up":
                    with dve.Fori(0, FC // 2) as i:
                        for x in range(2):
                            for n in range(3):
                                g = 3 * x + n
                                if c == 0:
                                    dve.wait_ge(sm.rms_ready, n + 1)
                                product_ready(u + x, i, 4 * n + 4)
                                dve.wait_ge(sm.usq_made, at(ups + g + 1, i, 6))
                                stt(tm[g % 2][:, :], pg[n][:, 0:TH], 0.0, r_b[:, cols(n)], MAX, MUL) \
                                    .then_inc(sm.evacuated, 4)
                                dve.wait_ge(sm.u_hi_made, at(ups + g + 1, i, 6))
                                k = ds(2 * i + x, 1)
                                tt(rows(u_lo[c % 2][:, k, cols(n)]), sq[g % 2][:, :],
                                   rows(u_hi[c % 2][:, k, cols(n)]).bitcast(f32), SUB).then_inc(sm.u_lo_made, 1)
                            unit_done(u + x, i)
                    ups += 3 * FC
                else:
                    with dve.Fori(0, 2) as i:
                        for x in range(2):
                            for g in range(6):
                                product_ready(u + x, i, 2 * g + 2)
                                x_t = rows(xres[:, ds(4 * i + 2 * x + g // 3, 1), cols(g % 3)])
                                tt(x_t, x_t, pg[g % 3][:, 0:TH], ADD).then_inc(sm.evacuated, 2)
                            unit_done(u + x, i)
            split_x(n_ple, 0, 3 * KD)
            split_x(n_ple, 1, 3 * KD)
            split_x(n_ple, 2, 3 * KD)
            for hf in range(2):
                u = U_PLE + 5 * hf

                def gates(i):
                    for x in range(2):
                        for n in range(3):
                            g = 3 * x + n
                            if hf == 0:
                                dve.wait_ge(sm.rms_ready, 3 + n + 1)
                            product_ready(u + x, i, 4 * n + 4)
                            dve.wait_ge(sm.gate_made, at(12 * hf + g + 1, i, 6))
                            tt(tm[g % 2][:, :], pg[n][:, 0:TH], r_b[:, cols(n)], MUL).then_inc(sm.evacuated, 4)
                        unit_done(u + x, i)

                if hf == 0:
                    with dve.Fori(0, 2) as i:
                        gates(i)
                else:
                    for i in range(2):
                        gates(i)
                if hf == 0:
                    for k in range(KP):
                        for i in range(2):
                            dve.wait_ge(sm.p_hi_made, 2 * k + i + 1)
                            tt(p_lo[:, k, i * 512:(i + 1) * 512], bk[2 * k + i][:, :],
                               p_hi[:, k, i * 512:(i + 1) * 512].bitcast(f32), SUB).then_inc(sm.p_lo_made, 1)
                    for k in range(KP):
                        dve.wait_ge(sm.p_hi_made, 3 * KP)
                        tt(p_lo[:, k, TP:T], bk[4][:, k * TS:(k + 1) * TS], p_hi[:, k, TP:T].bitcast(f32), SUB) \
                            .then_inc(sm.p_lo_made, 1)
                dve.wait_ge(sm.gate_made, 12 * (hf + 1) + 2)
                for g in range(12):
                    product_ready(u + 4, 0, g + 1)
                    tt(tm[g % 2][:, :], pg[g % 3][:, 0:TH], gate[:, g // 3, cols(g % 3)], MUL).then_inc(sm.evacuated, 1)
                    dve.wait_ge(sm.evacuated, twelfths(u + 4, 0, g + 1))
                    x_t = xres[:, 4 * hf + g // 3, cols(g % 3)]
                    tt(x_t, x_t, tm[g % 2][:, :], ADD).then_inc(sm.x_made, 1)
                unit_done(u + 4, 0)
            dve.wait_ge(sm.rt_root, 2)
            nc.vector.reciprocal(r_tok[:, :], r_tok[:, :]).then_inc(sm.rt_ready, 1)
            dve.wait_ge(sm.rt_ready, 1)
            for t in range(NTT + 1):
                n = tokens(t)
                dve.wait_ge(sm.y_turned, t + 1)
                if t >= 3:
                    dve.wait_ge(y_sent[t % 3], 16 * (t // 3))
                ts_(y_tok[t % 3][0:n, 512:D], bk[2 * (t % 2) + 1][0:n, :], r_tok[0:n, t:t + 1], None, MUL) \
                    .then_inc(sm.y_dve, 1)

        @block.gpsimd
        def _(pool):
            tt, copy = nc.gpsimd.tensor_tensor, nc.gpsimd.tensor_copy

            def load(dst, src):
                pool.dma_start(dst, src, allow_slow_non_contiguous=True).then_inc(sm.params_in, 16)

            nc.gpsimd.memset(ident[:, :], 0.0).then_inc(sm.made, 1)
            nc.gpsimd.memset(ones[:, :], 1.0).then_inc(sm.consts_made, 1)
            nc.gpsimd.memset(eps[:, :], EPS).then_inc(sm.consts_made, 1)
            pool.wait_ge(sm.made, 1)
            nc.gpsimd.affine_select(out=ident[:, :], in_=ident[:, :], compare_op=ALU.not_equal, fill=1.0,
                                    base=0, pattern=[[-1, P]], channel_multiplier=1).then_inc(sm.consts_made, 1)
            pool.dma_start(n_mix[:, :], norm_mix[0].rearrange("(k p) -> p k", p=P), allow_slow_non_contiguous=True) \
                .then_inc(sm.gain_in, 16)
            nc.gpsimd.memset(r_tok[:, :], 1.0).then_inc(sm.r_tok_set, 1)
            nc.gpsimd.memset(token[:, 13:14], 0.0).then_inc(sm.r_tok_set, 1)
            free = [(sm.silu_made, 2), (sm.conv_step, 8), (sm.y_made, 3), (sm.last_kept, 1),
                    (sm.qg_made, 1), (sm.ssq_added, 2), (sm.u_lo_made, 2), (sm.usq_made, 2), (sm.gate_made, 2),
                    (sm.o_made, 1)]
            for i, (s, v) in enumerate(free):
                nc.gpsimd.memset(token[:, i:i + 1], 0.0).then_inc(s, v)
            for t in range(NTT + 1):
                n = tokens(t)
                i = 2 * t + 1
                pool.wait_ge(sm.xhi_made, i + 1)
                tt(act_lo[:, 4:8, t * P:t * P + n], Tb[i % 4][:, :, 0:n],
                   act_hi[:, 4:8, t * P:t * P + n].bitcast(f32), SUB).then_inc(sm.xlo_odd, 1)
                if t == 0:
                    for w in range(CW):
                        load(cq_w[:, :, w], w_cq[0, w].rearrange("(j p) -> p j", p=P))
                    for w in range(SW):
                        load(cs_w[:, :, w], w_cs[0, w].rearrange("(j p) -> p j", p=P))
                    for dst, src in ((n_mlp, norm_mlp), (n_ple, norm_ple)):
                        load(dst[:, :], src[0].rearrange("(k p) -> p k", p=P))
                    load(n_fin[:, :], norm_f.rearrange("(k p) -> p k", p=P))
                    load(gnw[:, :], w_gn.rearrange("a p -> p a"))
                    load(alog[:, :], a_log.to_broadcast([P, H]))
                    load(dtb[:, :], dt_bias.to_broadcast([P, H]))
            for buf in (par[:, :, :], g_tok[:, :, :], pre[0][:, 0:PAD], pre[1][:, 0:PAD]):
                nc.gpsimd.memset(buf, 0.0).then_inc(sm.buffers_zeroed, 1)
            nc.gpsimd.memset(S[:, :, :], 0.0).then_inc(sm.buffers_zeroed, 1)
            pool.wait_ge(sm.buffers_zeroed, ZEROED)
            for dst in (m_inc[:, :], m_smp[:, :], m_blk[:, :], m_bat[:, :]):
                nc.gpsimd.memset(dst, 1.0).then_inc(sm.made, 1)
            for l in range(LEVELS):
                nc.gpsimd.memset(m_lev[l][:, :], 0.0).then_inc(sm.made, 1)
            pool.wait_ge(sm.made, 5 + LEVELS)
            for l in range(LEVELS):
                v = m_lev[l][:, :].rearrange("p (n r) -> p n r", r=2 << l)[:, :, 1 << l:2 << l]
                nc.gpsimd.memset(v, 1.0).then_inc(sm.made, 1)
            made = [5 + 2 * LEVELS]

            def keep(ap, base, pattern, mult):
                pool.wait_ge(sm.made, made[0])
                nc.gpsimd.affine_select(out=ap, in_=ap, compare_op=ALU.is_ge, fill=0.0, base=base,
                                        pattern=pattern, channel_multiplier=mult).then_inc(sm.made, 1)
                made[0] += 1

            keep(m_inc[:, :], 0, [[1, P]], -1)
            keep(m_smp[:, :], 0, [[1, TS]], -1)
            for m in (m_smp, m_blk):
                v = m[:, :].rearrange("p (n r) -> p n r", r=NT)
                keep(v, 0, [[-NT, NB], [0, NT]], 1)
                keep(v, NT - 1, [[NT, NB], [0, NT]], -1)
            keep(m_bat[:, :], 0, [[-NT, NB]], 1)
            keep(m_bat[:, :], NT - 1, [[NT, NB]], -1)
            for l in range(LEVELS):
                h, nb = 1 << l, P >> (l + 1)
                v = m_lev[l][:, :].rearrange("p (n r) -> p n r", r=2 * h)[:, :, h:2 * h]
                keep(v, 0, [[-2 * h, nb], [0, h]], 1)
                keep(v, h - 1, [[2 * h, nb], [0, h]], -1)
            pool.wait_ge(sm.made, made[0])
            nc.gpsimd.memset(token[:, 15:16], 0.0).then_inc(sm.masks_made, 1)
            nc.gpsimd.memset(token[:, 14:15], 0.0).then_inc(sm.s_updated, 4)
            pool.wait_ge(sm.st_ready, 2)

            def sequences(ap, n):
                return ap.rearrange("p a (b w) -> p (a b) w", w=n)

            with pool.Fori(0, NQ // 2) as i:
                for x in range(2):
                    j = ds(2 * i + x, 1)
                    pool.wait_ge(sm.conv_step, at(4 * x + 4, i, 8))
                    pool.wait_ge(sm.buffers_zeroed, ZEROED)
                    copy(samples(pre[x])[:, :, 0:PAD], sequences(st_T[:, j, :], PAD)).then_inc(sm.state_put, 1)
                    if x == 1:
                        for xx in range(2):
                            jj = ds(2 * i + xx, 1)
                            pool.wait_ge(sm.evacuated, twelfths(U_QKV + xx, i, 12))
                            pool.wait_ge(sm.buffers_zeroed, ZEROED)
                            copy(st_O[:, jj, 0:PAD].rearrange("p a w -> p (a w)"), pre[xx][:, TP:TP + PAD]) \
                                .then_inc(sm.state_saved, 1)
                            copy(sequences(st_O[:, jj, PAD:PAD * (NB + 1)], PAD), samples(pre[xx])[:, :, NT:SEG]) \
                                .then_inc(sm.state_saved, 1)

            pool.wait_ge(sm.conv_step, 8 + 4 * NQ)

            def third(t, j):
                m, n = divmod(t, 3)
                b, p = U_B + m, 2 * j
                if t == 2:
                    pool.wait_ge(sm.evacuated, twelfths(b, p, 12))
                    pool.wait_ge(sm.buffers_zeroed, ZEROED)
                    pool.dma_start(z_dram[ds(j, 1)].rearrange("a p t -> p (a t)"), cv[0][:, 0:T]) \
                        .then_inc(sm.z_spilled, 16)
                if t == 3:
                    copy(samples(pre[1])[:, :, 1:PAD], sequences(sc_T[:, ds(j, 1), :], 2)).then_inc(sm.sc_put, 1)
                if m == 2:
                    pool.wait_ge(sm.evacuated, twelfths(b, p, 4 * n + 4))
                    a = n * TH
                    e = min(a + TH, TP)
                    last = tt(pre[1][:, PAD + a:PAD + e], pre[1][:, PAD + a:PAD + e], cv[1][:, a:e], MUL)
                    if n == 2:
                        now = samples(pre[1])[:, :, PAD:SEG]
                        last.then_inc(sm.h_scaled, 1)
                        last = tt(now, now, cv[1][:, TP:T].rearrange("p (b t) -> p b t", t=NT), MUL)
                    last.then_inc(sm.ch_made, 1)
                    if n == 2:
                        pool.wait_ge(sm.ch_made, 3 * j + 3)
                        pool.wait_ge(sm.h_scaled, j + 1)
                        pool.wait_ge(sm.buffers_zeroed, ZEROED)
                        copy(sc_O[:, ds(j, 1), 0:2].rearrange("p a w -> p (a w)"), pre[1][:, TP + 1:TP + PAD]) \
                            .then_inc(sm.state_saved, 1)
                        copy(sequences(sc_O[:, ds(j, 1), 2:2 * (NB + 1)], 2), samples(pre[1])[:, :, NT + 1:SEG]) \
                            .then_inc(sm.state_saved, 1)
                if m == 3:
                    pool.wait_ge(sm.evacuated, twelfths(b, p, 4 * n + 4))
                    pool.wait_ge(sm.sc_step, 3 * j + 3)
                    a = n * TH
                    e = min(a + TH, TP)
                    last = tt(cv[1][:, a:e], cv[1][:, a:e], cv[0][:, a:e], MUL)
                    if n == 2:
                        now = cv[1][:, TP:T].rearrange("p (b t) -> p b t", t=NT)
                        last = tt(now, now, sample_cv(cv[0]), MUL)
                    last.then_inc(sm.y_made, 1)
                    if n == 2:
                        pool.wait_ge(sm.buffers_zeroed, ZEROED)
                        pool.wait_ge(sm.y_made, 3 * j + 6)
                        pool.dma_start(y_dram[ds(j * P, P), :], cv[1][:, 0:T]) \
                            .then_inc(sm.y_spilled, 16)

            def all_heads(m):
                return m[:, None, :].to_broadcast([P, H, P])

            with pool.Fori(0, NSC) as j:
                for step in STEPS:
                    x = int(step[-1]) if step[0] not in "yz" else int(step[1])
                    c1 = 2 * j + x + 1
                    c = ds(2 * j + x, 1)

                    def level(l):
                        tt(Tb[2 + x][:, :, :], AT[x][:, :, :], all_heads(m_lev[l]), MUL).then_inc(sm.lt_made, 1)

                    if step.startswith("prep_norm"):
                        pool.wait_ge(sm.decay_made, c1)
                        tt(Tb[2][:, :, :], Tb[2][:, :, :], all_heads(m_inc), MUL).then_inc(sm.masked, 1)
                        pool.wait_ge(sm.buffers_zeroed, ZEROED)
                        pool.wait_ge(sm.eg_made, c1)
                        copy(egl[x][:, :], Tb[3][:, :, P - 1:P].rearrange("p h a -> p (h a)")).then_inc(sm.last_kept, 1)
                        pool.wait_ge(sm.buffers_zeroed, ZEROED)
                        pool.wait_ge(sm.masked, c1)
                        copy(ktl[x][:, :], Tb[2][:, :, P - 1:P].rearrange("p h a -> p (h a)")).then_inc(sm.last_kept, 1)
                        tt(AT[x][:, :, :], Tb[2][:, :, :], spread(beta[:, c, :].rearrange("p a h -> p (a h)"), P), MUL) \
                            .then_inc(sm.at_scaled, 1)
                        pool.wait_ge(sm.qk_made, at(2 * x + 1, j, 4))
                        tt(qg[x][:, :, :], Tb[4][:, :, :], Tb[3][:, :, :], MUL).then_inc(sm.qg_made, 1)
                    elif step.startswith("prep_kk"):
                        pool.wait_ge(sm.at_made, c1)
                        tt(XT[x][:, :, :], AT[x][:, :, :], all_heads(m_lev[0]), MUL).then_inc(sm.xt_made, 1)
                        pool.wait_ge(sm.xt_made, at(2 * x + 1, j, 4))
                        tt(XT[x][:, :, :], all_heads(ident), XT[x][:, :, :], SUB).then_inc(sm.xt_made, 1)
                    elif step.startswith("prep_x"):
                        level(1)
                    elif step[0] == "y" and int(step[3:]) < LEVELS - 1:
                        l = int(step[3:])
                        pool.wait_ge(sm.y_mm, at(2 * (l - 1) + x + 1, j, 12))
                        level(l + 1)
                    for t in thirds_after(step):
                        third(t, j)
                pool.wait_ge(sm.y_spilled, 16 * j + 16)

            F2, AT0, XT0 = flat(Tb[2]), flat(AT[0]), flat(XT[0])

            def small(ap):
                return hsmall(ap[0:TS, 0:SMALL])

            def small_mask(m):
                return m[0:TS, None, 0:TS].to_broadcast([TS, H, TS])

            pool.wait_ge(sm.q_act, 8)
            tt(small(F2), small(F2), small_mask(m_smp), MUL).then_inc(sm.q_pool, 1)
            pool.wait_ge(sm.q_pool, 1)
            tt(small(AT0), small(F2), spread(beta[0:TS, NTT, :], TS), MUL).then_inc(sm.q_pool, 1)
            pool.wait_ge(sm.q_dve, 5)
            tt(small(F2), small(AT0), small_mask(m_lev[1]), MUL).then_inc(sm.q_pool, 1)
            tt(small(XT0), small(AT0), small_mask(m_lev[0]), MUL).then_inc(sm.q_pool, 1)
            pool.wait_ge(sm.q_pool, 4)
            tt(small(XT0), small_mask(ident), small(XT0), SUB).then_inc(sm.q_pool, 1)
            pool.wait_ge(sm.q_dve, 10)
            for i in range(2 * H):
                if i >= 2:
                    pool.wait_ge(sm.q_pe, 8 + i)
                tt((AT, X)[i % 2][0][0:TS, :, :],
                   F2[0:TS, None, i // 2 * P:(i // 2 + 1) * P].to_broadcast([TS, 4, P]),
                   spread(m_bat[:, 4 * (i % 2):4 * (i % 2) + 4], P), MUL).then_inc(sm.q_pool, 1)

            def zero_sums():
                nc.gpsimd.memset(ssq[:, :], 0.0).then_inc(sm.ssq_zeroed, 1)

            def add_squares(g, base, i=0, step=0):
                n = g % 3
                pool.wait_ge(sm.sq_made, at(base + g + 1, i, step))
                tt(ssq[:, cols(n)], ssq[:, cols(n)], sq[g % 2][:, :], ADD).then_inc(sm.ssq_added, 1)

            pool.wait_ge(sm.mix_hi, 1)
            zero_sums()
            pool.wait_ge(sm.ssq_zeroed, 1)
            with pool.Fori(0, KD // 2) as i:
                for g in range(6):
                    add_squares(g, 0, i, 6)
            for r in range(1, 3):
                pool.wait_ge(sm.rms_mm, r)
                zero_sums()
                pool.wait_ge(sm.ssq_zeroed, r + 1)
                with pool.Fori(0, KD // 2) as i:
                    for g in range(6):
                        add_squares(g, r * 3 * KD, i, 6)


def kernel(**inputs):
    import numpy as np
    import concourse.bacc as bacc
    from concourse.bass_utils import run_bass_kernel_spmd as run

    nc = bacc.Bacc("TRN2", target_bir_lowering=False, num_devices=1)
    names = ["x_prompt", "x_sample", "state_gdn_conv", "state_gdn", "state_sc_conv", "p_prompt", "p_sample",
             "norm_mix", "w_in", "w_conv_qkv", "a_log", "dt_bias", "w_gdn_norm", "w_conv_sc", "w_out",
             "norm_mlp", "w_up", "w_down", "norm_ple", "w_ple_gate", "w_ple_proj", "norm_f"]
    outs = [(1, TP, D), (NB, NT, D), (1, 1, PAD, QKV), (1, 1, H, P, P), (1, 1, SW - 1, SCW),
            (1, NB, PAD, QKV), (1, NB, H, P, P), (1, NB, SW - 1, SCW)]
    arrays, args = {}, []
    for name in names:
        a = np.ascontiguousarray(inputs[name])
        if name in ("w_in", "w_out", "w_up", "w_down", "w_ple_gate", "w_ple_proj"):
            a = a.reshape(a.shape[1:])
        arrays[f"in_{name}"] = a
        args.append(nc.dram_tensor(f"in_{name}", a.shape, mybir.dt.float32, kind="ExternalInput").ap())
    for i, shape in enumerate(outs):
        args.append(nc.dram_tensor(f"out_{i}", shape, mybir.dt.float32, kind="ExternalOutput").ap())
    trunk(nc, *args)
    r = run(nc, [arrays], core_ids=[0])
    return tuple(r.results[0][f"out_{i}"] for i in range(len(outs)))
```

```python
import concourse.bass as bass
from concourse import mybir
from contextlib import ExitStack

P = 128
D = 1024
KD = D // P
TP = 1024
NB = 8
NT = 4
TS = NB * NT
T = TP + TS
TH = T // 3
NTT = TP // P
H = 4
GW = H * P
QKV = 3 * GW
NQ = QKV // P
SCW = D - GW
NSC = SCW // P
CW = 4
SW = 3
PAD = CW - 1
SEG = PAD + NT
PRE = PAD + TP + NB * SEG
CV = PRE - PAD
FF = 4 * D
FC = 4
NFC = FF // P // FC
PLE = 256
KP = PLE // P
EPS = 1e-6
OFF_A = QKV
OFF_Z = OFF_A + 2 * H
OFF_SB = OFF_Z + GW
OFF_SC = OFF_SB + SCW
OFF_SH = OFF_SC + SCW
QSCALE = float(P) ** -0.5
LEVELS = 7
NPAR = NTT + 1

STEPS = (["begin0", "prep_norm0", "prep_kk0", "prep_norm1", "prep_kk1", "prep_x0", "prep_x1"]
         + [f"{w}{x}_{l}" for l in range(1, LEVELS) for w, x in (("y", 0), ("y", 1), ("z", 0), ("z", 1))]
         + [f"{s}{x}" for x in range(2) for s in ("s_in", "s_solve", "s_out", "s_norm")])
BODY_MM = 4 * KD * 9
FILL = {"begin0": 50, "prep_norm0": 38, "prep_norm1": 38, "prep_kk0": 16, "prep_kk1": 21, "prep_x0": 4, "prep_x1": 2,
        "s_in0": 13, "s_in1": 22, "s_solve0": 8, "s_solve1": 8, "s_out0": 8, "s_out1": 8, "s_norm0": 2}
for _s in STEPS:
    if _s[0] in "yz":
        FILL[_s] = 2
FILL["s_norm1"] = BODY_MM - sum(FILL.values())


def fill_range(step):
    at = sum(FILL[s] for s in STEPS[:STEPS.index(step)])
    return at, at + FILL[step]


def thirds_after(step):
    a, b = fill_range(step)
    return [t for t in range(12) if a < 24 * (t + 1) <= b]


class Signals:

    def __init__(self, sem):
        self.params_in = sem("params_in")
        self.gain_in = sem("gain_in")
        self.states_in = sem("states_in")
        self.consts_made = sem("consts_made")
        self.masks_made = sem("masks_made")
        self.buffers_zeroed = sem("buffers_zeroed")
        self.made = sem("made")
        self.r_tok_set = sem("r_tok_set")
        self.x_turned = sem("x_turned")
        self.xw_made = sem("xw_made")
        self.xhi_made = sem("xhi_made")
        self.xlo_even = sem("xlo_even")
        self.xlo_odd = sem("xlo_odd")
        self.x_squared = sem("x_squared")
        self.x_root = sem("x_root")
        self.r_made = sem("r_made")
        self.rdiag_made = sem("rdiag_made")
        self.r_spread = sem("r_spread")
        self.r_ready = sem("r_ready")
        self.st_turned = sem("st_turned")
        self.st_ready = sem("st_ready")
        self.w_hi_made = sem("w_hi_made")
        self.w_lo_made = sem("w_lo_made")
        self.mm_done = sem("mm_done")
        self.evacuated = sem("evacuated")
        self.ab_turned = sem("ab_turned")
        self.ab_copied = sem("ab_copied")
        self.ab_exp = sem("ab_exp")
        self.chain = sem("chain")
        self.g_summed = sem("g_summed")
        self.g_copied = sem("g_copied")
        self.g_exp = sem("g_exp")
        self.state_put = sem("state_put")
        self.conv_step = sem("conv_step")
        self.silu_made = sem("silu_made")
        self.state_saved = sem("state_saved")
        self.z_spilled = sem("z_spilled")
        self.ch_made = sem("ch_made")
        self.sc_step = sem("sc_step")
        self.y_made = sem("y_made")
        self.y_spilled = sem("y_spilled")
        self.sc_put = sem("sc_put")
        self.h_scaled = sem("h_scaled")
        self.norms_summed = sem("norms_summed")
        self.kk_made = sem("kk_made")
        self.xt_turned = sem("xt_turned")
        self.y_mm = sem("y_mm")
        self.z_mm = sem("z_mm")
        self.in_mm = sem("in_mm")
        self.solve_mm = sem("solve_mm")
        self.out_mm = sem("out_mm")
        self.onorm_mm = sem("onorm_mm")
        self.squared = sem("squared")
        self.rsq_made = sem("rsq_made")
        self.eg_made = sem("eg_made")
        self.decay_made = sem("decay_made")
        self.x_copied = sem("x_copied")
        self.ycopy_made = sem("ycopy_made")
        self.v_staged = sem("v_staged")
        self.vtok_made = sem("vtok_made")
        self.o_squared = sem("o_squared")
        self.o_rs_made = sem("o_rs_made")
        self.diag_made = sem("diag_made")
        self.diff_made = sem("diff_made")
        self.qk_made = sem("qk_made")
        self.pt_made = sem("pt_made")
        self.at_made = sem("at_made")
        self.x_updated = sem("x_updated")
        self.ktok_made = sem("ktok_made")
        self.r_vec = sem("r_vec")
        self.vnew_made = sem("vnew_made")
        self.s_updated = sem("s_updated")
        self.o_made = sem("o_made")
        self.masked = sem("masked")
        self.at_scaled = sem("at_scaled")
        self.qg_made = sem("qg_made")
        self.lt_made = sem("lt_made")
        self.xt_made = sem("xt_made")
        self.last_kept = sem("last_kept")
        self.sin_loaded = sem("sin_loaded")
        self.q_pe = sem("q_pe")
        self.q_act = sem("q_act")
        self.q_dve = sem("q_dve")
        self.q_pool = sem("q_pool")
        self.so_turned = sem("so_turned")
        self.so_copied = sem("so_copied")
        self.s_out_made = sem("s_out_made")
        self.states_out = sem("states_out")
        self.sample_states_out = sem("sample_states_out")
        self.yt_loaded = sem("yt_loaded")
        self.zt_loaded = sem("zt_loaded")
        self.zs_loaded = sem("zs_loaded")
        self.mix_y_hi = sem("mix_y_hi")
        self.mix_y_lo = sem("mix_y_lo")
        self.z_silu = sem("z_silu")
        self.gated = sem("gated")
        self.mix_hi = sem("mix_hi")
        self.mix_lo = sem("mix_lo")
        self.xcol_turned = sem("xcol_turned")
        self.xcol_turned3 = sem("xcol_turned3")
        self.xr_copied = sem("xr_copied")
        self.x_made = sem("x_made")
        self.sq_made = sem("sq_made")
        self.ssq_added = sem("ssq_added")
        self.ssq_zeroed = sem("ssq_zeroed")
        self.rms_mm = sem("rms_mm")
        self.rms_log = sem("rms_log")
        self.rms_ready = sem("rms_ready")
        self.split_hi = sem("split_hi")
        self.split_lo = sem("split_lo")
        self.usq_made = sem("usq_made")
        self.u_hi_made = sem("u_hi_made")
        self.u_lo_made = sem("u_lo_made")
        self.p_loaded = sem("p_loaded")
        self.p_turned = sem("p_turned")
        self.p_hi_made = sem("p_hi_made")
        self.p_lo_made = sem("p_lo_made")
        self.gate_made = sem("gate_made")
        self.x_scaled = sem("x_scaled")
        self.rt_mm = sem("rt_mm")
        self.rt_root = sem("rt_root")
        self.rt_ready = sem("rt_ready")
        self.y_turned = sem("y_turned")
        self.y_act = sem("y_act")
        self.y_dve = sem("y_dve")


def trunk(nc, x_p, x_s, st_qkv, st_gdn, st_sc, p_p, p_s, norm_mix, w_in, w_cq, a_log, dt_bias, w_gn, w_cs,
          w_out, norm_mlp, w_up, w_down, norm_ple, w_gate, w_proj, norm_f,
          y_p, y_s, oc_p, os_p, osc_p, oc_s, os_s, osc_s):
    f32, f32r = mybir.dt.float32, mybir.dt.float32r
    ALU, ACT = mybir.AluOpType, mybir.ActivationFunctionType
    MUL, ADD, SUB, MAX, MIN = ALU.mult, ALU.add, ALU.subtract, ALU.max, ALU.min
    ds = bass.ds

    z_dram = nc.dram_tensor("z_spill", (H, P, T), f32, kind="Internal").ap()
    y_dram = nc.dram_tensor("ysc_spill", (NSC * P, T), f32, kind="Internal").ap()

    win_v = w_in.rearrange("(k p) n -> p k n", p=P)
    wout_v = w_out.rearrange("(k p) n -> p k n", p=P)
    wup_v = w_up.rearrange("(k p) n -> p k n", p=P)
    wdn_v = w_down.rearrange("(k p) n -> p k n", p=P)
    wg_v = w_gate.rearrange("(k p) n -> p k n", p=P)
    wp_v = w_proj.rearrange("(k p) n -> p k n", p=P)

    ctx = ExitStack()
    with ctx:
        def sb(name, shape, dt=f32, scope=ctx):
            return scope.enter_context(nc.sbuf_tensor(name, shape, dt))

        def sem(name):
            return ctx.enter_context(nc.semaphore(name))

        act_hi = sb("act_hi", [P, KD, T], f32r)
        act_lo = sb("act_lo", [P, KD, T], f32r)
        w_raw = [sb(f"w_raw{i}", [P, KD, P]) for i in range(2)]
        w_hi = [sb(f"w_hi{i}", [P, KD, P], f32r) for i in range(2)]
        w_lo = [sb(f"w_lo{i}", [P, KD, P], f32r) for i in range(2)]
        ident = sb("ident", [P, P])
        ones = sb("ones", [P, P])
        r_b = sb("r_b", [P, T])
        n_mix = sb("n_mix", [P, KD])
        n_mlp = sb("n_mlp", [P, KD])
        n_ple = sb("n_ple", [P, KD])
        n_fin = sb("n_fin", [P, KD])
        eps = sb("eps", [P, 1])
        gnw = sb("gnw", [P, 1])
        r_tok = sb("r_tok", [P, NPAR])
        token = sb("token", [P, 20])

        mixer = ExitStack()
        stage_x = ExitStack()
        x_tok = [sb(f"x_tok{t}", [P, D], scope=stage_x) for t in range(NTT + 1)]
        x_sqr = sb("x_sqr", [P, D], scope=stage_x)
        st_in = sb("st_in", [3 * NB, QKV], scope=stage_x)
        sc_in = sb("sc_in", [2 * NB, SCW], scope=stage_x)
        stage_x.close()
        qkv = sb("qkv", [P, NQ, T], scope=mixer)
        m_inc = sb("m_inc", [P, P], scope=mixer)
        m_lev = [sb(f"m_lev{l}", [P, P], scope=mixer) for l in range(LEVELS)]
        m_smp = sb("m_smp", [TS, TS], scope=mixer)
        m_blk = sb("m_blk", [TS, TS], scope=mixer)
        st_T = sb("st_T", [P, NQ, PAD * NB], scope=mixer)
        sc_T = sb("sc_T", [P, NSC, 2 * NB], scope=mixer)
        st_O = sb("st_O", [P, NQ, PAD * (NB + 1)], scope=mixer)
        sc_O = sb("sc_O", [P, NSC, 2 * (NB + 1)], scope=mixer)
        cq_w = sb("cq_w", [P, NQ, CW], scope=mixer)
        cs_w = sb("cs_w", [P, NSC, SW], scope=mixer)
        par = sb("par", [P, NPAR, 2 * H], scope=mixer)
        alog = sb("alog", [P, H], scope=mixer)
        dtb = sb("dtb", [P, H], scope=mixer)
        log_a = sb("log_a", [P, NPAR, H], scope=mixer)
        beta = sb("beta", [P, NPAR, H], scope=mixer)
        g_tok = sb("g_tok", [P, NPAR, H], scope=mixer)
        eneg = sb("eneg", [P, NPAR, H], scope=mixer)
        kf = sb("kf", [TS, H], scope=mixer)
        t_a = sb("t_a", [P, NPAR, H], scope=mixer)
        t_b = sb("t_b", [P, NPAR, H], scope=mixer)
        t_c = sb("t_c", [P, NPAR, H], scope=mixer)
        egl = [sb(f"egl{x}", [P, H], scope=mixer) for x in range(2)]
        ktl = [sb(f"ktl{x}", [P, H], scope=mixer) for x in range(2)]
        S = sb("S", [P, H, P], scope=mixer)
        Tb = [sb(f"Tb{i}", [P, H, P], scope=mixer) for i in range(5)]
        kn = [sb(f"kn{x}", [P, H, P], scope=mixer) for x in range(2)]
        AT = [sb(f"AT{x}", [P, H, P], scope=mixer) for x in range(2)]
        PT = [sb(f"PT{x}", [P, H, P], scope=mixer) for x in range(2)]
        qg = [sb(f"qg{x}", [P, H, P], scope=mixer) for x in range(2)]
        X = [sb(f"X{x}", [P, H, P], scope=mixer) for x in range(2)]
        XT = [sb(f"XT{x}", [P, H, P], scope=mixer) for x in range(2)]
        m_bat = sb("m_bat", [TS, NB], scope=mixer)
        conv = ExitStack()
        pre = [sb(f"pre{i}", [P, PRE], scope=conv) for i in range(2)]
        cv = [sb(f"cv{i}", [P, PRE], scope=conv) for i in range(2)]
        conv.close()
        S_in = sb("S_in", [P, H, NB, P], scope=mixer)
        mixer.close()

        tail = ExitStack()
        u_hi = [sb(f"u_hi{i}", [P, FC, T], f32r, scope=tail) for i in range(2)]
        u_lo = [sb(f"u_lo{i}", [P, FC, T], f32r, scope=tail) for i in range(2)]
        xres = sb("xres", [P, KD, T], scope=tail)
        ssq = sb("ssq", [P, T], scope=tail)
        tm = [sb(f"tm{i}", [P, TH], scope=tail) for i in range(2)]
        sq = [sb(f"sq{i}", [P, TH], scope=tail) for i in range(2)]
        tail.close()
        late = ExitStack()
        qkv_room = sb("qkv_room", [P, NQ, T], scope=late)
        x_col = [sb(f"x_col{i}", [P, NTT + 1, P], scope=late) for i in range(2)]
        late.close()
        ple = ExitStack()
        p_hi = sb("p_hi", [P, KP, T], f32r, scope=ple)
        p_lo = sb("p_lo", [P, KP, T], f32r, scope=ple)
        p_tok = [sb(f"p_tok{t}", [P, PLE], scope=ple) for t in range(NTT + 1)]
        gate = sb("gate", [P, H, T], scope=ple)
        y_tok = [sb(f"y_tok{i}", [P, D], scope=ple) for i in range(3)]
        ple.close()

        pg = [ctx.enter_context(nc.psum_tensor(f"pg{i}", [P, 512], f32)) for i in range(3)]
        bk = [ctx.enter_context(nc.psum_tensor(f"bk{i}", [P, 512], f32)) for i in range(5)]

        x_loaded = [sem(f"x_loaded{t}") for t in range(NTT + 1)]
        raw_in = [sem(f"raw_in{i}") for i in range(2)]
        xcol_in = [sem(f"xcol_in{i}") for i in range(2)]
        y_sent = [sem(f"y_sent{i}") for i in range(3)]
        sm = Signals(sem)

        def at(base, p=0, step=1):
            return base if isinstance(p, int) and p == 0 else p * step + base

        def twelfths(b, p, q):
            return at(12 * b + q, p, 24)

        def cols(n):
            return slice(n * TH, (n + 1) * TH)

        def tokens(t):
            return P if t < NTT else TS

        def heads(ap):
            return ap.rearrange("p (h t) -> p h t", h=H)

        def spread(ap, n):
            return ap[:, :, None].to_broadcast([ap.shape[0], ap.shape[1], n])

        def samples(ap):
            return ap[:, PAD + TP:PRE].rearrange("p (b s) -> p b s", s=SEG)

        def sample_cv(ap):
            return samples(ap)[:, :, 0:NT]

        def flat(ap):
            return ap[:, :, :].rearrange("p h t -> p (h t)")

        SMALL = H * TS

        def hsmall(ap):
            return ap.rearrange("p (h t) -> p h t", h=H)

        U_QKV, U_B, U_OUT = 1, 1 + NQ, 1 + NQ + 16
        U_MLP = U_OUT + KD
        U_PLE = U_MLP + 8 * NFC
        N_UNITS = U_PLE + 10

        def up_unit(c):
            return U_MLP if c == 0 else U_MLP + 4 + 8 * (c - 1)

        def down_unit(c):
            return U_MLP + 8 * (c + 1) if c < NFC - 1 else U_MLP + 8 * NFC - 4

        MLP_ORDER = [("up", 0)]
        for _c in range(NFC):
            if _c + 1 < NFC:
                MLP_ORDER.append(("up", _c + 1))
            MLP_ORDER.append(("down", _c))
        LAST_TILES = (range(0, 2), range(2, 5), range(5, NTT + 1))

        def last_product(hf, g):
            return (g // 3, g % 3) if hf == 0 else (g % 4, g // 4)

        WIDE = 2 * P
        CHAIN_ABS, CHAIN_LOG_A, CHAIN_G = 3, 20, 23
        PARAMS = 16 * (6 + CW + SW)
        ZEROED = 5
        STATES_OUT = 16 * (1 + 6 + 2)
        MASKS = 1

        block = ctx.enter_context(nc.Block())

        @block.sync
        def _(sp):
            def load_w(b, p, src, kt):
                if b >= 2 or not isinstance(p, int):
                    sp.wait_ge(sm.w_lo_made, at(b - 1, p, 2))
                dst = w_raw[b % 2][:, :, :].rearrange("p (k d) m -> p k (d m)", k=kt)
                sp.dma_start(dst, src).then_inc(raw_in[b % 2], 16)

            for t in range(NTT + 1):
                src = x_p[0, t * P:(t + 1) * P, :] if t < NTT else x_s.rearrange("b t d -> (b t) d")
                sp.dma_start(x_tok[t][0:tokens(t), :], src).then_inc(x_loaded[t], 16)
                if t == 0:
                    sp.dma_start(n_mix[:, :], norm_mix[0].rearrange("(k p) -> p k", p=P),
                                 allow_slow_non_contiguous=True).then_inc(sm.gain_in, 16)
                if t == 1:
                    load_w(0, 0, win_v[:, :, OFF_A:OFF_A + P], KD)
            sp.dma_start(st_in[:, :], st_qkv[0].rearrange("b w f -> (b w) f")).then_inc(sm.states_in, 16)
            sp.dma_start(sc_in[:, :], st_sc[0].rearrange("b w f -> (b w) f")).then_inc(sm.states_in, 16)
            load_w(U_QKV, 0, win_v[:, :, 0:P], KD)

            def load(dst, src):
                sp.dma_start(dst, src, allow_slow_non_contiguous=True).then_inc(sm.params_in, 16)

            load(alog[:, :], a_log.to_broadcast([P, H]))
            load(dtb[:, :], dt_bias.to_broadcast([P, H]))
            for w in range(CW):
                load(cq_w[:, :, w], w_cq[0, w].rearrange("(j p) -> p j", p=P))
            load_w(U_QKV + 1, 0, win_v[:, :, P:2 * P], KD)
            for w in range(SW):
                load(cs_w[:, :, w], w_cs[0, w].rearrange("(j p) -> p j", p=P))
            for dst, src in ((n_mlp, norm_mlp), (n_ple, norm_ple)):
                load(dst[:, :], src[0].rearrange("(k p) -> p k", p=P))
            load(n_fin[:, :], norm_f.rearrange("(k p) -> p k", p=P))
            load(gnw[:, :], w_gn.rearrange("a p -> p a"))
            with sp.Fori(1, NQ // 2) as i:
                for x in range(2):
                    load_w(U_QKV + x, i, win_v[:, :, ds(i * WIDE + x * P, P)], KD)
            with sp.Fori(0, NSC) as j:
                for m, off in enumerate((OFF_Z, OFF_SC, OFF_SH, OFF_SB)):
                    load_w(U_B + m, 2 * j, win_v[:, :, ds(j * P + off, P)], KD)
            early, rest = slice(0, TP - 2 * P), slice(TP - 2 * P, TP)
            sp.wait_ge(sm.o_made, NTT - 1)
            sp.wait_ge(sm.z_spilled, 16 * NSC)
            for i in range(H):
                sp.dma_start(qkv[:, 2 * H + i, early], z_dram[i, :, early]).then_inc(sm.zt_loaded, 16)
            sp.wait_ge(sm.y_spilled, 16 * (NSC - 1))
            for i in range(NSC - 1):
                sp.dma_start(qkv[:, H + i, early], y_dram[i * P:(i + 1) * P, early]).then_inc(sm.yt_loaded, 16)
            for x in range(2):
                load_w(U_OUT + x, 0, wout_v[:, :, x * P:(x + 1) * P], KD)
            sp.wait_ge(sm.y_spilled, 16 * NSC)
            sp.wait_ge(sm.z_spilled, 16 * NSC)
            for h in range(H):
                sp.dma_start(S_in[:, h, :, :], st_gdn[0, :, h, :, :].rearrange("b d e -> d b e")) \
                    .then_inc(sm.sin_loaded, 16)
            sp.wait_ge(sm.o_made, NTT + 1)
            sp.dma_start(XT[1][:, :, 0:TS], z_dram[:, :, TP:T].rearrange("h p t -> p h t")).then_inc(sm.zs_loaded, 16)
            sp.dma_start(XT[1][:, :, TS:2 * TS], y_dram[:, TP:T].rearrange("(h p) t -> p h t", p=P)) \
                .then_inc(sm.zs_loaded, 16)
            for i in range(NSC):
                part = rest if i < NSC - 1 else slice(0, TP)
                sp.dma_start(qkv[:, H + i, part], y_dram[i * P:(i + 1) * P, part]).then_inc(sm.yt_loaded, 16)
            for i in range(H):
                sp.dma_start(qkv[:, 2 * H + i, rest], z_dram[i, :, rest]).then_inc(sm.zt_loaded, 16)
            sp.wait_ge(sm.s_updated, 4 * (NTT + 1))
            sp.dma_start(os_p[0, 0].rearrange("h d e -> d h e"), S[:, :, :]).then_inc(sm.states_out, 16)
            sp.wait_ge(sm.so_copied, 4)
            for i, buf in enumerate((kn[1], AT[1], PT[1])):
                f = slice(i * GW, (i + 1) * GW)
                flat = buf[:, :, :].rearrange("p h t -> p (h t)")
                sp.dma_start(oc_p[0, 0, :, f], flat[0:PAD, :]).then_inc(sm.states_out, 16)
                sp.dma_start(oc_s[0, :, :, f].rearrange("b w f -> (b w) f"),
                             flat[PAD:PAD * (NB + 1), :]).then_inc(sm.states_out, 16)
            flat = qg[1][:, :, :].rearrange("p h t -> p (h t)")
            sp.dma_start(osc_p[0, 0], flat[0:2, :]).then_inc(sm.states_out, 16)
            sp.dma_start(osc_s[0].rearrange("b w f -> (b w) f"), flat[2:2 * (NB + 1), :]) \
                .then_inc(sm.states_out, 16)
            sp.wait_ge(sm.o_made, NTT + 2)

            def load_xcol(x, i):
                f = ds(i * WIDE + x * P, P)
                sp.dma_start(x_col[x][:, 0:NTT, :], x_p[0].rearrange("(t p) d -> p t d", p=P)[:, :, f]) \
                    .then_inc(xcol_in[x], 16)
                sp.dma_start(x_col[x][0:TS, NTT, :], x_s.rearrange("b t d -> (b t) d")[:, f]) \
                    .then_inc(xcol_in[x], 16)

            for x in range(2):
                f = slice(x * P, (x + 1) * P)
                sp.dma_start(x_col[x][:, 0:NTT, :], x_p[0].rearrange("(t p) d -> p t d", p=P)[:, :, f]) \
                    .then_inc(xcol_in[x], 16)
                sp.dma_start(x_col[x][0:TS, NTT, :], x_s.rearrange("b t d -> (b t) d")[:, f]) \
                    .then_inc(xcol_in[x], 16)
            for h in range(H):
                sp.wait_ge(sm.s_out_made, 2 * (h + 1))
                sp.dma_start(os_s[0, :, h, :, :].rearrange("b d e -> d b e"), S_in[:, h, :, :]) \
                    .then_inc(sm.sample_states_out, 16)
            sp.wait_ge(sm.sample_states_out, 16 * H)
            with sp.Fori(1, KD // 2) as i:
                for x in range(2):
                    load_w(U_OUT + x, i, wout_v[:, :, ds(i * WIDE + x * P, P)], KD)
                    sp.wait_ge(sm.xcol_turned, at(x - 1, i, 2))
                    load_xcol(x, i)
            for kind, c in MLP_ORDER:
                if kind == "up":
                    with sp.Fori(0, FC // 2) as i:
                        for x in range(2):
                            load_w(up_unit(c) + x, i, wup_v[:, :, ds(i * WIDE + (c * FC + x) * P, P)], KD)
                else:
                    with sp.Fori(0, 2) as i:
                        for x in range(2):
                            load_w(down_unit(c) + x, i,
                                   wdn_v[:, c * FC:(c + 1) * FC, ds(i * 2 * WIDE + x * WIDE, WIDE)], FC)
            for hf in range(2):
                with sp.Fori(0, 2) as i:
                    for x in range(2):
                        load_w(U_PLE + 5 * hf + x, i,
                               wg_v[:, :, ds(i * WIDE + (4 * hf + x) * P, P)], KD)
                load_w(U_PLE + 5 * hf + 4, 0, wp_v[:, :, hf * 4 * P:(hf + 1) * 4 * P], KP)
                if hf == 0:
                    sp.wait_ge(sm.mm_done, 12 * U_PLE)
                    for t in range(NTT + 1):
                        src = p_p[0, 0, t * P:(t + 1) * P, :] if t < NTT else p_s[0].rearrange("b t d -> (b t) d")
                        sp.dma_start(p_tok[t][0:tokens(t), :], src).then_inc(sm.p_loaded, 16)
            for t in range(NTT + 1):
                sp.wait_ge(sm.y_act, t + 1)
                sp.wait_ge(sm.y_dve, t + 1)
                dst = y_p[0, t * P:(t + 1) * P, :] if t < NTT else y_s.rearrange("b t d -> (b t) d")
                sp.dma_start(dst, y_tok[t % 3][0:tokens(t), :]).then_inc(y_sent[t % 3], 16)
            for i in range(3):
                sp.wait_ge(y_sent[i], 16 * 3)

        @block.tensor
        def _(pe):
            mm, turn = nc.tensor.matmul, nc.tensor.transpose

            def group(b, p, q, s, bank, terms):
                if 12 * b + q - 2 * s > 0:
                    pe.wait_ge(sm.evacuated, twelfths(b, p, q - 2 * s))
                for i, (w, a) in enumerate(terms):
                    last = mm(pg[bank][:, 0:TH], w, a, start=i == 0, stop=i == len(terms) - 1)
                last.then_inc(sm.mm_done, s)

            def panel_ready(b, p):
                pe.wait_ge(sm.w_lo_made, at(b + 1, p, 2))

            def parts(slot, kt, d, hi, lo, n):
                wh = w_hi[slot][:, :, :].rearrange("p (k d) m -> p k d m", k=kt)
                wl = w_lo[slot][:, :, :].rearrange("p (k d) m -> p k d m", k=kt)
                out = []
                for k in range(kt):
                    out += [(wh[:, k, d, :], hi[:, k, cols(n)]), (wh[:, k, d, :], lo[:, k, cols(n)]),
                            (wl[:, k, d, :], hi[:, k, cols(n)])]
                return out

            def unit(b, p, kt, hi, lo, ready=None, banks_out=None, then=None):
                panel_ready(b, p)
                per = KD // kt
                for d in range(per):
                    for n in range(3):
                        if ready is not None and d == 0:
                            pe.wait_ge(*ready(n))
                        if banks_out is not None and d == 0:
                            pe.wait_ge(sm.evacuated, banks_out[n])
                        s = 4 // per
                        group(b, p, (3 * d + n) * s, s, n, parts(b % 2, kt, d, hi, lo, n))
                        if then is not None and d == 0 and n == 1:
                            then()

            pe.wait_ge(sm.consts_made, 3)
            for t in range(NTT + 1):
                n = tokens(t)
                pe.wait_ge(x_loaded[t], 16)
                for hf in range(2):
                    i = 2 * t + hf
                    if i >= 4:
                        pe.wait_ge(sm.xw_made, i - 3)
                    for k in range(4):
                        f = slice((4 * hf + k) * P, (4 * hf + k + 1) * P)
                        last = turn(bk[i % 4][:, k * P:k * P + n], x_tok[t][0:n, f], ident[0:n, 0:n])
                    last.then_inc(sm.x_turned, 1)
                if t in (4, 7):
                    whole = 3 if t == 4 else 6
                    pe.wait_ge(sm.xlo_even, whole)
                    pe.wait_ge(sm.xlo_odd, whole)
                    panel_ready(0, 0)
                    g = (t - 4) // 3
                    group(0, 0, 4 * g, 4, g, parts(0, KD, 0, act_hi, act_lo, g))
            pe.wait_ge(sm.states_in, 32)
            for j in range(NQ):
                turn(bk[4][:, j * 24:(j + 1) * 24], st_in[:, j * P:(j + 1) * P], ident[0:24, 0:24])
            for j in range(NSC):
                last = turn(bk[4][:, 288 + j * 16:288 + (j + 1) * 16], sc_in[:, j * P:(j + 1) * P],
                            ident[0:16, 0:16])
            last.then_inc(sm.st_turned, 1)
            pe.wait_ge(sm.xlo_even, NTT + 1)
            pe.wait_ge(sm.xlo_odd, NTT + 1)
            group(0, 0, 8, 4, 2, parts(0, KD, 0, act_hi, act_lo, 2))
            pe.wait_ge(sm.rdiag_made, 3)
            pe.wait_ge(sm.xw_made, 2 * (NTT + 1))
            mm(bk[0][:, :], ones[:, :], Tb[0][:, :, :], start=True, stop=True)
            mm(bk[1][:, :], ones[:, :], Tb[1][:, :, :], start=True, stop=True)
            mm(bk[2][:, 0:TS], ones[0:TS, :], Tb[2][0:TS, 0, 0:TS], start=True, stop=True) \
                .then_inc(sm.r_spread, 1)
            pe.wait_ge(sm.evacuated, 12)
            pe.wait_ge(sm.r_ready, 3)
            for t in range(NTT + 1):
                last = turn(bk[0][0:tokens(t), t * 8:(t + 1) * 8], cv[0][0:8, t * P:t * P + tokens(t)],
                            ident[0:8, 0:8])
            last.then_inc(sm.ab_turned, 1)
            with pe.Fori(0, NQ // 2) as i:
                for x in range(2):
                    unit(U_QKV + x, i, KD, act_hi, act_lo)
            pe.wait_ge(sm.chain, CHAIN_LOG_A)
            pe.wait_ge(sm.masks_made, MASKS)
            mm(bk[0][:, 0:32], m_inc[:, :], log_a[:, 0:NTT, :], start=True, stop=True)
            mm(bk[0][0:TS, 32:36], m_smp[:, :], log_a[0:TS, NTT, :], start=True, stop=True)
            mm(bk[0][0:TS, 36:40], m_blk[:, :], log_a[0:TS, NTT, :], start=True, stop=True) \
                .then_inc(sm.g_summed, 1)

            with pe.Fori(0, NSC) as j:
                def fill(step):
                    a, b = fill_range(step)
                    for i in range(a, b):
                        m, r = divmod(i, KD * 9)
                        n, r = divmod(r, KD * 3)
                        if r == 0:
                            if n == 0:
                                panel_ready(U_B + m, 2 * j)
                            pe.wait_ge(sm.evacuated, twelfths(U_B + m, 2 * j, 4 * n - 8))
                        k, r = divmod(r, 3)
                        slot = (U_B + m) % 2
                        w = (w_hi, w_hi, w_lo)[r][slot][:, k, :]
                        last = mm(pg[n][:, 0:TH], w, (act_hi, act_lo, act_hi)[r][:, k, cols(n)],
                                  start=k == 0 and r == 0, stop=k == KD - 1 and r == 2)
                        if k == KD - 1 and r == 2:
                            last.then_inc(sm.mm_done, 4)

                def per_head(f):
                    for h in range(H):
                        last = f(h, slice(h * P, (h + 1) * P))
                    return last

                fill("begin0")
                for x in range(2):
                    c1 = 2 * j + x + 1
                    pe.wait_ge(sm.squared, 2 * c1)
                    if x == 0:
                        pe.wait_ge(sm.o_made, 2 * j + 1)
                    else:
                        pe.wait_ge(sm.at_made, 2 * j + 1)
                    mm(bk[0][:, :], ones[:, :], Tb[0][:, :, :], start=True, stop=True)
                    mm(bk[1][:, :], ones[:, :], Tb[1][:, :, :], start=True, stop=True)
                    pe.wait_ge(sm.diag_made, c1)
                    mm(bk[2][:, :], ones[:, :], X[x][:, :, :], start=True, stop=True) \
                        .then_inc(sm.norms_summed, 1)
                    fill(f"prep_norm{x}")
                    pe.wait_ge(sm.qk_made, 2 * c1)
                    per_head(lambda h, s: mm(bk[0][:, s], kn[x][:, h, :], kn[x][:, h, :], start=True, stop=True))
                    per_head(lambda h, s: mm(bk[1][:, s], kn[x][:, h, :], Tb[4][:, h, :], start=True, stop=True)) \
                        .then_inc(sm.kk_made, 1)
                    fill(f"prep_kk{x}")
                for x in range(2):
                    pe.wait_ge(sm.xt_made, 4 * j + 2 * x + 2)
                    per_head(lambda h, s: turn(bk[3 + x][:, s], XT[x][:, h, :], ident[:, :])) \
                        .then_inc(sm.xt_turned, 1)
                    fill(f"prep_x{x}")
                for l in range(1, LEVELS):
                    for x in range(2):
                        n1 = at(2 * (l - 1) + x + 1, j, 12)
                        pe.wait_ge(sm.lt_made, n1)
                        pe.wait_ge(sm.x_copied if l == 1 else sm.x_updated,
                                   at(x + 1, j, 2) if l == 1 else at(4 * (l - 2) + 2 * x + 2, j, 22))
                        per_head(lambda h, s: mm(bk[x][:, s], Tb[2 + x][:, h, :], X[x][:, h, :],
                                                 start=True, stop=True)).then_inc(sm.y_mm, 1)
                        fill(f"y{x}_{l}")
                    for x in range(2):
                        zb, ztb = (bk[2], bk[3]) if x == 0 else (bk[4], bk[1])
                        pe.wait_ge(sm.ycopy_made, at(2 * (l - 1) + x + 1, j, 12))
                        if l < LEVELS - 1:
                            per_head(lambda h, s: mm(zb[:, s], XT[x][:, h, :], Tb[x][:, h, :],
                                                     start=True, stop=True))
                        per_head(lambda h, s: mm(ztb[:, s], Tb[x][:, h, :], XT[x][:, h, :],
                                                 start=True, stop=True)).then_inc(sm.z_mm, 1)
                        fill(f"z{x}_{l}")
                for x in range(2):
                    c1 = 2 * j + x + 1
                    pe.wait_ge(sm.v_staged, c1)
                    pe.wait_ge(sm.x_updated, at(21 + x, j, 22))
                    pe.wait_ge(sm.s_updated, at(4 * x + 4, j, 8))
                    per_head(lambda h, s: turn(bk[4][:, s], kn[x][:, h, :], ident[:, :]))
                    per_head(lambda h, s: turn(bk[3][:, s], X[x][:, h, :], ident[:, :]))
                    per_head(lambda h, s: mm(bk[2][:, s], kn[x][:, h, :], S[:, h, :], start=True, stop=True)) \
                        .then_inc(sm.in_mm, 1)
                    fill(f"s_in{x}")
                    pe.wait_ge(sm.r_vec, 4 * c1)
                    if x == 1:
                        pe.wait_ge(sm.o_rs_made, 4 * j + 1)
                    per_head(lambda h, s: mm(bk[0][:, s], XT[x][:, h, :], Tb[0][:, h, :], start=True, stop=True)) \
                        .then_inc(sm.solve_mm, 1)
                    fill(f"s_solve{x}")
                    pe.wait_ge(sm.qg_made, 2 * j + x + 2)
                    pe.wait_ge(sm.vnew_made, c1)
                    pe.wait_ge(sm.ktok_made, c1)
                    pe.wait_ge(sm.o_made, 2 * j + x + 1)

                    def out_head(h, s):
                        mm(bk[1][:, s], S[:, h, :], qg[x][:, h, :], start=True, stop=False)
                        return mm(bk[1][:, s], Tb[1][:, h, :], PT[x][:, h, :], start=False, stop=True)

                    per_head(out_head)
                    per_head(lambda h, s: mm(bk[3][:, s], Tb[2][:, h, :], Tb[1][:, h, :], start=True, stop=True)) \
                        .then_inc(sm.out_mm, 1)
                    fill(f"s_out{x}")
                    pe.wait_ge(sm.o_squared, c1)
                    mm(bk[0][:, :], ones[:, :], Tb[4][:, :, :], start=True, stop=True).then_inc(sm.onorm_mm, 1)
                    fill(f"s_norm{x}")

            small = slice(0, H * TS)

            def hs(h):
                return slice(h * TS, (h + 1) * TS)

            T4 = [b[:, :, :].rearrange("p h t -> p (h t)") for b in Tb]
            knf, ATf, PTf, XTf, Xf = [b[0][:, :, :].rearrange("p h t -> p (h t)") for b in (kn, AT, PT, XT, X)]
            pe.wait_ge(sm.q_act, 2)
            pe.wait_ge(sm.q_dve, 1)
            pe.wait_ge(sm.o_made, NTT + 1)
            mm(bk[0][:, small], ones[:, :], T4[0][:, small], start=True, stop=True)
            mm(bk[1][:, small], ones[:, :], T4[1][:, small], start=True, stop=True)
            mm(bk[2][:, small], ones[0:TS, :], Xf[0:TS, small], start=True, stop=True).then_inc(sm.q_pe, 1)
            pe.wait_ge(sm.q_dve, 3)
            pe.wait_ge(sm.q_act, 6)
            for h in range(H):
                mm(bk[0][0:TS, hs(h)], knf[:, hs(h)], knf[:, hs(h)], start=True, stop=True)
            for h in range(H):
                mm(bk[1][0:TS, hs(h)], knf[:, hs(h)], T4[4][:, hs(h)], start=True, stop=True)
            for h in range(H):
                last = turn(bk[3][0:TS, h * P:(h + 1) * P], knf[:, hs(h)], ident[:, :])
            last.then_inc(sm.q_pe, 1)
            pe.wait_ge(sm.q_pool, 5)
            for h in range(H):
                last = turn(bk[0][0:TS, 256 + h * TS:256 + (h + 1) * TS], XTf[0:TS, hs(h)], ident[0:TS, 0:TS])
            last.then_inc(sm.q_pe, 1)
            pe.wait_ge(sm.q_dve, 7)
            pe.wait_ge(sm.sin_loaded, 16 * H)
            def against_state(h):
                for b in range(NB):
                    c = (h * NB + b) * 8
                    last = mm(bk[4][:, c:c + 8], S_in[:, h, b, :], T4[0][:, c:c + 8], start=True, stop=True)
                return last

            against_state(0)
            pe.wait_ge(sm.q_act, 9)
            for h in range(H):
                last = mm(bk[1][0:TS, 256 + h * TS:256 + (h + 1) * TS], T4[2][0:TS, hs(h)], Xf[0:TS, hs(h)],
                          start=True, stop=True)
            last.then_inc(sm.q_pe, 1)
            against_state(1)
            pe.wait_ge(sm.q_act, 10)
            for h in range(H):
                last = mm(bk[2][0:TS, hs(h)], T4[3][0:TS, hs(h)], XTf[0:TS, hs(h)], start=True, stop=True)
            last.then_inc(sm.q_pe, 1)
            against_state(2)
            against_state(3).then_inc(sm.q_pe, 1)
            pe.wait_ge(sm.q_dve, 8)
            for h in range(H):
                last = turn(bk[0][0:TS, h * P:(h + 1) * P], T4[1][:, hs(h)], ident[:, :])
            last.then_inc(sm.q_pe, 1)

            pe.wait_ge(sm.mix_lo, H)
            pe.wait_ge(sm.mix_y_lo, NSC)
            panel_ready(U_OUT, 0)
            group(U_OUT, 0, 0, 4, 0, parts(U_OUT % 2, KD, 0, act_hi, act_lo, 0))
            pe.wait_ge(sm.q_dve, 9)
            pe.wait_ge(sm.q_act, 11)
            for h in range(H):
                last = mm(bk[2][0:TS, h * P:(h + 1) * P], XTf[0:TS, hs(h)], T4[3][0:TS, h * P:(h + 1) * P],
                          start=True, stop=True)
            last.then_inc(sm.q_pe, 1)
            pe.wait_ge(sm.q_dve, 10)
            for h in range(H):
                last = mm(bk[1][:, hs(h)], T4[2][0:TS, h * P:(h + 1) * P], PTf[0:TS, hs(h)], start=True, stop=True)
            last.then_inc(sm.q_pe, 1)
            group(U_OUT, 0, 4, 4, 1, parts(U_OUT % 2, KD, 0, act_hi, act_lo, 1))
            pe.wait_ge(sm.q_act, 12)
            mm(bk[0][:, small], ones[:, :], T4[4][:, small], start=True, stop=True).then_inc(sm.onorm_mm, 1)
            def state_product(i):
                pe.wait_ge(sm.q_pool, 6 + i)
                if i >= 4:
                    pe.wait_ge(sm.s_out_made, i - 3)
                mm(bk[i % 4][:, :], T4[0][0:TS, i // 2 * P:(i // 2 + 1) * P], by_seq[i % 4][0:TS, :, :],
                   start=True, stop=True).then_inc(sm.q_pe, 1)

            by_seq = (AT[0], X[0], X[1], Tb[3])
            pe.wait_ge(sm.q_dve, 11)
            pe.wait_ge(sm.q_act, 13)
            for i in range(3):
                state_product(i)
            for i in range(NQ):
                if i % 4 == 0 and i > 0:
                    pe.wait_ge(sm.so_copied, i // 4)
                last = turn(bk[3][0:27, (i % 4) * P:(i % 4 + 1) * P], st_O[:, i, :], ident[:, :])
                if i % 4 == 3:
                    last.then_inc(sm.so_turned, 1)
            pe.wait_ge(sm.so_copied, 3)
            for i in range(NSC):
                last = turn(bk[3][0:18, i * P:(i + 1) * P], sc_O[:, i, :], ident[:, :])
            last.then_inc(sm.so_turned, 1)
            pe.wait_ge(sm.mix_lo, H + 1)
            pe.wait_ge(sm.mix_y_lo, NSC + 1)
            group(U_OUT, 0, 8, 4, 2, parts(U_OUT % 2, KD, 0, act_hi, act_lo, 2))
            pe.wait_ge(sm.so_copied, 4)
            for i in range(3, 2 * H):
                state_product(i)
            pieces = [[(0, 0, 128, 0), (1, 0, 128, 128), (2, 0, 96, 256)],
                      [(2, 96, 128, 0), (3, 0, 128, 32), (4, 0, 128, 160), (5, 0, 64, 288)],
                      [(5, 64, 128, 0), (6, 0, 128, 64), (7, 0, 128, 192), (8, 0, 32, 320)]]

            def out_unit(x, i):
                b = U_OUT + x
                panel_ready(b, i)
                for n in range(3):
                    if not isinstance(i, int) or x > 0:
                        group(b, i, 4 * n, 4, n, parts(b % 2, KD, 0, act_hi, act_lo, n))
                    pe.wait_ge(sm.consts_made, 3)
                    pe.wait_ge(xcol_in[x], at(32, i, 32))
                    for t, a, e, c in pieces[n]:
                        last = turn(bk[n][:, c:c + e - a], x_col[x][a:e, t, :], ident[a:e, a:e])
                    last.then_inc(sm.xcol_turned if n == 2 else sm.xcol_turned3, 1)

            pe.wait_ge(sm.s_out_made, 2 * H)
            for x in range(2):
                out_unit(x, 0)
            with pe.Fori(1, KD // 2) as i:
                for x in range(2):
                    out_unit(x, i)

            def sum_squares():
                for n in range(3):
                    last = mm(bk[n][:, 0:TH], ones[:, :], ssq[:, cols(n)], start=True, stop=True)
                last.then_inc(sm.rms_mm, 1)

            def mlp_sums():
                pe.wait_ge(sm.ssq_added, 2 + 3 * KD)
                pe.wait_ge(sm.evacuated, 12 * U_MLP)
                sum_squares()

            def p_turns():
                pe.wait_ge(sm.p_loaded, 16 * (NTT + 1))
                pe.wait_ge(sm.rms_ready, 6)
                for k in range(KP):
                    for t in range(NTT):
                        turn(bk[2 * k + t // 4][:, (t % 4) * P:(t % 4 + 1) * P],
                             p_tok[t][:, k * P:(k + 1) * P], ident[:, :])
                for k in range(KP):
                    last = turn(bk[4][:, k * TS:(k + 1) * TS], p_tok[NTT][0:TS, k * P:(k + 1) * P],
                                ident[0:TS, 0:TS])
                last.then_inc(sm.p_turned, 1)

            def ple_sums():
                pe.wait_ge(sm.ssq_added, 2 + 6 * KD)
                sum_squares()

            for kind, c in MLP_ORDER:
                u = up_unit(c) if kind == "up" else down_unit(c)
                if kind == "up" and c == 0:
                    for i in range(FC // 2):
                        for x in range(2):
                            unit(u + x, i, KD, act_hi, act_lo, lambda n: (sm.split_lo, KD * (n + 1)),
                                 then=mlp_sums if i == x == 0 else None)
                elif kind == "up":
                    pe.wait_ge(sm.evacuated, 12 * u - 2)
                    with pe.Fori(0, FC // 2) as i:
                        for x in range(2):
                            unit(u + x, i, KD, act_hi, act_lo, lambda n: (sm.split_lo, KD * (n + 1)))
                else:
                    with pe.Fori(0, 2) as i:
                        for x in range(2):
                            unit(u + x, i, FC, u_hi[c % 2], u_lo[c % 2],
                                 lambda n: (sm.u_lo_made, 2 + 3 * FC * (c + 1)))
            for hf in range(2):
                u = U_PLE + 5 * hf
                for i in range(2):
                    for x in range(2):
                        unit(u + x, i, KD, act_hi, act_lo, lambda n: (sm.split_lo, 3 * KD + KD * (n + 1)),
                             banks_out=[12 * u - (2, 1)[hf] * (2 - n) for n in range(3)] if i == x == 0 else None,
                             then={(0, 0, 0): ple_sums, (0, 1, 1): p_turns}.get((hf, i, x)))
                if hf == 0:
                    unit(u + 4, 0, KP, p_hi, p_lo, lambda n: (sm.p_lo_made, 6))

            def last_norm(third):
                pe.wait_ge(sm.ssq_added, 2 + 6 * KD + 12 + 4 * (third + 1))
                if third > 0:
                    pe.wait_ge(sm.rt_root, third)
                for t in LAST_TILES[third]:
                    n = tokens(t)
                    last = mm(bk[4][0:n, t:t + 1], ssq[:, t * P:t * P + n], ones[:, 0:1], start=True, stop=True)
                last.then_inc(sm.rt_mm, 1)
                pe.wait_ge(sm.x_scaled, 12 + 4 * (third + 1))
                for t in LAST_TILES[third]:
                    n = tokens(t)
                    if t >= 2:
                        pe.wait_ge(sm.y_act, t - 1)
                        pe.wait_ge(sm.y_dve, t - 1)
                    for k in range(KD):
                        last = turn(bk[2 * (t % 2) + k // 4][0:n, (k % 4) * P:(k % 4 + 1) * P],
                                    xres[:, k, t * P:t * P + n], ident[:, :])
                    last.then_inc(sm.y_turned, 1)

            b = U_PLE + 9
            panel_ready(b, 0)
            for g in range(12):
                d, n = last_product(1, g)
                group(b, 0, g, 1, g % 3, parts(b % 2, KP, d, p_hi, p_lo, n))
                if g == 7:
                    last_norm(0)
            last_norm(1)
            last_norm(2)

        @block.scalar
        def _(act):
            def op(out, in_, func, **kw):
                return nc.scalar.activation(out, in_, func, **kw)

            def split_w(b, p):
                if b >= 2:
                    act.wait_ge(sm.mm_done, twelfths(b - 1, p, 0))
                act.wait_ge(raw_in[b % 2], at(16 * (b // 2 + 1), p, 16))
                act.wait_ge(sm.consts_made, 3)
                op(w_hi[b % 2][:, :, :], w_raw[b % 2][:, :, :], ACT.Copy).then_inc(sm.w_hi_made, 1)

            def unit_done(b, p):
                if b + 2 + (2 * p if isinstance(p, int) else 0) < N_UNITS:
                    split_w(b + 2, p)

            act.wait_ge(sm.consts_made, 3)
            for t in range(NTT + 1):
                n = tokens(t)
                for hf in range(2):
                    i = 2 * t + hf
                    act.wait_ge(sm.xw_made, i + 1)
                    op(act_hi[:, 4 * hf:4 * hf + 4, t * P:t * P + n], Tb[i % 4][:, :, 0:n], ACT.Copy) \
                        .then_inc(sm.xhi_made, 1)
                if t == 0:
                    act.wait_ge(sm.r_tok_set, 2)
                else:
                    act.wait_ge(sm.x_squared, t)
                op(x_sqr[0:n, :], x_tok[t][0:n, :], ACT.Square, accum_out=r_tok[0:n, t:t + 1]) \
                    .then_inc(sm.x_squared, 1)
                if t == 2:
                    split_w(0, 0)
            act.wait_ge(sm.x_squared, NTT + 1)
            op(r_tok[:, :], r_tok[:, :], ACT.Sqrt, scale=1.0 / D, bias=eps[:, 0:1]).then_inc(sm.x_root, 1)
            split_w(1, 0)
            act.wait_ge(sm.st_turned, 1)
            op(st_T[:, :, :], bk[4][:, 0:288].rearrange("p (j b) -> p j b", j=NQ), ACT.Copy).then_inc(sm.st_ready, 1)
            op(sc_T[:, :, :], bk[4][:, 288:352].rearrange("p (j b) -> p j b", j=NSC), ACT.Copy) \
                .then_inc(sm.st_ready, 1)
            act.wait_ge(sm.r_spread, 1)
            op(r_b[:, 0:512], bk[0][:, :], ACT.Copy).then_inc(sm.r_ready, 1)
            op(r_b[:, 512:TP], bk[1][:, :], ACT.Copy).then_inc(sm.r_ready, 1)
            op(r_b[:, TP:T], bk[2][:, 0:TS], ACT.Copy).then_inc(sm.r_ready, 1)
            unit_done(0, 0)
            act.wait_ge(sm.ab_turned, 1)
            act.wait_ge(sm.buffers_zeroed, ZEROED)
            op(par[:, 0:NTT, :], bk[0][:, 0:64].rearrange("p (t c) -> p t c", t=NTT), ACT.Copy) \
                .then_inc(sm.ab_copied, 1)
            op(par[0:TS, NTT, :], bk[0][0:TS, 64:72], ACT.Copy).then_inc(sm.ab_copied, 1)
            act.wait_ge(sm.ab_copied, 2)
            act.wait_ge(sm.params_in, PARAMS)
            op(beta[:, :, :], par[:, :, H:2 * H], ACT.Exp, scale=-1.0).then_inc(sm.ab_exp, 1)
            op(alog[:, :], alog[:, :], ACT.Exp).then_inc(sm.ab_exp, 1)
            act.wait_ge(sm.chain, CHAIN_ABS)
            op(t_b[:, :, :], t_b[:, :, :], ACT.Exp, scale=-1.0).then_inc(sm.ab_exp, 1)
            with act.Fori(0, NQ // 2) as i:
                for x in range(2):
                    b = U_QKV + x
                    unit_done(b, i)
                    act.wait_ge(sm.conv_step, at(12 + 4 * x, i, 8))
                    act.wait_ge(sm.consts_made, 3)
                    j = ds(2 * i + x, 1)
                    op(qkv[:, j, 0:TP].rearrange("p a t -> p (a t)"), cv[x][:, 0:TP], ACT.Silu)
                    op(qkv[:, j, TP:T].rearrange("p a (b t) -> p (a b) t", t=NT), sample_cv(cv[x]), ACT.Silu) \
                        .then_inc(sm.silu_made, 1)
            act.wait_ge(sm.g_summed, 1)
            op(g_tok[:, 0:NTT, :], bk[0][:, 0:32].rearrange("p (t h) -> p t h", h=H), ACT.Copy).then_inc(sm.g_copied, 1)
            op(g_tok[0:TS, NTT, :], bk[0][0:TS, 32:36], ACT.Copy).then_inc(sm.g_copied, 1)
            act.wait_ge(sm.g_copied, 2)
            op(eneg[:, :, :], g_tok[:, :, :], ACT.Exp).then_inc(sm.g_exp, 1)
            act.wait_ge(sm.chain, CHAIN_G)
            op(kf[:, :], kf[:, :], ACT.Exp).then_inc(sm.g_exp, 1)

            with act.Fori(0, NSC) as j:
                def chunk_cols(x):
                    return ds(j * 2 * P + x * P, P)

                def squares(x):
                    op(Tb[0][:, :, :], qkv[:, 0:H, chunk_cols(x)], ACT.Square).then_inc(sm.squared, 1)
                    op(Tb[1][:, :, :], qkv[:, H:2 * H, chunk_cols(x)], ACT.Square).then_inc(sm.squared, 1)

                def norm_root(x):
                    act.wait_ge(sm.o_rs_made, at(2 * x + 1, j, 4))
                    act.wait_ge(sm.consts_made, 3)
                    op(Tb[4][:, :, :], Tb[4][:, :, :], ACT.Exp, scale=-0.5).then_inc(sm.o_rs_made, 1)

                squares(0)
                for step in STEPS:
                    x = int(step[-1]) if step[0] not in "yz" else int(step[1])
                    c1 = 2 * j + x + 1
                    if step.startswith("prep_norm"):
                        act.wait_ge(sm.norms_summed, c1)
                        act.wait_ge(sm.consts_made, 3)
                        op(Tb[0][:, :, :], heads(bk[0]), ACT.Ln, bias=eps[:, 0:1]).then_inc(sm.rsq_made, 1)
                        op(Tb[1][:, :, :], heads(bk[1]), ACT.Ln, bias=eps[:, 0:1]).then_inc(sm.rsq_made, 1)
                        act.wait_ge(sm.qg_made, c1)
                        op(Tb[3][:, :, :], heads(bk[2]), ACT.Exp).then_inc(sm.eg_made, 1)
                        for i in range(2):
                            act.wait_ge(sm.rsq_made, at(4 * x + 1 + i, j, 8))
                            act.wait_ge(sm.consts_made, 3)
                            op(Tb[i][:, :, :], Tb[i][:, :, :], ACT.Exp, scale=-0.5).then_inc(sm.rsq_made, 1)
                        act.wait_ge(sm.diff_made, 4 * c1)
                        op(Tb[2][:, :, :], Tb[2][:, :, :], ACT.Exp).then_inc(sm.decay_made, 1)
                        if x == 0:
                            act.wait_ge(sm.qk_made, 2 * c1)
                            act.wait_ge(sm.consts_made, 3)
                            squares(1)
                    elif step.startswith("prep_x"):
                        act.wait_ge(sm.xt_turned, c1)
                        op(X[x][:, :, :], heads(bk[3 + x]), ACT.Copy).then_inc(sm.x_copied, 1)
                    elif step[0] == "y":
                        l = int(step[3:])
                        act.wait_ge(sm.y_mm, at(2 * (l - 1) + x + 1, j, 12))
                        op(Tb[x][:, :, :], heads(bk[x]), ACT.Copy).then_inc(sm.ycopy_made, 1)
                    elif step == f"z1_{LEVELS - 1}":
                        act.wait_ge(sm.z_mm, at(12, j, 12))
                        act.wait_ge(sm.consts_made, 3)
                        for xx in range(2):
                            op(X[xx][:, :, :], qkv[:, 2 * H:3 * H, chunk_cols(xx)], ACT.Copy).then_inc(sm.v_staged, 1)
                    elif step.startswith("s_in"):
                        act.wait_ge(sm.in_mm, c1)
                        op(Tb[3][:, :, :], heads(bk[3]), ACT.Copy).then_inc(sm.vtok_made, 1)
                        if x == 1:
                            norm_root(0)
                    elif step.startswith("s_out"):
                        act.wait_ge(sm.out_mm, c1)
                        act.wait_ge(sm.qg_made, 2 * j + 3)
                        act.wait_ge(sm.o_made, c1)
                        op(Tb[4][:, :, :], heads(bk[1]), ACT.Square).then_inc(sm.o_squared, 1)
                    elif step.startswith("s_norm"):
                        act.wait_ge(sm.onorm_mm, c1)
                        act.wait_ge(sm.consts_made, 3)
                        op(Tb[4][:, :, :], heads(bk[0]), ACT.Ln, scale=1.0 / P, bias=eps[:, 0:1]) \
                            .then_inc(sm.o_rs_made, 1)
                        if x == 1:
                            norm_root(1)
                    for t in thirds_after(step):
                        if t % 3 == 2:
                            unit_done(U_B + t // 3, 2 * j)

            F = [flat(b) for b in Tb]
            sm_q, sm_k = qkv[:, 0:H, TP:T], qkv[:, H:2 * H, TP:T]
            act.wait_ge(sm.o_made, NTT + 1)
            op(hsmall(F[0][:, 0:SMALL]), sm_q, ACT.Square).then_inc(sm.q_act, 1)
            op(hsmall(F[1][:, 0:SMALL]), sm_k, ACT.Square).then_inc(sm.q_act, 1)
            act.wait_ge(sm.q_pe, 1)
            for i in range(2):
                op(F[i][:, 0:SMALL], bk[i][:, 0:SMALL], ACT.Ln, bias=eps[:, 0:1]).then_inc(sm.q_act, 1)
            for i in range(2):
                act.wait_ge(sm.q_act, 3 + i)
                op(F[i][:, 0:SMALL], F[i][:, 0:SMALL], ACT.Exp, scale=-0.5).then_inc(sm.q_act, 1)
            op(flat(qg[0])[:, 0:SMALL], bk[2][:, 0:SMALL], ACT.Exp).then_inc(sm.q_act, 1)
            act.wait_ge(sm.diff_made, 4 * (NTT + 1))
            op(F[2][0:TS, 0:SMALL], F[2][0:TS, 0:SMALL], ACT.Exp).then_inc(sm.q_act, 1)
            act.wait_ge(sm.q_pe, 3)
            op(flat(X[0])[0:TS, 0:SMALL], bk[0][0:TS, 256:256 + SMALL], ACT.Copy).then_inc(sm.q_act, 1)
            act.wait_ge(sm.yt_loaded, 16 * (2 * NSC - 1))
            act.wait_ge(sm.mm_done, 12 * U_OUT)
            for i in range(NSC):
                op(act_hi[:, H + i, 0:TP], qkv[:, H + i, 0:TP], ACT.Copy).then_inc(sm.mix_y_hi, 1)
            act.wait_ge(sm.zs_loaded, 32)
            op(act_hi[:, H:KD, TP:T], XT[1][:, :, TS:2 * TS], ACT.Copy).then_inc(sm.mix_y_hi, 1)
            act.wait_ge(sm.q_pe, 4)
            op(F[3][0:TS, 0:SMALL], bk[1][0:TS, 256:256 + SMALL], ACT.Copy).then_inc(sm.q_act, 1)
            act.wait_ge(sm.zt_loaded, 32 * H)
            for i in range(H):
                op(qkv[:, 2 * H + i, 0:TP], qkv[:, 2 * H + i, 0:TP], ACT.Silu).then_inc(sm.z_silu, 1)
            op(XT[1][:, :, 0:TS], XT[1][:, :, 0:TS], ACT.Silu).then_inc(sm.z_silu, 1)
            for i in range(H):
                act.wait_ge(sm.gated, i + 1)
                op(act_hi[:, i, 0:TP], qkv[:, i, 0:TP], ACT.Copy).then_inc(sm.mix_hi, 1)
            act.wait_ge(sm.q_pe, 7)
            op(F[3][0:TS, :], bk[0][0:TS, :], ACT.Copy).then_inc(sm.q_act, 1)
            act.wait_ge(sm.q_dve, 12)
            op(F[4][:, 0:SMALL], F[1][:, 0:SMALL], ACT.Square).then_inc(sm.q_act, 1)
            act.wait_ge(sm.onorm_mm, NTT + 1)
            op(F[4][:, 0:SMALL], bk[0][:, 0:SMALL], ACT.Ln, scale=1.0 / P, bias=eps[:, 0:1]).then_inc(sm.q_act, 1)
            act.wait_ge(sm.q_act, 13)
            op(F[4][:, 0:SMALL], F[4][:, 0:SMALL], ACT.Exp, scale=-0.5).then_inc(sm.q_act, 1)
            act.wait_ge(sm.gated, H + 1)
            op(act_hi[:, 0:H, TP:T], qkv[:, 0:H, TP:T], ACT.Copy).then_inc(sm.mix_hi, 1)
            for i, buf in enumerate((kn[1], AT[1], PT[1], qg[1])):
                n = 27 if i < 3 else 18
                act.wait_ge(sm.so_turned, i + 1)
                op(flat(buf)[0:n, :], bk[3][0:n, :], ACT.Copy).then_inc(sm.so_copied, 1)

            def rms(scale_count):
                act.wait_ge(sm.rms_mm, scale_count)
                for n in range(3):
                    op(r_b[:, cols(n)], bk[n][:, 0:TH], ACT.Ln, scale=1.0 / D, bias=eps[:, 0:1]) \
                        .then_inc(sm.rms_log, 1)
                for n in range(3):
                    act.wait_ge(sm.rms_log, 3 * scale_count)
                    op(r_b[:, cols(n)], r_b[:, cols(n)], ACT.Exp, scale=-0.5).then_inc(sm.rms_ready, 1)

            def split_x(gain, n):
                for k in range(KD):
                    op(act_hi[:, k, cols(n)], xres[:, k, cols(n)], ACT.Copy, scale=gain[:, k:k + 1]) \
                        .then_inc(sm.split_hi, 1)

            act.wait_ge(sm.states_out, STATES_OUT)
            act.wait_ge(sm.s_out_made, 2 * H)
            x_flat = xres[:, :, :].rearrange("p k t -> p (k t)")
            def out_pair(i):
                last = isinstance(i, int)
                for x in range(2):
                    b = U_OUT + x
                    def residual(n):
                        act.wait_ge(sm.xcol_turned if n == 2 else sm.xcol_turned3,
                                    at(x + 1, i, 2) if n == 2 else at(2 * x + n + 1, i, 4))
                        act.wait_ge(sm.consts_made, 3)
                        op(xres[:, ds(2 * i + x, 1), cols(n)].rearrange("p a t -> p (a t)"), bk[n][:, 0:TH],
                           ACT.Copy).then_inc(sm.xr_copied, 1)

                    splits = last and x == 1
                    residual(0)
                    residual(1)
                    if not splits:
                        residual(2)
                    act.wait_ge(sm.sample_states_out, 16 * H)
                    for n in range(3):
                        g = 3 * x + n
                        if n == 2:
                            unit_done(b, i)
                        act.wait_ge(sm.evacuated, twelfths(b, i, 4 * n + 4))
                        act.wait_ge(sm.ssq_added, at(g + 1, i, 6))
                        if x == 0:
                            op(token[:, 16 + n:17 + n], token[:, 13:14], ACT.Copy)
                        op(sq[g % 2][:, :], x_flat[:, ds(i * 2 * T + x * T + n * TH, TH)], ACT.Square) \
                            .then_inc(sm.sq_made, 1)
                        if splits:
                            split_x(n_mlp, n)
                            if n == 0:
                                residual(2)

            with act.Fori(0, KD // 2 - 1) as i:
                out_pair(i)
            out_pair(KD // 2 - 1)
            rms(1)

            ups = 0
            for kind, c in MLP_ORDER:
                u = up_unit(c) if kind == "up" else down_unit(c)
                if kind == "up":
                    with act.Fori(0, FC // 2) as i:
                        for x in range(2):
                            for n in range(3):
                                g = 3 * x + n
                                base = ups + g + 1
                                act.wait_ge(sm.evacuated, twelfths(u + x, i, 4 * n + 4))
                                act.wait_ge(sm.u_lo_made, at(base, i, 6))
                                op(sq[g % 2][:, :], tm[g % 2][:, :], ACT.Square).then_inc(sm.usq_made, 1)
                                act.wait_ge(sm.usq_made, at(2 + base, i, 6))
                                if c >= 2 and n == 0:
                                    act.wait_ge(sm.mm_done, 12 * (down_unit(c - 2) + 4))
                                act.wait_ge(sm.consts_made, 3)
                                op(u_hi[c % 2][:, ds(2 * i + x, 1), cols(n)].rearrange("p a t -> p (a t)"),
                                   sq[g % 2][:, :], ACT.Copy).then_inc(sm.u_hi_made, 1)
                            unit_done(u + x, i)
                    ups += 3 * FC
                elif c < NFC - 1:
                    with act.Fori(0, 2) as i:
                        for x in range(2):
                            unit_done(u + x, i)
                else:
                    for i in range(2):
                        for x in range(2):
                            for g in range(6):
                                act.wait_ge(sm.evacuated, twelfths(u + x, i, 2 * g + 2))
                                act.wait_ge(sm.ssq_added, at(3 * KD + 6 * x + g + 1, i, 12))
                                op(sq[g % 2][:, :], xres[:, 4 * i + 2 * x + g // 3, cols(g % 3)], ACT.Square) \
                                    .then_inc(sm.sq_made, 1)
                                if i == x == 1 and g >= 3:
                                    split_x(n_ple, g - 3)
                            unit_done(u + x, i)
            rms(2)

            def last_norm(third):
                tiles = LAST_TILES[third]
                a, e = tiles[0], min(tiles[-1] + 1, NTT)
                act.wait_ge(sm.rt_mm, third + 1)
                op(r_tok[:, a:e], bk[4][:, a:e], ACT.Sqrt, scale=1.0 / D, bias=eps[:, 0:1]).then_inc(sm.rt_root, 1)
                if third == 2:
                    op(r_tok[0:TS, NTT:NPAR], bk[4][0:TS, NTT:NPAR], ACT.Sqrt, scale=1.0 / D, bias=eps[0:TS, 0:1]) \
                        .then_inc(sm.rt_root, 1)
                act.wait_ge(sm.rt_ready, third + 1)
                for t in tiles:
                    n = tokens(t)
                    act.wait_ge(sm.y_turned, t + 1)
                    if t >= 3:
                        act.wait_ge(y_sent[t % 3], 16 * (t // 3))
                    op(y_tok[t % 3][0:n, 0:512], bk[2 * (t % 2)][0:n, :], ACT.Copy, scale=r_tok[0:n, t:t + 1]) \
                        .then_inc(sm.y_act, 1)

            def p_high():
                act.wait_ge(sm.p_turned, 1)
                for k in range(KP):
                    for i in range(2):
                        op(p_hi[:, k, i * 512:(i + 1) * 512], bk[2 * k + i][:, :], ACT.Copy) \
                            .then_inc(sm.p_hi_made, 1)
                for k in range(KP):
                    op(p_hi[:, k, TP:T], bk[4][:, k * TS:(k + 1) * TS], ACT.Copy).then_inc(sm.p_hi_made, 1)

            for hf in range(2):
                u = U_PLE + 5 * hf

                def gates(i):
                    for x in range(2):
                        for n in range(3):
                            act.wait_ge(sm.evacuated, twelfths(u + x, i, 4 * n + 4))
                            act.wait_ge(sm.consts_made, 3)
                            op(gate[:, ds(2 * i + x, 1), cols(n)].rearrange("p a t -> p (a t)"),
                               tm[(3 * x + n) % 2][:, :], ACT.Sigmoid).then_inc(sm.gate_made, 1)
                            if (hf, i, x, n) == (0, 1, 1, 1):
                                p_high()
                        unit_done(u + x, i)

                for i in range(2):
                    gates(i)
                for g in range(12):
                    d, n = last_product(hf, g)
                    k = 4 * hf + d
                    act.wait_ge(sm.x_made, 12 * hf + g + 1)
                    act.wait_ge(sm.ssq_added, 6 * KD + 12 * hf + g + 1)
                    op(sq[g % 2][:, :], xres[:, k, cols(n)], ACT.Square).then_inc(sm.sq_made, 1)
                    act.wait_ge(sm.sq_made, 6 * KD + 12 * hf + g + 1)
                    op(xres[:, k, cols(n)], xres[:, k, cols(n)], ACT.Copy, scale=n_fin[:, k:k + 1]) \
                        .then_inc(sm.x_scaled, 1)
                    if (hf, g) == (1, 9):
                        last_norm(0)
                unit_done(u + 4, 0)
            last_norm(1)
            last_norm(2)

        @block.vector
        def _(dve):
            tt, ts_, stt = nc.vector.tensor_tensor, nc.vector.tensor_scalar, nc.vector.scalar_tensor_tensor

            def split_w(b, p):
                dve.wait_ge(sm.w_hi_made, at(b + 1, p, 2))
                tt(w_lo[b % 2][:, :, :], w_raw[b % 2][:, :, :], w_hi[b % 2][:, :, :].bitcast(f32), SUB) \
                    .then_inc(sm.w_lo_made, 1)

            def unit_done(b, p):
                if b + 2 + (2 * p if isinstance(p, int) else 0) < N_UNITS:
                    split_w(b + 2, p)

            def product_ready(b, p, q):
                dve.wait_ge(sm.mm_done, twelfths(b, p, q))

            steps = [0]

            def link(ins):
                steps[0] += 1
                ins.then_inc(sm.chain, 1)
                dve.wait_ge(sm.chain, steps[0])

            dve.wait_ge(sm.gain_in, 16)
            for t in range(NTT + 1):
                n = tokens(t)
                for hf in range(2):
                    i = 2 * t + hf
                    dve.wait_ge(sm.x_turned, i + 1)
                    if i >= 4:
                        dve.wait_ge(sm.xlo_odd if hf else sm.xlo_even, t - 1)
                    tt(Tb[i % 4][:, :, 0:n], heads(bk[i % 4])[:, :, 0:n], spread(n_mix[:, 4 * hf:4 * hf + 4], n), MUL) \
                        .then_inc(sm.xw_made, 1)
                dve.wait_ge(sm.xhi_made, 2 * t + 1)
                tt(act_lo[:, 0:4, t * P:t * P + n], Tb[2 * t % 4][:, :, 0:n],
                   act_hi[:, 0:4, t * P:t * P + n].bitcast(f32), SUB).then_inc(sm.xlo_even, 1)
                if t == 2:
                    split_w(0, 0)
            dve.wait_ge(sm.x_root, 1)
            nc.vector.reciprocal(r_tok[:, :], r_tok[:, :]).then_inc(sm.r_made, 1)
            dve.wait_ge(sm.r_made, 1)
            dve.wait_ge(sm.xlo_odd, NTT + 1)
            dve.wait_ge(sm.xlo_even, NTT + 1)
            for i in range(2):
                tt(Tb[i][:, :, :], ident[:, None, :].to_broadcast([P, 4, P]), spread(r_tok[:, 4 * i:4 * i + 4], P),
                   MUL).then_inc(sm.rdiag_made, 1)
            ts_(Tb[2][0:TS, 0, 0:TS], ident[0:TS, 0:TS], r_tok[0:TS, NTT:NPAR], None, MUL).then_inc(sm.rdiag_made, 1)
            split_w(1, 0)
            dve.wait_ge(sm.r_ready, 3)
            for n in range(3):
                product_ready(0, 0, 4 * n + 4)
                tt(cv[0][0:8, cols(n)], pg[n][0:8, 0:TH], r_b[0:8, cols(n)], MUL).then_inc(sm.evacuated, 4)
            unit_done(0, 0)
            dve.wait_ge(sm.ab_copied, 2)
            dve.wait_ge(sm.params_in, PARAMS)
            link(tt(t_a[:, :, :], par[:, :, 0:H], dtb[:, None, :].to_broadcast([P, NPAR, H]), ADD))
            link(ts_(t_b[:, :, :], t_a[:, :, :], -1.0, None, MUL))
            link(tt(t_b[:, :, :], t_b[:, :, :], t_a[:, :, :], MAX))
            assert steps[0] == CHAIN_ABS
            dve.wait_ge(sm.ab_exp, 3)
            link(ts_(t_c[:, :, :], t_b[:, :, :], 2.0, None, ADD))
            link(nc.vector.reciprocal(t_c[:, :, :], t_c[:, :, :]))
            link(tt(t_b[:, :, :], t_b[:, :, :], t_c[:, :, :], MUL))
            link(tt(t_c[:, :, :], t_b[:, :, :], t_b[:, :, :], MUL))
            link(ts_(log_a[:, :, :], t_c[:, :, :], 1.0 / 19, None, MUL))
            for d in (17, 15, 13, 11, 9, 7, 5, 3):
                link(stt(log_a[:, :, :], log_a[:, :, :], 1.0 / d, t_c[:, :, :], ADD, MUL))
            link(stt(log_a[:, :, :], log_a[:, :, :], 1.0, t_b[:, :, :], ADD, MUL))
            link(ts_(t_a[:, :, :], t_a[:, :, :], 0.0, None, MAX))
            link(stt(log_a[:, :, :], log_a[:, :, :], 2.0, t_a[:, :, :], MUL, ADD))
            link(stt(log_a[:, :, :], log_a[:, :, :], -1.0, alog[:, None, :].to_broadcast([P, NPAR, H]), MUL, MUL))
            assert steps[0] == CHAIN_LOG_A
            link(ts_(beta[:, :, :], beta[:, :, :], 1.0, None, ADD))
            link(nc.vector.reciprocal(beta[:, :, :], beta[:, :, :]))

            def to_columns(buf, n, b, p, inc):
                a = n * TH
                e = min(a + TH, TP)
                last = tt(buf[:, PAD + a:PAD + e], pg[n][:, 0:e - a], r_b[:, a:e], MUL)
                if n == 2:
                    last = tt(samples(buf)[:, :, PAD:SEG], pg[n][:, e - a:TH].rearrange("p (b t) -> p b t", t=NT),
                              r_b[:, TP:T].rearrange("p (b t) -> p b t", t=NT), MUL)
                last.then_inc(sm.evacuated, inc)

            with dve.Fori(0, NQ // 2) as i:
                for x in range(2):
                    b = U_QKV + x
                    dve.wait_ge(sm.state_put, at(x + 1, i, 2))
                    for n in range(3):
                        product_ready(b, i, 4 * n + 4)
                        to_columns(pre[x], n, b, i, 4)
                    unit_done(b, i)
                    dve.wait_ge(sm.evacuated, twelfths(b, i, 12))
                    dve.wait_ge(sm.silu_made, at(x + 1, i, 2))
                    j = ds(2 * i + x, 1)

                    def tap(w):
                        return cq_w[:, j, w:w + 1].rearrange("p a w -> p (a w)")

                    ts_(cv[x][:, 0:CV], pre[x][:, 0:CV], tap(0), None, MUL).then_inc(sm.conv_step, 1)
                    for w in range(1, CW):
                        dve.wait_ge(sm.conv_step, at(8 + 4 * x + w, i, 8))
                        stt(cv[x][:, 0:CV], pre[x][:, w:w + CV], tap(w), cv[x][:, 0:CV], MUL, ADD) \
                            .then_inc(sm.conv_step, 1)
            dve.wait_ge(sm.g_copied, 2)
            link(tt(kf[:, :], bk[0][0:TS, 36:40], g_tok[0:TS, NTT, :], SUB))
            assert steps[0] == CHAIN_G
            dve.wait_ge(sm.g_exp, 1)
            link(ts_(eneg[:, :, :], eneg[:, :, :], -1.0, None, MUL))
            dve.wait_ge(sm.silu_made, NQ + 2)

            def chunk(ap, c):
                return ap[:, c, :].rearrange("p a h -> p (a h)")

            def third(t, j):
                m, n = divmod(t, 3)
                b, p = U_B + m, 2 * j
                product_ready(b, p, 4 * n + 4)
                if m == 2:
                    if n == 0:
                        dve.wait_ge(sm.sc_put, j + 1)
                    to_columns(pre[1], n, b, p, 4)
                else:
                    if t == 0:
                        dve.wait_ge(sm.y_made, 3 * j + 3)
                    if t == 9:
                        dve.wait_ge(sm.ch_made, 3 * j + 3)
                    tt(cv[0 if m == 0 else 1][:, cols(n)], pg[n][:, 0:TH], r_b[:, cols(n)], MUL) \
                        .then_inc(sm.evacuated, 4)
                if n == 2:
                    unit_done(b, p)
                if t == 9:
                    dve.wait_ge(sm.z_spilled, 16 * j + 16)
                    for w in range(SW):
                        tap = cs_w[:, ds(j, 1), w:w + 1].rearrange("p a w -> p (a w)")
                        src = pre[1][:, w + 1:w + 1 + CV]
                        if w == 0:
                            ts_(cv[0][:, 0:CV], src, tap, None, MUL).then_inc(sm.sc_step, 1)
                        else:
                            dve.wait_ge(sm.sc_step, at(w, j, 3))
                            stt(cv[0][:, 0:CV], src, tap, cv[0][:, 0:CV], MUL, ADD).then_inc(sm.sc_step, 1)

            with dve.Fori(0, NSC) as j:
                def diagonal(x):
                    tt(X[x][:, :, :], ident[:, None, :].to_broadcast([P, H, P]),
                       spread(chunk(g_tok, ds(2 * j + x, 1)), P), MUL).then_inc(sm.diag_made, 1)

                def normed_output(x):
                    dve.wait_ge(sm.o_rs_made, at(2 * x + 2, j, 4))
                    tt(qkv[:, 0:H, ds(j * 2 * P + x * P, P)], heads(bk[1]), Tb[4][:, :, :], MUL) \
                        .then_inc(sm.o_made, 1)

                diagonal(0)
                for step in STEPS:
                    x = int(step[-1]) if step[0] not in "yz" else int(step[1])
                    c1 = 2 * j + x + 1
                    c = ds(2 * j + x, 1)
                    tok = ds(j * 2 * P + x * P, P)
                    if step.startswith("prep_norm"):
                        if x == 0:
                            diagonal(1)
                        dve.wait_ge(sm.norms_summed, c1)
                        dve.wait_ge(sm.last_kept, at(2 * x + 1, j, 4))
                        dve.wait_ge(sm.eg_made, c1)
                        for h in range(H):
                            ts_(Tb[2][:, h, :], bk[2][:, h * P:(h + 1) * P],
                                g_tok[:, c, h:h + 1].rearrange("p a h -> p (a h)"), 0.0, SUB, MIN) \
                                .then_inc(sm.diff_made, 1)
                        dve.wait_ge(sm.rsq_made, 4 * c1)
                        dve.wait_ge(sm.qg_made, c1)
                        for h in range(H):
                            last = stt(Tb[4][:, h, :], qkv[:, h, tok], QSCALE, Tb[0][:, h, :], MUL, MUL)
                        last.then_inc(sm.qk_made, 1)
                        tt(kn[x][:, :, :], qkv[:, H:2 * H, tok], Tb[1][:, :, :], MUL).then_inc(sm.qk_made, 1)
                    elif step.startswith("prep_kk"):
                        dve.wait_ge(sm.kk_made, c1)
                        dve.wait_ge(sm.masked, c1)
                        tt(PT[x][:, :, :], heads(bk[1]), Tb[2][:, :, :], MUL).then_inc(sm.pt_made, 1)
                        dve.wait_ge(sm.at_scaled, c1)
                        tt(AT[x][:, :, :], heads(bk[0]), AT[x][:, :, :], MUL).then_inc(sm.at_made, 1)
                    elif step[0] == "z":
                        l = int(step[3:])
                        dve.wait_ge(sm.z_mm, at(2 * (l - 1) + x + 1, j, 12))
                        zb, ztb = (bk[2], bk[3]) if x == 0 else (bk[4], bk[1])
                        if l == 1:
                            dve.wait_ge(sm.x_copied, c1)
                        if l > 1:
                            dve.wait_ge(sm.x_updated, at(4 * (l - 2) + 2 * x + 2, j, 22))
                        if l < LEVELS - 1:
                            tt(X[x][:, :, :], X[x][:, :, :], heads(zb), SUB).then_inc(sm.x_updated, 1)
                        tt(XT[x][:, :, :], XT[x][:, :, :], heads(ztb), SUB).then_inc(sm.x_updated, 1)
                    elif step.startswith("s_in"):
                        dve.wait_ge(sm.in_mm, c1)
                        tt(Tb[2][:, :, :], heads(bk[4]), spread(ktl[x][:, :], P), MUL).then_inc(sm.ktok_made, 1)
                        dve.wait_ge(sm.vtok_made, c1)
                        for h in range(H):
                            stt(Tb[0][:, h, :], bk[2][:, h * P:(h + 1) * P],
                                eneg[:, c, h:h + 1].rearrange("p a h -> p (a h)"), Tb[3][:, h, :], MUL, ADD) \
                                .then_inc(sm.r_vec, 1)
                        if x == 1:
                            normed_output(0)
                    elif step.startswith("s_solve"):
                        dve.wait_ge(sm.solve_mm, c1)
                        tt(Tb[1][:, :, :], heads(bk[0]), spread(chunk(beta, c), P), MUL).then_inc(sm.vnew_made, 1)
                    elif step.startswith("s_out"):
                        dve.wait_ge(sm.out_mm, c1)
                        for h in range(H):
                            stt(S[:, h, :], S[:, h, :], egl[x][:, h:h + 1], bk[3][:, h * P:(h + 1) * P], MUL, ADD) \
                                .then_inc(sm.s_updated, 1)
                    elif step == "s_norm1":
                        normed_output(1)
                    for t in thirds_after(step):
                        third(t, j)

            F = [flat(b) for b in Tb]
            X0, XT0, AT0, PT0, G0 = [flat(b[0]) for b in (X, XT, AT, PT, qg)]
            sq_, sk_, sv_ = [qkv[:, a * H:(a + 1) * H, TP:T] for a in range(3)]
            tt(hsmall(X0[0:TS, 0:SMALL]), ident[0:TS, None, 0:TS].to_broadcast([TS, H, TS]),
               spread(g_tok[0:TS, NTT, :], TS), MUL).then_inc(sm.q_dve, 1)
            dve.wait_ge(sm.q_pe, 1)
            dve.wait_ge(sm.q_act, 7)
            for h in range(H):
                ts_(F[2][0:TS, h * TS:(h + 1) * TS], bk[2][0:TS, h * TS:(h + 1) * TS], g_tok[0:TS, NTT, h:h + 1],
                    0.0, SUB, MIN).then_inc(sm.diff_made, 1)
            dve.wait_ge(sm.q_act, 6)
            stt(hsmall(F[4][:, 0:SMALL]), sq_, QSCALE, hsmall(F[0][:, 0:SMALL]), MUL, MUL).then_inc(sm.q_dve, 1)
            tt(hsmall(flat(kn[0])[:, 0:SMALL]), sk_, hsmall(F[1][:, 0:SMALL]), MUL).then_inc(sm.q_dve, 1)
            dve.wait_ge(sm.q_pe, 2)
            dve.wait_ge(sm.q_pool, 1)
            tt(PT0[0:TS, 0:SMALL], bk[1][0:TS, 0:SMALL], F[2][0:TS, 0:SMALL], MUL).then_inc(sm.q_dve, 1)
            dve.wait_ge(sm.q_pool, 2)
            tt(AT0[0:TS, 0:SMALL], bk[0][0:TS, 0:SMALL], AT0[0:TS, 0:SMALL], MUL).then_inc(sm.q_dve, 1)
            dve.wait_ge(sm.q_act, 7)
            dve.wait_ge(sm.q_dve, 3)
            kq = F[0][:, 0:2 * SMALL].rearrange("p (h b a t) -> p (h b) a t", b=NB, a=2, t=NT)

            def by_sequence(ap):
                return ap.rearrange("p (hb t) -> p hb t", t=NT)

            for a, src in enumerate((flat(kn[0]), F[4])):
                tt(kq[:, :, a, :], by_sequence(src[:, 0:SMALL]), by_sequence(G0[:, 0:SMALL]), MUL).then_inc(sm.q_dve, 1)
            for i in range(H):
                dve.wait_ge(sm.z_silu, i + 1)
                stt(qkv[:, i, 0:TP], qkv[:, i, 0:TP], gnw[:, 0:1], qkv[:, 2 * H + i, 0:TP], MUL, MUL) \
                    .then_inc(sm.gated, 1)
            for i in range(H):
                dve.wait_ge(sm.mix_hi, i + 1)
                tt(act_lo[:, i, 0:TP], qkv[:, i, 0:TP], act_hi[:, i, 0:TP].bitcast(f32), SUB).then_inc(sm.mix_lo, 1)
            dve.wait_ge(sm.q_pe, 6)
            kqs = bk[4][:, 0:2 * SMALL].rearrange("p (h b a t) -> p h b a t", h=H, a=2, t=NT)
            for h in range(H):
                last = tt(F[1][:, h * TS:(h + 1) * TS].rearrange("p (b t) -> p b t", t=NT),
                          sv_[:, h, :].rearrange("p (b t) -> p b t", t=NT), kqs[:, h, :, 0, :], SUB)
            last.then_inc(sm.q_dve, 1)
            dve.wait_ge(sm.q_pe, 6)
            tt(XT0[0:TS, 0:SMALL], XT0[0:TS, 0:SMALL], bk[2][0:TS, 0:SMALL], SUB).then_inc(sm.q_dve, 1)

            dve.wait_ge(sm.q_pe, 8)
            tt(heads(F[2])[0:TS], heads(bk[2])[0:TS], spread(beta[0:TS, NTT, :], P), MUL).then_inc(sm.q_dve, 1)
            tt(heads(F[0])[0:TS], heads(bk[3])[0:TS], spread(kf[:, :], P), MUL).then_inc(sm.q_dve, 1)
            dve.wait_ge(sm.q_pe, 9)
            link(nc.vector.tensor_copy(F[1][:, 0:SMALL], bk[1][:, 0:SMALL]))
            tt(by_sequence(F[1][:, 0:SMALL]), by_sequence(F[1][:, 0:SMALL]),
               bk[4][:, 0:2 * SMALL].rearrange("p (hb a t) -> p hb a t", a=2, t=NT)[:, :, 1, :], ADD) \
                .then_inc(sm.q_dve, 1)

            gl = G0[:, 0:SMALL].rearrange("p (h b t) -> p h b t", h=H, t=NT)
            for h in range(H):
                tt(S_in[:, h, :, :], S_in[:, h, :, :], gl[:, h, :, NT - 1:NT].to_broadcast([P, NB, P]), MUL) \
                    .then_inc(sm.q_dve, 1)
            dve.wait_ge(sm.q_act, 14)
            tt(qkv[:, 0:H, TP:T], hsmall(F[1][:, 0:SMALL]), hsmall(F[4][:, 0:SMALL]), MUL).then_inc(sm.o_made, 1)

            dve.wait_ge(sm.o_made, NTT + 2)
            dve.wait_ge(sm.z_silu, H + 1)
            stt(qkv[:, 0:H, TP:T], qkv[:, 0:H, TP:T], gnw[:, 0:1], XT[1][:, :, 0:TS], MUL, MUL).then_inc(sm.gated, 1)
            dve.wait_ge(sm.mix_hi, H + 1)
            tt(act_lo[:, 0:H, TP:T], qkv[:, 0:H, TP:T], act_hi[:, 0:H, TP:T].bitcast(f32), SUB).then_inc(sm.mix_lo, 1)
            for i in range(2 * H):
                dve.wait_ge(sm.q_pe, 10 + i)
                dve.wait_ge(sm.q_dve, 13 + i // 2)
                part = S_in[:, i // 2, 4 * (i % 2):4 * (i % 2) + 4, :]
                tt(part, part, heads(bk[i % 4]), ADD).then_inc(sm.s_out_made, 1)

            def split_x(gain, n, count):
                for k in range(KD):
                    dve.wait_ge(sm.split_hi, count + KD * n + k + 1)
                    stt(act_lo[:, k, cols(n)], xres[:, k, cols(n)], gain[:, k:k + 1],
                        act_hi[:, k, cols(n)].bitcast(f32), MUL, SUB).then_inc(sm.split_lo, 1)

            def rows(ap):
                return ap.rearrange("p a t -> p (a t)")

            def out_pair(i):
                for x in range(2):
                    b = U_OUT + x
                    for n in range(3):
                        product_ready(b, i, 4 * n + 4)
                        dve.wait_ge(sm.xr_copied, at(3 * x + n + 1, i, 6))
                        x_t = rows(xres[:, ds(2 * i + x, 1), cols(n)])
                        tt(x_t, x_t, pg[n][:, 0:TH], ADD).then_inc(sm.evacuated, 4)
                        if isinstance(i, int) and x == 1:
                            split_x(n_mlp, n, 0)
                    unit_done(b, i)

            with dve.Fori(0, KD // 2 - 1) as i:
                out_pair(i)
            out_pair(KD // 2 - 1)
            ups = 0
            for kind, c in MLP_ORDER:
                u = up_unit(c) if kind == "up" else down_unit(c)
                if kind == "up":
                    with dve.Fori(0, FC // 2) as i:
                        for x in range(2):
                            for n in range(3):
                                g = 3 * x + n
                                if c == 0:
                                    dve.wait_ge(sm.rms_ready, n + 1)
                                product_ready(u + x, i, 4 * n + 4)
                                dve.wait_ge(sm.usq_made, at(ups + g + 1, i, 6))
                                stt(tm[g % 2][:, :], pg[n][:, 0:TH], 0.0, r_b[:, cols(n)], MAX, MUL) \
                                    .then_inc(sm.evacuated, 4)
                                dve.wait_ge(sm.u_hi_made, at(ups + g + 1, i, 6))
                                k = ds(2 * i + x, 1)
                                tt(rows(u_lo[c % 2][:, k, cols(n)]), sq[g % 2][:, :],
                                   rows(u_hi[c % 2][:, k, cols(n)]).bitcast(f32), SUB).then_inc(sm.u_lo_made, 1)
                            unit_done(u + x, i)
                    ups += 3 * FC
                else:
                    def down_pair(i):
                        for x in range(2):
                            for g in range(6):
                                product_ready(u + x, i, 2 * g + 2)
                                x_t = rows(xres[:, ds(4 * i + 2 * x + g // 3, 1), cols(g % 3)])
                                tt(x_t, x_t, pg[g % 3][:, 0:TH], ADD).then_inc(sm.evacuated, 2)
                                if c == NFC - 1 and i == x == 1 and g >= 3:
                                    split_x(n_ple, g - 3, 3 * KD)
                            unit_done(u + x, i)

                    if c < NFC - 1:
                        with dve.Fori(0, 2) as i:
                            down_pair(i)
                    else:
                        for i in range(2):
                            down_pair(i)
            def last_norm(third):
                tiles = LAST_TILES[third]
                dve.wait_ge(sm.rt_root, (1, 2, 4)[third])
                v = r_tok[:, tiles[0]:tiles[-1] + 1]
                nc.vector.reciprocal(v, v).then_inc(sm.rt_ready, 1)
                dve.wait_ge(sm.rt_ready, third + 1)
                for t in tiles:
                    n = tokens(t)
                    dve.wait_ge(sm.y_turned, t + 1)
                    if t >= 3:
                        dve.wait_ge(y_sent[t % 3], 16 * (t // 3))
                    ts_(y_tok[t % 3][0:n, 512:D], bk[2 * (t % 2) + 1][0:n, :], r_tok[0:n, t:t + 1], None, MUL) \
                        .then_inc(sm.y_dve, 1)

            def p_low():
                for k in range(KP):
                    for i in range(2):
                        dve.wait_ge(sm.p_hi_made, 2 * k + i + 1)
                        tt(p_lo[:, k, i * 512:(i + 1) * 512], bk[2 * k + i][:, :],
                           p_hi[:, k, i * 512:(i + 1) * 512].bitcast(f32), SUB).then_inc(sm.p_lo_made, 1)
                for k in range(KP):
                    dve.wait_ge(sm.p_hi_made, 3 * KP)
                    tt(p_lo[:, k, TP:T], bk[4][:, k * TS:(k + 1) * TS], p_hi[:, k, TP:T].bitcast(f32), SUB) \
                        .then_inc(sm.p_lo_made, 1)

            for hf in range(2):
                u = U_PLE + 5 * hf

                def gates(i):
                    for x in range(2):
                        for n in range(3):
                            g = 3 * x + n
                            if hf == 0:
                                dve.wait_ge(sm.rms_ready, 3 + n + 1)
                            product_ready(u + x, i, 4 * n + 4)
                            dve.wait_ge(sm.gate_made, at(12 * hf + g + 1, i, 6))
                            tt(tm[g % 2][:, :], pg[n][:, 0:TH], r_b[:, cols(n)], MUL).then_inc(sm.evacuated, 4)
                            if (hf, i, x, n) == (0, 1, 1, 1):
                                p_low()
                        unit_done(u + x, i)

                for i in range(2):
                    gates(i)
                dve.wait_ge(sm.gate_made, 12 * (hf + 1) + 2)
                for g in range(12):
                    d, n = last_product(hf, g)
                    product_ready(u + 4, 0, g + 1)
                    tt(tm[g % 2][:, :], pg[g % 3][:, 0:TH], gate[:, d, cols(n)], MUL).then_inc(sm.evacuated, 1)
                    dve.wait_ge(sm.evacuated, twelfths(u + 4, 0, g + 1))
                    x_t = xres[:, 4 * hf + d, cols(n)]
                    tt(x_t, x_t, tm[g % 2][:, :], ADD).then_inc(sm.x_made, 1)
                    if (hf, g) == (1, 9):
                        last_norm(0)
                unit_done(u + 4, 0)
            last_norm(1)
            last_norm(2)

        @block.gpsimd
        def _(pool):
            tt, copy = nc.gpsimd.tensor_tensor, nc.gpsimd.tensor_copy

            nc.gpsimd.memset(ident[:, :], 0.0).then_inc(sm.made, 1)
            nc.gpsimd.memset(ones[:, :], 1.0).then_inc(sm.consts_made, 1)
            nc.gpsimd.memset(eps[:, :], EPS).then_inc(sm.consts_made, 1)
            pool.wait_ge(sm.made, 1)
            nc.gpsimd.affine_select(out=ident[:, :], in_=ident[:, :], compare_op=ALU.not_equal, fill=1.0,
                                    base=0, pattern=[[-1, P]], channel_multiplier=1).then_inc(sm.consts_made, 1)

            nc.gpsimd.memset(r_tok[:, :], 1.0).then_inc(sm.r_tok_set, 1)
            nc.gpsimd.memset(token[:, 13:14], 0.0).then_inc(sm.r_tok_set, 1)
            free = [(sm.silu_made, 2), (sm.conv_step, 8), (sm.y_made, 3), (sm.last_kept, 1),
                    (sm.qg_made, 1), (sm.ssq_added, 2), (sm.u_lo_made, 2), (sm.usq_made, 2), (sm.gate_made, 2),
                    (sm.o_made, 1)]
            for i, (s, v) in enumerate(free):
                nc.gpsimd.memset(token[:, i:i + 1], 0.0).then_inc(s, v)
            for t in range(NTT + 1):
                n = tokens(t)
                i = 2 * t + 1
                pool.wait_ge(sm.xhi_made, i + 1)
                tt(act_lo[:, 4:8, t * P:t * P + n], Tb[i % 4][:, :, 0:n],
                   act_hi[:, 4:8, t * P:t * P + n].bitcast(f32), SUB).then_inc(sm.xlo_odd, 1)

            for buf in (par[:, :, :], g_tok[:, :, :], pre[0][:, 0:PAD], pre[1][:, 0:PAD]):
                nc.gpsimd.memset(buf, 0.0).then_inc(sm.buffers_zeroed, 1)
            nc.gpsimd.memset(S[:, :, :], 0.0).then_inc(sm.buffers_zeroed, 1)
            pool.wait_ge(sm.buffers_zeroed, ZEROED)
            for dst in (m_inc[:, :], m_smp[:, :], m_blk[:, :], m_bat[:, :]):
                nc.gpsimd.memset(dst, 1.0).then_inc(sm.made, 1)
            for l in range(LEVELS):
                nc.gpsimd.memset(m_lev[l][:, :], 0.0).then_inc(sm.made, 1)
            pool.wait_ge(sm.made, 5 + LEVELS)
            for l in range(LEVELS):
                v = m_lev[l][:, :].rearrange("p (n r) -> p n r", r=2 << l)[:, :, 1 << l:2 << l]
                nc.gpsimd.memset(v, 1.0).then_inc(sm.made, 1)
            made = [5 + 2 * LEVELS]

            def keep(ap, base, pattern, mult):
                pool.wait_ge(sm.made, made[0])
                nc.gpsimd.affine_select(out=ap, in_=ap, compare_op=ALU.is_ge, fill=0.0, base=base,
                                        pattern=pattern, channel_multiplier=mult).then_inc(sm.made, 1)
                made[0] += 1

            keep(m_inc[:, :], 0, [[1, P]], -1)
            keep(m_smp[:, :], 0, [[1, TS]], -1)
            for m in (m_smp, m_blk):
                v = m[:, :].rearrange("p (n r) -> p n r", r=NT)
                keep(v, 0, [[-NT, NB], [0, NT]], 1)
                keep(v, NT - 1, [[NT, NB], [0, NT]], -1)
            keep(m_bat[:, :], 0, [[-NT, NB]], 1)
            keep(m_bat[:, :], NT - 1, [[NT, NB]], -1)
            for l in range(LEVELS):
                h, nb = 1 << l, P >> (l + 1)
                v = m_lev[l][:, :].rearrange("p (n r) -> p n r", r=2 * h)[:, :, h:2 * h]
                keep(v, 0, [[-2 * h, nb], [0, h]], 1)
                keep(v, h - 1, [[2 * h, nb], [0, h]], -1)
            pool.wait_ge(sm.made, made[0])
            nc.gpsimd.memset(token[:, 15:16], 0.0).then_inc(sm.masks_made, 1)
            nc.gpsimd.memset(token[:, 14:15], 0.0).then_inc(sm.s_updated, 4)
            pool.wait_ge(sm.st_ready, 2)

            def sequences(ap, n):
                return ap.rearrange("p a (b w) -> p (a b) w", w=n)

            with pool.Fori(0, NQ // 2) as i:
                for x in range(2):
                    j = ds(2 * i + x, 1)
                    pool.wait_ge(sm.conv_step, at(4 * x + 4, i, 8))
                    pool.wait_ge(sm.buffers_zeroed, ZEROED)
                    copy(samples(pre[x])[:, :, 0:PAD], sequences(st_T[:, j, :], PAD)).then_inc(sm.state_put, 1)
                    if x == 1:
                        for xx in range(2):
                            jj = ds(2 * i + xx, 1)
                            pool.wait_ge(sm.evacuated, twelfths(U_QKV + xx, i, 12))
                            pool.wait_ge(sm.buffers_zeroed, ZEROED)
                            copy(st_O[:, jj, 0:PAD].rearrange("p a w -> p (a w)"), pre[xx][:, TP:TP + PAD]) \
                                .then_inc(sm.state_saved, 1)
                            copy(sequences(st_O[:, jj, PAD:PAD * (NB + 1)], PAD), samples(pre[xx])[:, :, NT:SEG]) \
                                .then_inc(sm.state_saved, 1)

            pool.wait_ge(sm.conv_step, 8 + 4 * NQ)

            def third(t, j):
                m, n = divmod(t, 3)
                b, p = U_B + m, 2 * j
                if t == 2:
                    pool.wait_ge(sm.evacuated, twelfths(b, p, 12))
                    pool.wait_ge(sm.buffers_zeroed, ZEROED)
                    pool.dma_start(z_dram[ds(j, 1)].rearrange("a p t -> p (a t)"), cv[0][:, 0:T]) \
                        .then_inc(sm.z_spilled, 16)
                if t == 3:
                    copy(samples(pre[1])[:, :, 1:PAD], sequences(sc_T[:, ds(j, 1), :], 2)).then_inc(sm.sc_put, 1)
                if m == 2:
                    pool.wait_ge(sm.evacuated, twelfths(b, p, 4 * n + 4))
                    a = n * TH
                    e = min(a + TH, TP)
                    last = tt(pre[1][:, PAD + a:PAD + e], pre[1][:, PAD + a:PAD + e], cv[1][:, a:e], MUL)
                    if n == 2:
                        now = samples(pre[1])[:, :, PAD:SEG]
                        last.then_inc(sm.h_scaled, 1)
                        last = tt(now, now, cv[1][:, TP:T].rearrange("p (b t) -> p b t", t=NT), MUL)
                    last.then_inc(sm.ch_made, 1)
                    if n == 2:
                        pool.wait_ge(sm.ch_made, 3 * j + 3)
                        pool.wait_ge(sm.h_scaled, j + 1)
                        pool.wait_ge(sm.buffers_zeroed, ZEROED)
                        copy(sc_O[:, ds(j, 1), 0:2].rearrange("p a w -> p (a w)"), pre[1][:, TP + 1:TP + PAD]) \
                            .then_inc(sm.state_saved, 1)
                        copy(sequences(sc_O[:, ds(j, 1), 2:2 * (NB + 1)], 2), samples(pre[1])[:, :, NT + 1:SEG]) \
                            .then_inc(sm.state_saved, 1)
                if m == 3:
                    pool.wait_ge(sm.evacuated, twelfths(b, p, 4 * n + 4))
                    pool.wait_ge(sm.sc_step, 3 * j + 3)
                    a = n * TH
                    e = min(a + TH, TP)
                    last = tt(cv[1][:, a:e], cv[1][:, a:e], cv[0][:, a:e], MUL)
                    if n == 2:
                        now = cv[1][:, TP:T].rearrange("p (b t) -> p b t", t=NT)
                        last = tt(now, now, sample_cv(cv[0]), MUL)
                    last.then_inc(sm.y_made, 1)
                    if n == 2:
                        pool.wait_ge(sm.buffers_zeroed, ZEROED)
                        pool.wait_ge(sm.y_made, 3 * j + 6)
                        pool.dma_start(y_dram[ds(j * P, P), :], cv[1][:, 0:T]) \
                            .then_inc(sm.y_spilled, 16)

            def all_heads(m):
                return m[:, None, :].to_broadcast([P, H, P])

            with pool.Fori(0, NSC) as j:
                for step in STEPS:
                    x = int(step[-1]) if step[0] not in "yz" else int(step[1])
                    c1 = 2 * j + x + 1
                    c = ds(2 * j + x, 1)

                    def level(l):
                        tt(Tb[2 + x][:, :, :], AT[x][:, :, :], all_heads(m_lev[l]), MUL).then_inc(sm.lt_made, 1)

                    if step.startswith("prep_norm"):
                        pool.wait_ge(sm.decay_made, c1)
                        tt(Tb[2][:, :, :], Tb[2][:, :, :], all_heads(m_inc), MUL).then_inc(sm.masked, 1)
                        pool.wait_ge(sm.buffers_zeroed, ZEROED)
                        pool.wait_ge(sm.eg_made, c1)
                        copy(egl[x][:, :], Tb[3][:, :, P - 1:P].rearrange("p h a -> p (h a)")).then_inc(sm.last_kept, 1)
                        pool.wait_ge(sm.buffers_zeroed, ZEROED)
                        pool.wait_ge(sm.masked, c1)
                        copy(ktl[x][:, :], Tb[2][:, :, P - 1:P].rearrange("p h a -> p (h a)")).then_inc(sm.last_kept, 1)
                        tt(AT[x][:, :, :], Tb[2][:, :, :], spread(beta[:, c, :].rearrange("p a h -> p (a h)"), P), MUL) \
                            .then_inc(sm.at_scaled, 1)
                        pool.wait_ge(sm.qk_made, at(2 * x + 1, j, 4))
                        tt(qg[x][:, :, :], Tb[4][:, :, :], Tb[3][:, :, :], MUL).then_inc(sm.qg_made, 1)
                    elif step.startswith("prep_kk"):
                        pool.wait_ge(sm.at_made, c1)
                        tt(XT[x][:, :, :], AT[x][:, :, :], all_heads(m_lev[0]), MUL).then_inc(sm.xt_made, 1)
                        pool.wait_ge(sm.xt_made, at(2 * x + 1, j, 4))
                        tt(XT[x][:, :, :], all_heads(ident), XT[x][:, :, :], SUB).then_inc(sm.xt_made, 1)
                    elif step.startswith("prep_x"):
                        level(1)
                    elif step[0] == "y" and int(step[3:]) < LEVELS - 1:
                        l = int(step[3:])
                        pool.wait_ge(sm.y_mm, at(2 * (l - 1) + x + 1, j, 12))
                        level(l + 1)
                    for t in thirds_after(step):
                        third(t, j)
                pool.wait_ge(sm.y_spilled, 16 * j + 16)

            F2, AT0, XT0 = flat(Tb[2]), flat(AT[0]), flat(XT[0])
            by_seq = (AT[0], X[0], X[1], Tb[3])

            def small(ap):
                return hsmall(ap[0:TS, 0:SMALL])

            def small_mask(m):
                return m[0:TS, None, 0:TS].to_broadcast([TS, H, TS])

            pool.wait_ge(sm.q_act, 8)
            tt(small(F2), small(F2), small_mask(m_smp), MUL).then_inc(sm.q_pool, 1)
            pool.wait_ge(sm.q_pool, 1)
            tt(small(AT0), small(F2), spread(beta[0:TS, NTT, :], TS), MUL).then_inc(sm.q_pool, 1)
            pool.wait_ge(sm.q_dve, 5)
            tt(small(F2), small(AT0), small_mask(m_lev[1]), MUL).then_inc(sm.q_pool, 1)
            tt(small(XT0), small(AT0), small_mask(m_lev[0]), MUL).then_inc(sm.q_pool, 1)
            pool.wait_ge(sm.q_pool, 4)
            tt(small(XT0), small_mask(ident), small(XT0), SUB).then_inc(sm.q_pool, 1)
            for i in range(NSC):
                pool.wait_ge(sm.mix_y_hi, i + 1)
                tt(act_lo[:, H + i, 0:TP], qkv[:, H + i, 0:TP], act_hi[:, H + i, 0:TP].bitcast(f32), SUB) \
                    .then_inc(sm.mix_y_lo, 1)
            pool.wait_ge(sm.mix_y_hi, NSC + 1)
            tt(act_lo[:, H:KD, TP:T], XT[1][:, :, TS:2 * TS], act_hi[:, H:KD, TP:T].bitcast(f32), SUB) \
                .then_inc(sm.mix_y_lo, 1)
            pool.wait_ge(sm.q_dve, 10)
            for i in range(2 * H):
                if i >= 4:
                    pool.wait_ge(sm.q_pe, 6 + i)
                tt(by_seq[i % 4][0:TS, :, :],
                   F2[0:TS, None, i // 2 * P:(i // 2 + 1) * P].to_broadcast([TS, 4, P]),
                   spread(m_bat[:, 4 * (i % 2):4 * (i % 2) + 4], P), MUL).then_inc(sm.q_pool, 1)

            def zero_sums():
                nc.gpsimd.memset(ssq[:, :], 0.0).then_inc(sm.ssq_zeroed, 1)

            def add_squares(g, base, i=0, step=0, third=None):
                n = g % 3 if third is None else third
                pool.wait_ge(sm.sq_made, at(base + g + 1, i, step))
                tt(ssq[:, cols(n)], ssq[:, cols(n)], sq[g % 2][:, :], ADD).then_inc(sm.ssq_added, 1)


            pool.wait_ge(sm.sample_states_out, 16 * H)
            zero_sums()
            pool.wait_ge(sm.ssq_zeroed, 1)
            with pool.Fori(0, KD // 2) as i:
                for g in range(6):
                    add_squares(g, 0, i, 6)
            for r in range(1, 3):
                pool.wait_ge(sm.rms_mm, r)
                zero_sums()
                pool.wait_ge(sm.ssq_zeroed, r + 1)
                with pool.Fori(0, KD // 2 if r == 1 else 2) as i:
                    for g in range(6):
                        add_squares(g, r * 3 * KD, i, 6)
            for g in range(12):
                pool.wait_ge(sm.ssq_added, 2 + 6 * KD + 12 + g)
                add_squares(g, 6 * KD + 12, third=last_product(1, g)[1])


def kernel(**inputs):
    import numpy as np
    import concourse.bacc as bacc
    from concourse.bass_utils import run_bass_kernel_spmd as run

    nc = bacc.Bacc("TRN2", target_bir_lowering=False, num_devices=1)
    names = ["x_prompt", "x_sample", "state_gdn_conv", "state_gdn", "state_sc_conv", "p_prompt", "p_sample",
             "norm_mix", "w_in", "w_conv_qkv", "a_log", "dt_bias", "w_gdn_norm", "w_conv_sc", "w_out",
             "norm_mlp", "w_up", "w_down", "norm_ple", "w_ple_gate", "w_ple_proj", "norm_f"]
    outs = [(1, TP, D), (NB, NT, D), (1, 1, PAD, QKV), (1, 1, H, P, P), (1, 1, SW - 1, SCW),
            (1, NB, PAD, QKV), (1, NB, H, P, P), (1, NB, SW - 1, SCW)]
    arrays, args = {}, []
    for name in names:
        a = np.ascontiguousarray(inputs[name])
        if name in ("w_in", "w_out", "w_up", "w_down", "w_ple_gate", "w_ple_proj"):
            a = a.reshape(a.shape[1:])
        arrays[f"in_{name}"] = a
        args.append(nc.dram_tensor(f"in_{name}", a.shape, mybir.dt.float32, kind="ExternalInput").ap())
    for i, shape in enumerate(outs):
        args.append(nc.dram_tensor(f"out_{i}", shape, mybir.dt.float32, kind="ExternalOutput").ap())
    trunk(nc, *args)
    r = run(nc, [arrays], core_ids=[0])
    return tuple(r.results[0][f"out_{i}"] for i in range(len(outs)))
```
